# Optimizing a Trainium2 kernel written in Bass

```python
import math
import jax, jax.numpy as jnp
from jax import lax
import numpy as np

D_MODEL = 2048
BATCH = 1
SEQ = 256
DEPTH = 1

MIX_DIM = D_MODEL
RWKV_HEAD = 64
RWKV_DIM = MIX_DIM // 2
RWKV_HEADS = RWKV_DIM // RWKV_HEAD
RWKV_DECAY_LORA = max(32, int(round(1.8 * RWKV_DIM ** 0.5 / 32)) * 32)
RWKV_AAA_LORA = max(32, int(round(1.8 * RWKV_DIM ** 0.5 / 32)) * 32)
RWKV_MV_LORA = max(32, int(round(0.6 * RWKV_DIM ** 0.5 / 32)) * 32)
RWKV_GATE_LORA = max(32, int(round(0.6 * RWKV_DIM ** 0.8 / 32)) * 32)
RWKV_GN_EPS = RWKV_HEAD * 1e-5
RWKV_L2_EPS = 1e-12

GDN_HEAD = 128
GDN_V_DIM = MIX_DIM - RWKV_DIM
GDN_V_HEADS = GDN_V_DIM // GDN_HEAD
GDN_QK_HEADS = GDN_V_HEADS // 2
GDN_QK_DIM = GDN_QK_HEADS * GDN_HEAD
GDN_CONV = 4
GDN_CHUNK = 64
GDN_L2_EPS = 1e-6
GDN_NORM_EPS = 1e-6

D_FF = -(-8 * D_MODEL // (3 * 256)) * 256
NORM_EPS = 1e-5

N_RWKV_IN = 3 * RWKV_DIM + RWKV_DECAY_LORA + RWKV_AAA_LORA + RWKV_GATE_LORA
N_GDN_IN = 2 * GDN_QK_DIM + 2 * GDN_V_DIM + 2 * GDN_V_HEADS
N_IN = N_RWKV_IN + N_GDN_IN


def split_cols(p, sizes):
    offsets = np.cumsum(np.array(sizes))[:-1].tolist()
    return jnp.split(p, offsets, axis=-1)

def rms_norm(x, w, eps=NORM_EPS):
    x32 = x.astype(jnp.float32)
    y = x32 * lax.rsqrt(jnp.mean(x32 * x32, axis=-1, keepdims=True) + eps)
    return (y * w.astype(jnp.float32)).astype(x.dtype)

def l2_normalize(x, eps):
    x32 = x.astype(jnp.float32)
    return x32 * lax.rsqrt(jnp.sum(x32 * x32, axis=-1, keepdims=True) + eps)

def token_shift_lerp(p, mu):
    prev = jnp.pad(p, ((0, 0), (1, 0), (0, 0)))[:, :-1]
    return p + (prev - p) * mu

def causal_depthwise_conv(x, w):
    K, C = w.shape
    return lax.conv_general_dilated(
        x, w[:, None, :].astype(x.dtype), window_strides=(1,), padding=((K - 1, 0),),
        dimension_numbers=('NWC', 'WIO', 'NWC'), feature_group_count=C)

def rwkv7_recurrence(r, w, k, v, a, b):
    B, T, H, N = r.shape

    def step(S, inp):
        r_t, w_t, k_t, v_t, a_t, b_t = inp
        Sa = jnp.einsum('bhvk,bhk->bhv', S, a_t)
        S = S * w_t[:, :, None, :] + Sa[..., None] * b_t[:, :, None, :] + v_t[..., None] * k_t[:, :, None, :]
        return S, jnp.einsum('bhvk,bhk->bhv', S, r_t)

    xs = tuple(jnp.moveaxis(t, 1, 0) for t in (r, w, k, v, a, b))
    S0 = jnp.zeros((B, H, N, N), jnp.float32)
    _, y = lax.scan(step, S0, xs)
    return jnp.moveaxis(y, 0, 1)

def rwkv7_mixer(p, vres, v_first, mu, w0, w_up, a0, a_up, g_up, k_k, k_a, r_k, ln_w, ln_b):
    B, T, _ = p.shape
    H, N = RWKV_HEADS, RWKV_HEAD
    p = token_shift_lerp(p.astype(jnp.float32), mu)
    r, k, v, wd, ad, gd = split_cols(
        p, (RWKV_DIM, RWKV_DIM, RWKV_DIM, RWKV_DECAY_LORA, RWKV_AAA_LORA, RWKV_GATE_LORA))
    w = -jax.nn.softplus(-(w0 + jnp.tanh(wd) @ w_up)) - 0.5
    decay = jnp.exp(-jnp.exp(w))
    if vres is None:
        v_first = v
    else:
        vd, v_up, v0 = vres
        v = v + (v_first - v) * jax.nn.sigmoid(v0 + vd @ v_up)
    a = jax.nn.sigmoid(a0 + ad @ a_up)
    g = jax.nn.sigmoid(gd) @ g_up
    heads = lambda t: t.reshape(B, T, H, N)
    kk = l2_normalize(heads(k * k_k), RWKV_L2_EPS)
    k = k * (1.0 + (a - 1.0) * k_a)
    r, k, v, a, decay = map(heads, (r, k, v, a, decay))
    y = rwkv7_recurrence(r, decay, k, v, -kk, kk * a)
    mean = jnp.mean(y, axis=-1, keepdims=True)
    var = jnp.mean(jnp.square(y - mean), axis=-1, keepdims=True)
    y = ((y - mean) * lax.rsqrt(var + RWKV_GN_EPS)).reshape(B, T, RWKV_DIM) * ln_w + ln_b
    bonus = (jnp.sum(r * k * r_k, axis=-1, keepdims=True) * v).reshape(B, T, RWKV_DIM)
    return (y + bonus) * g, v_first

def gated_delta_rule_chunked(q, k, v, g, beta):
    B, T, H, dk = q.shape
    dv = v.shape[-1]
    C = GDN_CHUNK
    NC = T // C
    q = l2_normalize(q, GDN_L2_EPS) * (dk ** -0.5)
    k = l2_normalize(k, GDN_L2_EPS)

    def to_chunks(t):
        t = t.reshape((B, NC, C, H) + t.shape[3:])
        return jnp.moveaxis(t, 3, 1)

    q, k, v, g, beta = map(to_chunks, (q, k, v, g, beta))
    g = jnp.cumsum(g, axis=-1)
    idx = jnp.arange(C)
    causal = idx[:, None] >= idx[None, :]
    strict = idx[:, None] > idx[None, :]
    gamma = jnp.exp(jnp.where(causal, g[..., :, None] - g[..., None, :], -jnp.inf))
    k_beta = k * beta[..., None]
    v_beta = v * beta[..., None]
    L = jnp.where(strict, jnp.einsum('bhnid,bhnjd->bhnij', k_beta, k) * gamma, 0.0)
    eye = jnp.eye(C, dtype=L.dtype)
    rhs = jnp.concatenate([v_beta, k_beta * jnp.exp(g)[..., None]], axis=-1)
    sol = lax.linalg.triangular_solve(L + eye, rhs, left_side=True, lower=True, unit_diagonal=True)
    u, w = sol[..., :dv], sol[..., dv:]
    A_qk = jnp.einsum('bhnid,bhnjd->bhnij', q, k) * gamma
    q_g = q * jnp.exp(g)[..., None]
    g_last = g[..., -1]
    k_g = k * jnp.exp(g_last[..., None] - g)[..., None]

    def step(S, inp):
        u_i, w_i, qg_i, kg_i, A_i, gl_i = inp
        v_new = u_i - jnp.einsum('bhck,bhkv->bhcv', w_i, S)
        o = jnp.einsum('bhck,bhkv->bhcv', qg_i, S) + jnp.einsum('bhij,bhjv->bhiv', A_i, v_new)
        S = S * jnp.exp(gl_i)[..., None, None] + jnp.einsum('bhck,bhcv->bhkv', kg_i, v_new)
        return S, o

    xs = tuple(jnp.moveaxis(t, 2, 0) for t in (u, w, q_g, k_g, A_qk, g_last))
    S0 = jnp.zeros((B, H, dk, dv), jnp.float32)
    _, o = lax.scan(step, S0, xs)
    return o.transpose(1, 0, 3, 2, 4).reshape(B, T, H, dv)

def gdn_mixer(p, conv_w, A_log, dt_bias, norm_w):
    B, T, _ = p.shape
    p = p.astype(jnp.float32)
    qkv, z, a, b = split_cols(p, (2 * GDN_QK_DIM + GDN_V_DIM, GDN_V_DIM, GDN_V_HEADS, GDN_V_HEADS))
    qkv = jax.nn.silu(causal_depthwise_conv(qkv, conv_w.astype(jnp.float32)))
    q, k, v = split_cols(qkv, (GDN_QK_DIM, GDN_QK_DIM, GDN_V_DIM))
    rep = GDN_V_HEADS // GDN_QK_HEADS
    q = jnp.repeat(q.reshape(B, T, GDN_QK_HEADS, GDN_HEAD), rep, axis=2)
    k = jnp.repeat(k.reshape(B, T, GDN_QK_HEADS, GDN_HEAD), rep, axis=2)
    v = v.reshape(B, T, GDN_V_HEADS, GDN_HEAD)
    g = -jnp.exp(A_log) * jax.nn.softplus(a + dt_bias)
    beta = jax.nn.sigmoid(b)
    o = gated_delta_rule_chunked(q, k, v, g, beta)
    o = o * lax.rsqrt(jnp.mean(o * o, axis=-1, keepdims=True) + GDN_NORM_EPS) * norm_w
    o = o * jax.nn.silu(z.reshape(B, T, GDN_V_HEADS, GDN_HEAD))
    return o.reshape(B, T, GDN_V_DIM)

def first_inputs(seed: int = 0) -> dict:
    key = jax.random.key(seed)
    ks = iter(jax.random.split(key, 40))
    L, D, Lv = DEPTH, D_MODEL, DEPTH - 1

    def nrm(shape, scale):
        return jax.random.normal(next(ks), shape, jnp.float32) * scale

    def unif(shape, lo, hi):
        return jax.random.uniform(next(ks), shape, jnp.float32, lo, hi)

    dt = jnp.exp(unif((L, GDN_V_HEADS), math.log(1e-3), math.log(1e-1)))
    return {
        'x': nrm((BATCH, SEQ, D), 1.0),
        'attn_norm_w': 1.0 + nrm((L, D), 0.05),
        'w_in': nrm((L, D, N_IN), D ** -0.5),
        'rwkv_mu': unif((L, N_RWKV_IN), 0.0, 1.0),
        'rwkv_w0': unif((L, RWKV_DIM), -6.0, -0.5),
        'rwkv_w_up': nrm((L, RWKV_DECAY_LORA, RWKV_DIM), 0.1 * RWKV_DECAY_LORA ** -0.5),
        'rwkv_a0': nrm((L, RWKV_DIM), 0.1),
        'rwkv_a_up': nrm((L, RWKV_AAA_LORA, RWKV_DIM), 0.5 * RWKV_AAA_LORA ** -0.5),
        'rwkv_g_up': nrm((L, RWKV_GATE_LORA, RWKV_DIM), RWKV_GATE_LORA ** -0.5),
        'rwkv_k_k': 0.85 + nrm((L, RWKV_DIM), 0.05),
        'rwkv_k_a': 1.0 + nrm((L, RWKV_DIM), 0.05),
        'rwkv_r_k': -0.04 + nrm((L, RWKV_HEADS, RWKV_HEAD), 0.02),
        'rwkv_ln_w': 1.0 + nrm((L, RWKV_DIM), 0.05),
        'rwkv_ln_b': nrm((L, RWKV_DIM), 0.02),
        'vres_down': nrm((Lv, D, RWKV_MV_LORA), D ** -0.5),
        'vres_mu': unif((Lv, RWKV_MV_LORA), 0.0, 1.0),
        'vres_up': nrm((Lv, RWKV_MV_LORA, RWKV_DIM), 0.5 * RWKV_MV_LORA ** -0.5),
        'vres_v0': 1.0 + nrm((Lv, RWKV_DIM), 0.1),
        'gdn_conv_w': nrm((L, GDN_CONV, 2 * GDN_QK_DIM + GDN_V_DIM), 0.5),
        'gdn_A_log': jnp.log(unif((L, GDN_V_HEADS), 1.0, 16.0)),
        'gdn_dt_bias': jnp.log(jnp.expm1(dt)),
        'gdn_norm_w': 1.0 + nrm((L, GDN_HEAD), 0.05),
        'w_out': nrm((L, MIX_DIM, D), MIX_DIM ** -0.5),
        'ffn_norm_w': 1.0 + nrm((L, D), 0.05),
        'ffn_w_gate': nrm((L, D, D_FF), D ** -0.5),
        'ffn_w_up': nrm((L, D, D_FF), D ** -0.5),
        'ffn_w_down': nrm((L, D_FF, D), D_FF ** -0.5),
        'final_norm_w': 1.0 + nrm((D,), 0.05),
    }

def first_block(x, attn_norm_w, w_in, rwkv_mu, rwkv_w0, rwkv_w_up, rwkv_a0, rwkv_a_up, rwkv_g_up,
              rwkv_k_k, rwkv_k_a, rwkv_r_k, rwkv_ln_w, rwkv_ln_b, vres_down, vres_mu, vres_up, vres_v0,
              gdn_conv_w, gdn_A_log, gdn_dt_bias, gdn_norm_w, w_out, ffn_norm_w, ffn_w_gate, ffn_w_up,
              ffn_w_down, final_norm_w):
    v_first = None
    for l in range(DEPTH):
        h = rms_norm(x, attn_norm_w[l])
        if l == 0:
            w_cat = w_in[0]
        else:
            w_cat = jnp.concatenate([w_in[l], vres_down[l - 1]], axis=1)
        proj = h @ w_cat
        p_rwkv = proj[..., :N_RWKV_IN]
        p_gdn = proj[..., N_RWKV_IN:N_IN]
        if l == 0:
            vres = None
        else:
            vd = token_shift_lerp(proj[..., N_IN:].astype(jnp.float32), vres_mu[l - 1])
            vres = (vd, vres_up[l - 1], vres_v0[l - 1])
        y_a, v_first = rwkv7_mixer(p_rwkv, vres, v_first, rwkv_mu[l], rwkv_w0[l], rwkv_w_up[l],
                                   rwkv_a0[l], rwkv_a_up[l], rwkv_g_up[l], rwkv_k_k[l], rwkv_k_a[l],
                                   rwkv_r_k[l], rwkv_ln_w[l], rwkv_ln_b[l])
        y_b = gdn_mixer(p_gdn, gdn_conv_w[l], gdn_A_log[l], gdn_dt_bias[l], gdn_norm_w[l])
        y = jnp.concatenate([y_a, y_b], axis=-1).astype(x.dtype)
        x = x + y @ w_out[l]
        h = rms_norm(x, ffn_norm_w[l])
        x = x + (jax.nn.silu(h @ ffn_w_gate[l]) * (h @ ffn_w_up[l])) @ ffn_w_down[l]
    return rms_norm(x, final_norm_w)


N_MIXERS = 4
HEAD_DIM = 128
N_HEADS = D_MODEL // HEAD_DIM
Q_BLOCK = 128
EPS = 1e-6

FOX_FGATE_BIAS = 2.0

MLA_Q_RANK = 512
MLA_KV_RANK = 512
MLA_NOPE = 128
MLA_ROPE = 64
MLA_V = 128
ROPE_THETA = 10000.0

SGU_CHUNK = 128
SGU_WIDTH = D_MODEL
SGU_GROUP_DIM = 128
SGU_GROUPS = SGU_WIDTH // SGU_GROUP_DIM

D_FF_2 = 5632
CONV_WIDTH = 3


def _n_layers_of(m):
    return len(range(m, DEPTH, N_MIXERS))

def rms_norm_2(x, gain):
    x32 = x.astype(jnp.float32)
    y = x32 * lax.rsqrt(jnp.mean(x32 * x32, axis=-1, keepdims=True) + EPS)
    return (y * gain.astype(jnp.float32)).astype(x.dtype)

def _sweep_query_blocks(block_fn, seq):
    out = lax.map(block_fn, jnp.arange(seq // Q_BLOCK))
    nb, b, qb, h, dv = out.shape
    return out.transpose(1, 0, 2, 3, 4).reshape(b, seq, h * dv)

def _causal_softmax(s, start, v):
    seq = s.shape[-1]
    q_pos = start + jnp.arange(Q_BLOCK)
    allowed = jnp.arange(seq)[None, :] <= q_pos[:, None]
    p = jax.nn.softmax(jnp.where(allowed, s, -jnp.inf), axis=-1)
    return jnp.einsum('bhqs,bshd->bqhd', p.astype(v.dtype), v)

def fox_mixer(h, w_in, b_f, q_gain, k_gain, w_out):
    bsz, seq, _ = h.shape
    hd = N_HEADS * HEAD_DIM
    q, k, v, f_logit = jnp.split(h @ w_in, [hd, 2 * hd, 3 * hd], axis=-1)
    q = rms_norm_2(q.reshape(bsz, seq, N_HEADS, HEAD_DIM), q_gain)
    k = rms_norm_2(k.reshape(bsz, seq, N_HEADS, HEAD_DIM), k_gain)
    v = v.reshape(bsz, seq, N_HEADS, HEAD_DIM)
    log_f = jax.nn.log_sigmoid(f_logit.astype(jnp.float32) + b_f.astype(jnp.float32))
    cum = jnp.cumsum(log_f, axis=1).transpose(0, 2, 1)
    scale = HEAD_DIM ** -0.5

    def block(i):
        start = i * Q_BLOCK
        qb = lax.dynamic_slice_in_dim(q, start, Q_BLOCK, axis=1)
        cq = lax.dynamic_slice_in_dim(cum, start, Q_BLOCK, axis=2)
        s = jnp.einsum('bqhd,bshd->bhqs', qb, k, preferred_element_type=jnp.float32) * scale
        s = s + (cq[..., :, None] - cum[:, :, None, :])
        return _causal_softmax(s, start, v)

    return _sweep_query_blocks(block, seq) @ w_out

def _rope_tables(positions):
    inv_freq = ROPE_THETA ** (-jnp.arange(0, MLA_ROPE, 2, dtype=jnp.float32) / MLA_ROPE)
    ang = positions.astype(jnp.float32)[..., None] * inv_freq
    return jnp.cos(ang)[:, :, None, :], jnp.sin(ang)[:, :, None, :]

def _apply_rope(x, cos, sin):
    x1, x2 = jnp.split(x.astype(jnp.float32), 2, axis=-1)
    return jnp.concatenate([x1 * cos - x2 * sin, x1 * sin + x2 * cos], axis=-1).astype(x.dtype)

def mla_mixer(h, positions, w_in, q_a_gain, kv_a_gain, w_q_b, w_kv_b, q_gain, k_gain, w_out):
    bsz, seq, _ = h.shape
    c_q, c_kv, k_rope = jnp.split(h @ w_in, [MLA_Q_RANK, MLA_Q_RANK + MLA_KV_RANK], axis=-1)
    q = (rms_norm_2(c_q, q_a_gain) @ w_q_b).reshape(bsz, seq, N_HEADS, MLA_NOPE + MLA_ROPE)
    kv = (rms_norm_2(c_kv, kv_a_gain) @ w_kv_b).reshape(bsz, seq, N_HEADS, MLA_NOPE + MLA_V)
    q_nope, q_rope = jnp.split(q, [MLA_NOPE], axis=-1)
    k_nope, v = jnp.split(kv, [MLA_NOPE], axis=-1)
    cos, sin = _rope_tables(positions)
    q_nope = rms_norm_2(q_nope, q_gain[:MLA_NOPE])
    k_nope = rms_norm_2(k_nope, k_gain[:MLA_NOPE])
    q_rope = _apply_rope(rms_norm_2(q_rope, q_gain[MLA_NOPE:]), cos, sin)
    k_rope = _apply_rope(rms_norm_2(k_rope[:, :, None, :], k_gain[MLA_NOPE:]), cos, sin)
    q = jnp.concatenate([q_nope, q_rope], axis=-1)
    k = jnp.concatenate([k_nope, jnp.broadcast_to(k_rope, (bsz, seq, N_HEADS, MLA_ROPE))], axis=-1)
    scale = (MLA_NOPE + MLA_ROPE) ** -0.5

    def block(i):
        start = i * Q_BLOCK
        qb = lax.dynamic_slice_in_dim(q, start, Q_BLOCK, axis=1)
        s = jnp.einsum('bqhd,bshd->bhqs', qb, k, preferred_element_type=jnp.float32) * scale
        return _causal_softmax(s, start, v)

    return _sweep_query_blocks(block, seq) @ w_out

def stick_breaking_mixer(h, w_in, q_gain, k_gain, w_out):
    bsz, seq, _ = h.shape
    hd = N_HEADS * HEAD_DIM
    q, k, v = jnp.split(h @ w_in, [hd, 2 * hd], axis=-1)
    q = rms_norm_2(q.reshape(bsz, seq, N_HEADS, HEAD_DIM), q_gain)
    k = rms_norm_2(k.reshape(bsz, seq, N_HEADS, HEAD_DIM), k_gain)
    v = v.reshape(bsz, seq, N_HEADS, HEAD_DIM)
    scale = HEAD_DIM ** -0.5

    def block(i):
        start = i * Q_BLOCK
        qb = lax.dynamic_slice_in_dim(q, start, Q_BLOCK, axis=1)
        z = jnp.einsum('bqhd,bshd->bhqs', qb, k, preferred_element_type=jnp.float32) * scale
        q_pos = start + jnp.arange(Q_BLOCK)
        strict = jnp.arange(seq)[None, :] < q_pos[:, None]
        log_keep = jnp.where(strict, -jax.nn.softplus(z), 0.0)
        after = lax.cumsum(log_keep, axis=3, reverse=True) - log_keep
        a = jnp.where(strict, jnp.exp(jax.nn.log_sigmoid(z) + after), 0.0)
        return jnp.einsum('bhqs,bshd->bqhd', a.astype(v.dtype), v)

    return _sweep_query_blocks(block, seq) @ w_out

def sgu_mixer(h, w_in, v_gain, w_s, b_s, w_out):
    bsz, seq, _ = h.shape
    u, vv = jnp.split(jax.nn.gelu(h @ w_in), 2, axis=-1)
    vv = rms_norm_2(vv, v_gain)
    n_chunks = seq // SGU_CHUNK
    vv = vv.reshape(bsz, n_chunks, SGU_CHUNK, SGU_GROUPS, SGU_GROUP_DIM)
    causal = jnp.tril(jnp.ones((SGU_CHUNK, SGU_CHUNK), dtype=bool))
    ws = jnp.where(causal[None], w_s, 0.0).astype(vv.dtype)
    mixed = jnp.einsum('gts,bnsgc->bntgc', ws, vv) + b_s.T[:, :, None]
    return (u * mixed.reshape(bsz, seq, SGU_WIDTH)) @ w_out

def conv_ffn(h, w_up, conv_w, conv_b, w_down):
    seq = h.shape[1]
    up = h @ w_up
    padded = jnp.pad(up, ((0, 0), (CONV_WIDTH - 1, 0), (0, 0)))
    y = conv_b + conv_w[0] * padded[:, 0:seq]
    for tap in range(1, CONV_WIDTH):
        y = y + conv_w[tap] * padded[:, tap:tap + seq]
    gate, val = jnp.split(y, 2, axis=-1)
    return (jax.nn.silu(gate) * val) @ w_down

def second_inputs(seed: int = 0) -> dict:
    key = jax.random.key(seed)
    ks = iter(list(jax.random.split(key, 32)))

    def w(shape, fan_in):
        return jax.random.normal(next(ks), shape, jnp.float32) * fan_in ** -0.5

    def gain(shape):
        return 1.0 + 0.1 * jax.random.normal(next(ks), shape, jnp.float32)

    n_a, n_b, n_c, n_d = (_n_layers_of(m) for m in range(N_MIXERS))
    hd = N_HEADS * HEAD_DIM
    x = jax.random.normal(next(ks), (BATCH, SEQ, D_MODEL), jnp.float32)
    offset = jax.random.randint(next(ks), (BATCH, 1), 0, 4096, dtype=jnp.int32)
    positions = offset + jnp.arange(SEQ, dtype=jnp.int32)[None, :]
    return {
        'x': x,
        'positions': positions,
        'mix_norm': gain((DEPTH, D_MODEL)),
        'ffn_norm': gain((DEPTH, D_MODEL)),
        'fox_w_in': w((n_a, D_MODEL, 3 * hd + N_HEADS), D_MODEL),
        'fox_b_f': FOX_FGATE_BIAS + 0.5 * jax.random.normal(next(ks), (n_a, N_HEADS), jnp.float32),
        'fox_q_gain': gain((n_a, HEAD_DIM)),
        'fox_k_gain': gain((n_a, HEAD_DIM)),
        'fox_w_out': w((n_a, hd, D_MODEL), hd),
        'mla_w_in': w((n_b, D_MODEL, MLA_Q_RANK + MLA_KV_RANK + MLA_ROPE), D_MODEL),
        'mla_q_a_gain': gain((n_b, MLA_Q_RANK)),
        'mla_kv_a_gain': gain((n_b, MLA_KV_RANK)),
        'mla_w_q_b': w((n_b, MLA_Q_RANK, N_HEADS * (MLA_NOPE + MLA_ROPE)), MLA_Q_RANK),
        'mla_w_kv_b': w((n_b, MLA_KV_RANK, N_HEADS * (MLA_NOPE + MLA_V)), MLA_KV_RANK),
        'mla_q_gain': gain((n_b, MLA_NOPE + MLA_ROPE)),
        'mla_k_gain': gain((n_b, MLA_NOPE + MLA_ROPE)),
        'mla_w_out': w((n_b, N_HEADS * MLA_V, D_MODEL), N_HEADS * MLA_V),
        'sb_w_in': w((n_c, D_MODEL, 3 * hd), D_MODEL),
        'sb_q_gain': gain((n_c, HEAD_DIM)),
        'sb_k_gain': gain((n_c, HEAD_DIM)),
        'sb_w_out': w((n_c, hd, D_MODEL), hd),
        'sgu_w_in': w((n_d, D_MODEL, 2 * SGU_WIDTH), D_MODEL),
        'sgu_v_gain': gain((n_d, SGU_WIDTH)),
        'sgu_w_s': w((n_d, SGU_GROUPS, SGU_CHUNK, SGU_CHUNK), SGU_CHUNK),
        'sgu_b_s': gain((n_d, SGU_GROUPS, SGU_CHUNK)),
        'sgu_w_out': w((n_d, SGU_WIDTH, D_MODEL), SGU_WIDTH),
        'ffn_w_up': w((DEPTH, D_MODEL, 2 * D_FF_2), D_MODEL),
        'ffn_conv_w': w((DEPTH, CONV_WIDTH, 2 * D_FF_2), CONV_WIDTH),
        'ffn_conv_b': 0.01 * jax.random.normal(next(ks), (DEPTH, 2 * D_FF_2), jnp.float32),
        'ffn_w_down': w((DEPTH, D_FF_2, D_MODEL), D_FF_2),
    }

def second_block(x, positions, mix_norm, ffn_norm,
              fox_w_in, fox_b_f, fox_q_gain, fox_k_gain, fox_w_out,
              mla_w_in, mla_q_a_gain, mla_kv_a_gain, mla_w_q_b, mla_w_kv_b,
              mla_q_gain, mla_k_gain, mla_w_out,
              sb_w_in, sb_q_gain, sb_k_gain, sb_w_out,
              sgu_w_in, sgu_v_gain, sgu_w_s, sgu_b_s, sgu_w_out,
              ffn_w_up, ffn_conv_w, ffn_conv_b, ffn_w_down):
    h = x
    for i in range(DEPTH):
        m, j = i % N_MIXERS, i // N_MIXERS
        a = rms_norm_2(h, mix_norm[i])
        if m == 0:
            mixed = fox_mixer(a, fox_w_in[j], fox_b_f[j], fox_q_gain[j], fox_k_gain[j], fox_w_out[j])
        elif m == 1:
            mixed = mla_mixer(a, positions, mla_w_in[j], mla_q_a_gain[j], mla_kv_a_gain[j],
                              mla_w_q_b[j], mla_w_kv_b[j], mla_q_gain[j], mla_k_gain[j], mla_w_out[j])
        elif m == 2:
            mixed = stick_breaking_mixer(a, sb_w_in[j], sb_q_gain[j], sb_k_gain[j], sb_w_out[j])
        else:
            mixed = sgu_mixer(a, sgu_w_in[j], sgu_v_gain[j], sgu_w_s[j], sgu_b_s[j], sgu_w_out[j])
        h = h + mixed
        h = h + conv_ffn(rms_norm_2(h, ffn_norm[i]), ffn_w_up[i], ffn_conv_w[i], ffn_conv_b[i], ffn_w_down[i])
    return h


def setup_inputs(seed=0):
    out = dict(first_inputs(seed))
    for name, value in second_inputs(seed + 1).items():
        if name != "x":
            out[name + "_2"] = value
    return out


def reference(
    x, attn_norm_w, w_in, rwkv_mu, rwkv_w0, rwkv_w_up, rwkv_a0, rwkv_a_up, rwkv_g_up, rwkv_k_k,
    rwkv_k_a, rwkv_r_k, rwkv_ln_w, rwkv_ln_b, vres_down, vres_mu, vres_up, vres_v0, gdn_conv_w,
    gdn_A_log, gdn_dt_bias, gdn_norm_w, w_out, ffn_norm_w, ffn_w_gate, ffn_w_up, ffn_w_down,
    final_norm_w, positions_2, mix_norm_2, ffn_norm_2, fox_w_in_2, fox_b_f_2, fox_q_gain_2,
    fox_k_gain_2, fox_w_out_2, mla_w_in_2, mla_q_a_gain_2, mla_kv_a_gain_2, mla_w_q_b_2,
    mla_w_kv_b_2, mla_q_gain_2, mla_k_gain_2, mla_w_out_2, sb_w_in_2, sb_q_gain_2, sb_k_gain_2,
    sb_w_out_2, sgu_w_in_2, sgu_v_gain_2, sgu_w_s_2, sgu_b_s_2, sgu_w_out_2, ffn_w_up_2,
    ffn_conv_w_2, ffn_conv_b_2, ffn_w_down_2,
):
    x = first_block(
        x, attn_norm_w, w_in, rwkv_mu, rwkv_w0, rwkv_w_up, rwkv_a0, rwkv_a_up, rwkv_g_up,
        rwkv_k_k, rwkv_k_a, rwkv_r_k, rwkv_ln_w, rwkv_ln_b, vres_down, vres_mu, vres_up,
        vres_v0, gdn_conv_w, gdn_A_log, gdn_dt_bias, gdn_norm_w, w_out, ffn_norm_w, ffn_w_gate,
        ffn_w_up, ffn_w_down, final_norm_w,
    )
    return second_block(
        x, positions_2, mix_norm_2, ffn_norm_2, fox_w_in_2, fox_b_f_2, fox_q_gain_2,
        fox_k_gain_2, fox_w_out_2, mla_w_in_2, mla_q_a_gain_2, mla_kv_a_gain_2, mla_w_q_b_2,
        mla_w_kv_b_2, mla_q_gain_2, mla_k_gain_2, mla_w_out_2, sb_w_in_2, sb_q_gain_2,
        sb_k_gain_2, sb_w_out_2, sgu_w_in_2, sgu_v_gain_2, sgu_w_s_2, sgu_b_s_2, sgu_w_out_2,
        ffn_w_up_2, ffn_conv_w_2, ffn_conv_b_2, ffn_w_down_2,
    )


_drawn_inputs = setup_inputs


def setup_inputs(seed=0):
    import zlib

    import numpy as np

    out = dict(_drawn_inputs(seed))
    spreads = {}
    factors = {'rwkv_w_up': 25.684,
     'rwkv_a0': 2.918,
     'rwkv_k_k': 12.072,
     'rwkv_r_k': 2.847,
     'rwkv_ln_b': 5.388,
     'ffn_conv_b_2': 8.0}
    for name, (base, spread) in spreads.items():
        noise = np.random.default_rng([zlib.crc32(name.encode()), seed]).standard_normal(out[name].shape)
        drawn = base * np.exp(spread * noise) if base else spread * noise
        out[name] = __import__('jax').numpy.asarray(drawn.astype(out[name].dtype))
    for name, factor in factors.items():
        out[name] = (out[name] * factor).astype(out[name].dtype)
    return out
```

```python
from contextlib import ExitStack

import concourse.bass as bass
from concourse import mybir

F32 = mybir.dt.float32
F32R = mybir.dt.float32r
ALU = mybir.AluOpType
ACT = mybir.ActivationFunctionType
AX_X = mybir.AxisListType.X

P = 128
T = 256
D = 2048
KT = D // P
FT = 5632 // P
C = 64
NCH = T // C
NT = T // P
UNIT = 2048
RAW_SLOTS, HI_SLOTS = 4, 2
GROUP = 8
UG = KT // 2

R_DIM, R_HEADS, R_HEAD = 1024, 16, 64
PAIRS = R_HEADS // 2
G_HEADS, G_QK = 8, 4
A_HEADS = 16
N_RWKV = 3360
DECAY_RATE = 0.6065306597126334
TP = 260
PAD = TP - T
T_WA, T_G0, T_G1 = 0, 1, 2
T_R, T_K, T_V, T_GQ, T_GK, T_GV, T_Z = 3, 11, 19, 27, 31, 35, 43
NTILES = 51

WEIGHTS = ["w_in", "w_out", "ffn_w_gate", "ffn_w_up", "ffn_w_down", "fox_w_in_2", "fox_w_out_2",
           "ffn_w_up_2", "ffn_w_down_2"]
NAMES = ["x", "attn_norm_w", "w_in", "rwkv_mu", "rwkv_w0", "rwkv_w_up", "rwkv_a0", "rwkv_a_up", "rwkv_g_up",
         "rwkv_k_k", "rwkv_k_a", "rwkv_r_k", "rwkv_ln_w", "rwkv_ln_b", "gdn_conv_w", "gdn_A_log",
         "gdn_dt_bias", "gdn_norm_w", "w_out", "ffn_norm_w", "ffn_w_gate", "ffn_w_up", "ffn_w_down",
         "final_norm_w", "mix_norm_2", "ffn_norm_2", "fox_w_in_2", "fox_b_f_2", "fox_q_gain_2",
         "fox_k_gain_2", "fox_w_out_2", "ffn_w_up_2", "ffn_conv_w_2", "ffn_conv_b_2", "ffn_w_down_2"]

PACKS = [
    [("attn_norm_w", 16), ("ffn_norm_w", 16), ("final_norm_w", 16), ("mix_norm_2", 16), ("ffn_norm_2", 16),
     ("gdn_norm_w", 1), ("fox_q_gain_2", 1), ("fox_k_gain_2", 1)],
    [("rwkv_mu", 27), ("rwkv_w0", 8), ("rwkv_a0", 8), ("rwkv_k_k", 8), ("rwkv_k_a", 8), ("rwkv_r_k", 8),
     ("rwkv_ln_w", 8), ("rwkv_ln_b", 8)],
    [("gdn_conv_w", 64)],
    [("conv0", 88)], [("conv1", 88)], [("conv2", 88)], [("ffn_conv_b_2", 88)],
]
COL, _c = {}, 0
for _pack in PACKS:
    for _name, _rows in _pack:
        COL[_name] = _c
        _c += _rows
VEC_COLS = _c


def build(nc, io, out):
    with ExitStack() as ctx:
        sems, counts = {}, {}

        def S(name):
            if name not in sems:
                sems[name] = ctx.enter_context(nc.semaphore(name))
            return sems[name]

        def tick(ins, name, by=1):
            ins.then_inc(S(name), by)
            counts[name] = counts.get(name, 0) + by
            return counts[name]

        def waiter(engine):
            seen = {}

            def got(name, by=1):
                seen[name] = seen.get(name, 0) + by
                engine.wait_ge(S(name), seen[name])
            return got

        def own(engine, name):
            engine.wait_ge(S(name), counts[name])

        def at(name, shape, offset, dt=F32):
            return nc.alloc_sbuf_tensor_at(name, shape, dt, offset=offset)

        o = nc.sbuf_base if isinstance(nc.sbuf_base, int) else 0
        o = (o + 63) // 64 * 64
        base0 = o
        X = at("X", [P, KT, T], o); o += 16384
        RAW = at("RAW", [P, RAW_SLOTS, UNIT], o)
        LOW = at("LOW", [P, RAW_SLOTS, UNIT], o, F32R); o += 32768
        HIW = at("HIW", [P, HI_SLOTS, UNIT], o, F32R); o += 16384
        ident = at("ident", [P, P], o); o += 512
        ones = at("ones", [P, P], o); o += 512
        headones = at("headones", [P, P], o); o += 512
        vec = at("vec", [P, VEC_COLS], o); o += (VEC_COLS * 4 + 63) // 64 * 64
        small = at("small", [P, 256], o); o += 1024
        causal = at("causal", [P, P], o); o += 512
        rstd = at("rstd", [P, T], o); o += 1024
        h0 = o
        H = at("H", [P, 2, KT, T], h0, F32R); o += 32768
        r2 = o
        end = base0 + 212800
        masks = end - 5632
        upper2 = at("upper2", [P, 2, P], masks)
        upper, upper_eq = upper2[:, 0, :], upper2[:, 1, :]
        lower1 = at("lower1", [P, P], masks + 1024)
        off = at("off", [P, 6, P], masks + 1536)
        chunk_go = at("chunk_go", [P, T], masks + 4608)
        assert r2 + 102192 <= masks and r2 + 90112 + 16600 <= end, (r2, masks, end)

        XIN = at("XIN", [P, NT, D], r2)
        VPACK = at("VPACK", [P, len(PACKS), P], r2 + 16384)
        NSQ = at("NSQ", [P, KT, T], r2)
        NSQ_H = at("NSQ_H", [P, KT, T], h0)
        PR = at("PR", [P, NTILES, TP], r2)
        a3 = r2 + 53056
        SHIFT = at("SHIFT", [P, 27, T], h0)
        GS = at("GS", [P, PAIRS, T], h0)
        ENG = at("ENG", [P, PAIRS, T], h0 + 8192)
        KK = at("KK", [P, PAIRS, T], h0 + 16384)
        TMP = at("TMP", [P, PAIRS, T], h0 + 24576)
        AR = at("AR", [P, PAIRS, 2, T], a3)
        RN = at("RN", [P, PAIRS, T], a3)
        RN2 = at("RN2", [P, PAIRS, T], a3 + 8192)
        BH = at("BH", [P, PAIRS, T], a3 + 16384)
        BON = at("BON", [P, PAIRS, T], a3 + 24576)
        WA_UP = at("WA_UP", [P, R_DIM], a3 + 24576)
        EG = at("EG", [P, PAIRS, T], a3 + 32768)
        G_UP = at("G_UP", [P, 2, R_DIM], a3 + 40960)
        VTOK = at("VTOK", [P, 4, P], a3 + 32768)
        BTOK = at("BTOK", [P, 4, P], a3 + 34816)
        KTOK = at("KTOK", [P, 4, P], a3 + 36864)
        ST = at("ST", [P, 4, P], a3 + 38912)
        R1 = at("R1", [P, 4, P], r2 + T_R * TP * 4 + 16)
        UU = at("UU", [P, 4, P], r2 + T_R * TP * 4 + 16 + 2048)
        LBR = at("LBR", [P, 8, 2, P], h0)
        LKR = at("LKR", [P, 8, 2, P], h0 + 8192)
        TT = at("TT", [P, 8, P], h0 + 16384)
        TM = at("TM", [P, 8, P], h0 + 20480)
        PM = at("PM", [P, 8, P], h0 + 24576)
        LO = at("LO", [P, 8, P], h0 + 28672)

        rdecay, gdecay = small[:, 0:32], small[:, 32:64]
        a_log, dt_bias, fox_bias = small[32:40, 64:65], small[32:40, 65:66], small[0:16, 66:67]
        sel1, sel2 = small[:, 80:111], small[:, 112:142]
        g_exp, k_left, beta_exp = (small[:, c:c + 16].rearrange("p (n h) -> p n h", n=NT) for c in (144, 160, 176))

        g1 = r2 + T_GQ * TP * 4 + 16
        QKVC = at("QKVC", [P, 16, T], a3)
        QC, KC, VC = QKVC[:, 0:4, :], QKVC[:, 4:8, :], QKVC[:, 8:16, :]
        QG = at("QG", [P, 8, T], a3 + 16384)
        VB = at("VB", [P, 8, P], a3 + 24576)
        KBE = at("KBE", [P, 8, P], a3 + 28672)
        KG = at("KG", [P, 8, P], a3 + 32768)
        GAM = at("GAM", [P, 8, P], a3 + 36864)
        AT = at("AT", [P, 8, P], a3 + 40960)
        VN = at("VN", [P, 8, P], a3 + 45056)
        OG = at("OG", [P, 8, T], g1)
        WT = at("WT", [P, 8, P], g1 + 8192)
        U0 = at("U0", [P, 8, P], g1 + 12288)
        gTT = at("gTT", [P, 8, P], r2)
        gTM = at("gTM", [P, 8, P], r2 + 4096)
        gPM = at("gPM", [P, 8, P], r2 + 8192)
        gLO = at("gLO", [P, 8, P], r2 + 12288)
        gLT = at("gLT", [P, 8, P], r2 + 16384)
        gS = at("gS", [P, 8, P], r2 + 20480)
        gBU = at("gBU", [P, 8, P], h0 + 8192)
        ROWS = at("ROWS", [P, T], h0 + 12288)
        RWK = at("RWK", [P, 2, T], h0 + 13312)
        COLS = at("COLS", [P, NT, P], h0 + 24576)
        GSQ = at("GSQ", [P, 8, T], r2)
        HID = at("HID", [P, 2, FT, T], r2, F32R)
        f0 = r2 + 2 * FT * T * 4
        SG = at("SG", [P, 4, T], f0)
        HS = at("HS", [P, 4, T], f0 + 4096)
        UC = at("UC", [P, 8, T + 2], f0)
        YG = at("YG", [P, 4, T], f0 + 8256)
        YV = at("YV", [P, 4, T], f0 + 12352)
        assert f0 + 16448 <= end
        QKV = at("QKV", [P, 48, T], r2)
        FM = at("FM", [P, T], r2 + 49152)
        VT = at("VT", [P, NT, D], r2 + 50176)
        ASQ = at("ASQ", [P, 16, T], r2 + 50176)
        CB = at("CB", [P, A_HEADS, 3, P], r2 + 66560)
        SC = at("SC", [P, 2, 384], r2 + 91136)
        PT = at("PT", [P, 2, 384], r2 + 94208)
        FW = at("FW", [P, 3, T], r2 + 97280)
        AST = at("AST", [P, 2, 8], r2 + 100352)
        FQ = at("FQ", [P, NT, A_HEADS], r2 + 100416)
        OUTT = at("OUTT", [P, NT, D], r2)

        ps = [ctx.enter_context(nc.psum_tensor(f"ps{i}", [P, 512], F32)) for i in range(8)]

        w_in, w_out = io["w_in"][0], io["w_out"][0]

        fox = io["fox_w_in_2"][0]
        wup2 = io["ffn_w_up_2"][0]
        U_MISC1, U_IN = 0, 4
        U_OUT = U_IN + 6 * UG
        U_FFN1 = U_OUT + 2 * UG
        U_DOWN1 = U_FFN1 + 11 * UG
        U_MISC2 = U_DOWN1 + FT
        U_FOX = U_MISC2 + 4
        U_OUT2 = U_FOX + 6 * UG
        U_FFN2 = U_OUT2 + 2 * UG
        U_DOWN2 = U_FFN2 + 11 * UG
        U_END = U_DOWN2 + FT
        N_MISC1, N_IN = 0, 8
        N_OUT = N_IN + 48
        N_FFN1 = N_OUT + 16
        N_DOWN1 = N_FFN1 + 88
        N_MISC2 = N_DOWN1 + 16
        N_FOX = N_MISC2 + 8
        N_OUT2 = N_FOX + 48
        N_FFN2 = N_OUT2 + 16
        N_DOWN2 = N_FFN2 + 88
        N_END = N_DOWN2 + 16

        M_IN, M_OUT, M_FFN1, M_DOWN1, M_FOX, M_OUT2, M_FFN2, M_DOWN2 = 2, 44, 58, 135, 149, 191, 205, 282

        landed = [S(f"weights_landed_{i}") for i in range(RAW_SLOTS)]
        unit_used = S("unit_used")
        hi_made, lo_made = S("hi_made"), S("lo_made")
        bank_freed = S("bank_freed")
        tile_summed = S("tile_summed")
        FREE_UNITS, FREE_BANKS = RAW_SLOTS, 8

        def rows(w, k, c0, n):
            return w[k * P:(k + 1) * P, c0:c0 + n]

        def unit_cols(u):
            return 1536 if u < U_IN else 512 if U_MISC2 <= u < U_FOX else UNIT

        HN = {0: 0, 1: 1, 3: 2, 4: 3}

        block = ctx.enter_context(nc.Block())

        @block.sync
        def _(sp):
            def slot_free(u):
                if isinstance(u, int) and u < RAW_SLOTS:
                    return
                sp.wait_ge(unit_used, u - RAW_SLOTS + 1 + FREE_UNITS)

            def load2(u, j, dsts, srcs):
                slot_free(u)
                for d, s in zip(dsts, srcs):
                    sp.dma_start(d, s).then_inc(landed[j % RAW_SLOTS], 16)

            def halves(j, cols=1024):
                s = RAW[:, j % RAW_SLOTS, :]
                return [s[:, 0:cols], s[:, cols:2 * cols]]

            def stream(u0, groups, sources):
                with sp.Fori(0, groups) as g:
                    for j in range(UG):
                        load2(g * UG + (u0 + j), u0 + j, halves(u0 + j), sources(g, j))

            def stream_down(u0, w):
                for half in range(2):
                    b = u0 + half * (FT // 2)

                    def srcs(k):
                        return [w[bass.ds(k * P + i * P, P) if not isinstance(k, int) else
                                  slice((k + i) * P, (k + i + 1) * P), half * 1024:half * 1024 + 1024]
                                for i in range(2)]
                    for j in range(2):
                        load2(b + j, b + j, halves(b + j), srcs(2 * j))
                    with sp.Fori(0, 5) as i:
                        for j in range(4):
                            load2(i * 4 + (b + 2 + j), b + 2 + j, halves(b + 2 + j), srcs(i * 8 + (4 + 2 * j)))

            for n in range(NT):
                sp.dma_start(XIN[:, n, :], io["x"][0, n * P:(n + 1) * P, :]).then_inc(S(f"x_landed_{n}"), 16)
            sp.wait_ge(S("vpack_zeroed"), 1)
            n_dma = 0
            for i, pack in enumerate(PACKS):
                r = 0
                for name, rows_ in pack:
                    if name.startswith("conv"):
                        src = io["ffn_conv_w_2"][0, int(name[4])].rearrange("(r q) -> r q", q=P)
                    elif name == "gdn_conv_w":
                        src = io[name][0].rearrange("k (r q) -> (k r) q", q=P)
                    elif name == "rwkv_r_k":
                        src = io[name][0].rearrange("(r e) q -> r (e q)", e=2)
                    elif name == "final_norm_w":
                        src = io[name].rearrange("(r q) -> r q", q=P)
                    elif name == "rwkv_mu":
                        src = io[name][0, 0:26 * P].rearrange("(r q) -> r q", q=P)
                        sp.dma_start(VPACK[r + 26:r + 27, i, 0:32], io[name][0:1, 26 * P:N_RWKV])\
                            .then_inc(S("vecs_landed"), 16)
                        n_dma += 1
                        rows_ = 26
                    else:
                        src = io[name][0].rearrange("(r q) -> r q", q=P)
                    sp.dma_start(VPACK[r:r + rows_, i, :], src).then_inc(S("vecs_landed"), 16)
                    n_dma += 1
                    r += 27 if name == "rwkv_mu" else rows_
            counts["vecs_landed"] = 16 * n_dma
            sp.wait_ge(S("misc_zeroed"), 1)
            for j in range(4):
                v = RAW[:, j, 0:1536].rearrange("p (k n) -> p k n", k=4)
                src = w_in[4 * j * P:4 * (j + 1) * P, :].rearrange("(k p) n -> p k n", p=P)
                slot_free(j)
                sp.dma_start(v[:, :, 0:288], src[:, :, 3072:3360]).then_inc(landed[j], 16)
                for e in range(2):
                    sp.dma_start(v[:, :, 288 + 32 * e:296 + 32 * e],
                                 src[:, :, 6432 + 8 * e:6440 + 8 * e]).then_inc(landed[j], 16)
            for part, c0 in ((0, 0), (1, N_RWKV)):
                stream(U_IN + part * 3 * UG, 3, lambda g, j, c0=c0: [
                    w_in[(2 * j + i) * P:(2 * j + i + 1) * P, bass.ds(g * 1024 + c0, 1024)] for i in range(2)])
            stream(U_OUT, 2, lambda g, j: [
                w_out[(2 * j + i) * P:(2 * j + i + 1) * P, bass.ds(g * 1024, 1024)] for i in range(2)])

            def gate_up(w_gate, w_up, shift):
                def sources(g, j):
                    return [w[2 * j * P:(2 * j + 2) * P, bass.ds(g * 512 + c, 512)]
                            .rearrange("(k p) n -> p k n", p=P) for w, c in ((w_gate, 0), (w_up, shift))]
                return sources

            def stream_gate_up(u0, sources):
                with sp.Fori(0, 11) as g:
                    for j in range(UG):
                        v = RAW[:, (u0 + j) % RAW_SLOTS, :].rearrange("p (k a n) -> p a k n", k=2, a=2)
                        load2(g * UG + (u0 + j), u0 + j, [v[:, 0], v[:, 1]], sources(g, j))

            stream_gate_up(U_FFN1, gate_up(io["ffn_w_gate"][0], io["ffn_w_up"][0], 0))
            stream_down(U_DOWN1, io["ffn_w_down"][0])
            for j in range(4):
                u = U_MISC2 + j
                v = RAW[:, j, 0:512].rearrange("p (k n) -> p k n", k=4)
                src = fox[4 * j * P:4 * (j + 1) * P, 6032:6160].rearrange("(k p) n -> p k n", p=P)
                load2(u, j, [v[:, 0:2], v[:, 2:4]], [src[:, 0:2], src[:, 2:4]])
            stream(U_FOX, 6, lambda g, j: [
                fox[(2 * j + i) * P:(2 * j + i + 1) * P, bass.ds(g * 1024, 1024)] for i in range(2)])
            fox_out = io["fox_w_out_2"][0]
            stream(U_OUT2, 2, lambda g, j: [
                fox_out[(2 * j + i) * P:(2 * j + i + 1) * P, bass.ds(g * 1024, 1024)] for i in range(2)])
            stream_gate_up(U_FFN2, gate_up(wup2, wup2, FT * P))
            stream_down(U_DOWN2, io["ffn_w_down_2"][0])
            for n in range(NT):
                for q in range(4):
                    sp.wait_ge(S(f"y_tokens_{n}"), q + 1)
                    sp.dma_start(out[0, n * P:(n + 1) * P, q * 512:(q + 1) * 512],
                                 OUTT[:, n, q * 512:(q + 1) * 512]).then_inc(S("y_stored"), 16)
            sp.wait_ge(S("y_stored"), 16 * 4 * NT)

        @block.gpsimd
        def _(pool):
            def sel(dst, pattern, base, mult, op=ALU.is_ge, fill=0.0):
                tick(nc.gpsimd.affine_select(out=dst, in_=dst, compare_op=op, fill=fill, base=base,
                                             pattern=pattern, channel_multiplier=mult), "pool_step")
                own(pool, "pool_step")

            nc.gpsimd.memset(VPACK[:], 0.0).then_inc(S("vpack_zeroed"), 1)
            for j in range(4):
                v = RAW[:, j, 0:1536].rearrange("p (k n) -> p k n", k=4)
                ins = nc.gpsimd.memset(v[:, :, 288:384], 0.0)
            ins.then_inc(S("misc_zeroed"), 1)
            tick(nc.gpsimd.memset(ident[:], 0.0), "pool_step")
            tick(nc.gpsimd.memset(ones[:], 1.0), "pool_step")
            own(pool, "pool_step")
            nc.gpsimd.affine_select(out=ident[:], in_=ident[:], compare_op=ALU.not_equal, fill=1.0, base=0,
                                    pattern=[[-1, P]], channel_multiplier=1).then_inc(S("ident_made"), 1)
            for i, m in enumerate((2, 4, 8, 16, 32, 64)):
                tick(nc.gpsimd.memset(off[:, i, :], 1.0), "pool_step")
            tick(nc.gpsimd.memset(upper, 1.0), "pool_step")
            tick(nc.gpsimd.memset(upper_eq, 1.0), "pool_step")
            tick(nc.gpsimd.memset(lower1[:], 1.0), "pool_step")
            tick(nc.gpsimd.memset(chunk_go[:], 1.0), "pool_step")
            own(pool, "pool_step")
            tick(nc.gpsimd.memset(chunk_go[:].rearrange("p (c t) -> p c t", t=C)[:, :, 0:1], 0.0), "pool_step")
            for i, m in enumerate((2, 4, 8, 16, 32, 64)):
                sel(off[:, i, :], [[-m, P // m], [0, m]], 0, 1)
                sel(off[:, i, :], [[m, P // m], [0, m]], m - 1, -1)
            sel(upper, [[1, P]], -1, -1)
            sel(upper_eq, [[1, P]], 0, -1)
            sel(lower1[:], [[-1, P]], -1, 1)
            tick(nc.gpsimd.memset(small[:, 80:144], 0.0), "pool_step")
            tick(nc.gpsimd.memset(causal[:], 0.0), "pool_step")
            own(pool, "pool_step")
            tick(nc.gpsimd.memset(small[:, 95:96], 1.0), "pool_step")
            own(pool, "pool_step")
            tick(nc.gpsimd.memset(small[0:64, 126:127], 1.0), "pool_step")
            own(pool, "pool_step")
            tick(nc.gpsimd.memset(small[64:128, 127:128], 1.0), "pool_step")
            own(pool, "pool_step")
            sel(causal[:], [[-1, P]], 0, 1, fill=-1e30)
            pool.sem_inc(S("masks_made"), 1)
            for k, sq in ((1, NSQ), (2, NSQ_H), (4, NSQ)):
                pool.wait_ge(S("squared"), KT * k + 8)
                for n in (4, 2):
                    tick(nc.gpsimd.tensor_tensor(sq[:, 0:n, :], sq[:, 0:n, :], sq[:, n:2 * n, :], ALU.add), "pool_step")
                    own(pool, "pool_step")
                nc.gpsimd.tensor_tensor(sq[:, 0, :], sq[:, 0, :], sq[:, 1, :], ALU.add)\
                    .then_inc(S("squares_presummed"), 1)

        @block.scalar
        def _(act):
            A = nc.scalar.activation

            def hi(u_const, g=None, step=0):
                lv = 32 * (u_const // 4 + 1)
                uv = u_const - HI_SLOTS + 1 + FREE_UNITS
                if g is not None:
                    lv = g * (8 * step) + lv
                    uv = g * step + uv
                if g is None and u_const < 4:
                    act.wait_ge(landed[u_const], 48)
                else:
                    act.wait_ge(landed[u_const % 4], lv + 16)
                act.wait_ge(unit_used, uv)
                n = unit_cols(u_const)
                A(HIW[:, u_const % 2, 0:n], RAW[:, u_const % 4, 0:n], ACT.Copy).then_inc(hi_made, 1)

            def summed(n0, f, u_end, g=None, nf=8, step=8):
                if f < nf - 1:
                    v = n0 // 8 * 7 + f + 1
                    act.wait_ge(tile_summed, v if g is None else g * 7 + v)
                else:
                    v = u_end + FREE_UNITS
                    act.wait_ge(unit_used, v if g is None else g * step + v)

            def group_phase(u0, groups, evac=None, n0=0):
                def rest(g):
                    for j in range(2, UG):
                        hi(u0 + j, g, UG)
                    hi(u0 + UG, g, UG)
                    if evac:
                        evac(g)
                    hi(u0 + UG + 1, g, UG)
                with act.Fori(0, groups) as g:
                    rest(g)

            def squares(n0, half, dst=None):
                for f in range(8 * half, 8 * half + 8):
                    act.wait_ge(bank_freed, n0 + f + 1 + FREE_BANKS)
                    A((dst or NSQ)[:, f, :], X[:, f, :], ACT.Square).then_inc(S("squared"), 1)

            def root(k):
                act.wait_ge(S("variance"), k + 1)
                A(rstd[:], rstd[:], ACT.Sqrt).then_inc(S("rooted"), 1)

            def high_parts(k):
                for e in range(8):
                    act.wait_ge(S("h_full"), 8 * HN[k] + e + 1)
                    A(H[:, 0, 2 * e:2 * e + 2, :], NSQ[:, 2 * e:2 * e + 2, :], ACT.Copy).then_inc(S("h_hi"), 1)

            def out_phase(u0, n0, k):
                for g in range(2):
                    u = u0 + g * UG
                    for j in range(2, UG + 1):
                        hi(u + j)
                    squares(n0, g)
                    if g == 1:
                        root(k)
                    hi(u + UG + 1)
                high_parts(k)

            got = waiter(act)
            for dst, src in ((WA_UP[0:64, :], io["rwkv_w_up"][0]), (WA_UP[64:128, :], io["rwkv_a_up"][0]),
                             (G_UP[:, 0, :], io["rwkv_g_up"][0, 0:P, :]),
                             (G_UP[0:32, 1, :], io["rwkv_g_up"][0, P:160, :])):
                act.dma_start(dst, src).then_inc(S("loras_landed"), 16)
            for dst, src in ((a_log, io["gdn_A_log"][0]), (dt_bias, io["gdn_dt_bias"][0]),
                             (fox_bias, io["fox_b_f_2"][0])):
                act.dma_start(dst, src.rearrange("(h a) -> h a", a=1)).then_inc(S("smalls_landed"), 16)
            for q in range(4):
                act.wait_ge(S("x_turned"), q + 1)
                A(X[:, 4 * q:4 * q + 4, 0:P], ps[q][:, :].rearrange("p (f t) -> p f t", f=4), ACT.Copy)\
                    .then_inc(S("x_tiles"), 1)
            hi(0)
            hi(1)
            act.wait_ge(S("x_tiles"), 8)
            for q in range(4):
                A(NSQ[:, 4 * q:4 * q + 4, :], X[:, 4 * q:4 * q + 4, :], ACT.Square).then_inc(S("squared"), 4)
            root(0)
            high_parts(0)
            hi(2)
            hi(3)
            hi(4)
            hi(5)
            group_phase(U_IN, 6)

            def head_root():
                got("hr_var")
                A(rstd[0:16], rstd[0:16], ACT.Sqrt).then_inc(S("hr_root"), 1)

            got("lowrank_shifted")
            A(PR[0:64, T_WA, PAD:TP], PR[0:64, T_WA, PAD:TP], ACT.Tanh)
            A(PR[0:32, T_G1, PAD:TP], PR[0:32, T_G1, PAD:TP], ACT.Sigmoid)
            A(PR[:, T_G0, PAD:TP], PR[:, T_G0, PAD:TP], ACT.Sigmoid).then_inc(S("lowrank_ready"), 1)
            for name, dst, bias in (("w_lora", EG, "rwkv_w0"), ("a_lora", BH, "rwkv_a0")):
                for t in range(PAIRS):
                    if t % 2 == 0:
                        got(name)
                    b = (0 if dst is EG else 4) + t // 2
                    c = COL[bias] + t
                    ins = A(dst[:, t, :], ps[b][:, (t % 2) * T:(t % 2 + 1) * T], ACT.Sigmoid, bias=vec[:, c:c + 1])
                ins.then_inc(S(f"{name}_sigmoid"), 1)
            got("kq_made")
            A(KK[:], TMP[:], ACT.Square).then_inc(S("hr_sq"), 1)
            head_root()
            got("decay_summed")
            A(EG[:], GS[:], ACT.Exp, scale=-DECAY_RATE).then_inc(S("decay_exp"), 1)
            A(ENG[:], GS[:], ACT.Exp, scale=DECAY_RATE).then_inc(S("decay_exp"), 1)

            def inversion(PM):
                for lev in range(1, 6):
                    for b in range(2):
                        got("inv_p")
                        A(PM[:, 4 * b:4 * b + 4, :], ps[1 + 3 * b][:, :].rearrange("p (h t) -> p h t", h=4),
                          ACT.Copy).then_inc(S("inv_pm"), 1)

            for hb in range(2):
                for n in range(NT):
                    got("tok_turned", 2)
                    A(VTOK[:], ps[0][:, :].rearrange("p (h t) -> p h t", h=4), ACT.Copy).then_inc(S("tok_made"), 1)
                    A(BTOK[:], ps[1][:, :].rearrange("p (h t) -> p h t", h=4), ACT.Copy).then_inc(S("tok_made"), 1)
                    inversion(PM)
                    for c in (2 * n, 2 * n + 1):
                        r = slice(C * (c % 2), C * (c % 2) + C)
                        got("r1_summed")
                        A(R1[r], ps[7][r, :].rearrange("p (h t) -> p h t", h=4), ACT.Copy).then_inc(S("r1_out"), 1)
                        got("y_summed")
                        A(BH[:, 4 * hb:4 * hb + 4, c * C:c * C + C],
                          ps[1][:, 0:256].rearrange("p (h t) -> p h t", h=4), ACT.Copy).then_inc(S("y_out"), 1)
            got("y_centred")
            A(RN[:], BH[:], ACT.Square).then_inc(S("hr_sq"), 1)
            head_root()
            got("ya_full")
            A(H[:, 0, 0:PAIRS, :], BH[:], ACT.Copy).then_inc(S("mix_hi"), 1)

            for f in range(16):
                c = COL["gdn_conv_w"] + f
                A(QKVC[:, f, :], PR[:, T_GQ + f, 1:1 + T], ACT.Copy, scale=vec[:, c:c + 1]).then_inc(S("tap0"), 1)
            got("rows_zeroed")
            A(ROWS[64:72, :], PR[64:72, T_G1, PAD:TP], ACT.Sigmoid).then_inc(S("beta_made"), 1)
            for f in range(0, 16, 4):
                got("conv_made")
                A(QKVC[:, f:f + 4, :], QKVC[:, f:f + 4, :], ACT.Silu).then_inc(S("conv_act"), 1)
            A(PR[:, T_Z:T_Z + 8, PAD:TP], PR[:, T_Z:T_Z + 8, PAD:TP], ACT.Silu).then_inc(S("z_act"), 1)
            got("smalls_landed", 48)
            A(a_log, a_log, ACT.Exp).then_inc(S("a_exp"), 1)
            got("softplus_abs")
            A(RWK[32:40, 1, :], RWK[32:40, 1, :], ACT.Exp, scale=-1.0).then_inc(S("softplus_exp"), 1)
            got("conv_act", 2)
            A(GSQ[:], QKVC[:, 0:8, :], ACT.Square).then_inc(S("hr_sq"), 1)
            got("softplus_plus1")
            A(RWK[32:40, 1, :], RWK[32:40, 1, :], ACT.Ln).then_inc(S("softplus_ln"), 1)
            head_root()
            got("cols_made")
            A(g_exp, COLS[:, :, 32:40], ACT.Exp)
            A(k_left, COLS[:, :, 96:104], ACT.Exp).then_inc(S("cols_exp"), 1)
            for b in range(4):
                got("g_rows")
                A(QG[:, 2 * b:2 * b + 2, :], ps[b][:, :].rearrange("p (h t) -> p h t", h=2), ACT.Exp)\
                    .then_inc(S("g_rows_exp"), 1)
            got("beta_exp_made")
            for n in range(NT):
                got("gam_diff")
                A(GAM[:], GAM[:], ACT.Exp).then_inc(S("gam_exp"), 1)
                got("gtok_turned")
                for h in range(G_HEADS):
                    kt = ps[6][:, (h // 2) * P:(h // 2 + 1) * P]
                    A(KBE[:, h, :], kt, ACT.Copy, scale=beta_exp[:, n, h:h + 1])
                    A(KG[:, h, :], kt, ACT.Copy, scale=k_left[:, n, h:h + 1])
                    if h % 4 == 0:
                        got("gvtok_turned")
                    vt = ps[(7, 4)[h // 4]][:, (h % 4) * P:(h % 4 + 1) * P]
                    ins = A(VB[:, h, :], vt, ACT.Copy, scale=COLS[:, n, 64 + h:65 + h])
                ins.then_inc(S("gtok_made"), 1)
                inversion(gPM)
                for b in range(2):
                    got("u0_summed")
                    A(U0[:, 4 * b:4 * b + 4, :], ps[b][:, :].rearrange("p (h t) -> p h t", h=4), ACT.Copy)\
                        .then_inc(S("u0_out"), 1)
                for c in (2 * n, 2 * n + 1):
                    got("o_summed")
                    A(OG[:, :, c * C:(c + 1) * C], ps[4][:, :].rearrange("p (h t) -> p h t", h=8), ACT.Copy)\
                        .then_inc(S("o_out"), 1)
            got("o_out", 4)
            A(GSQ[:], OG[:], ACT.Square).then_inc(S("hr_sq"), 1)
            head_root()
            got("yb_full")
            A(H[:, 0, PAIRS:KT, :], OG[:], ACT.Copy).then_inc(S("mix_hi"), 1)

            def ffn_phase(u0, evac, tail):
                for j in range(2, UG):
                    hi(u0 + j)
                with act.Fori(0, 10) as g:
                    hi(u0 + UG, g, UG)
                    evac(g)
                    for j in range(1, UG):
                        hi(u0 + UG + j, g, UG)
                        tail(g, j)
                hi(u0 + 11 * UG)
                evac(10)
                hi(u0 + 11 * UG + 1)
                for j in range(1, UG):
                    tail(10, j)

            def down(u0, n0=None, last=False):
                for half in range(2):
                    b = u0 + half * (FT // 2)
                    with act.Fori(0, 5) as i:
                        for j in range(4):
                            hi(b + 2 + j, i, 4)
                    if last and half:
                        return
                    hi(b + 22)
                    if not last:
                        squares(n0, half, NSQ_H)
                    if half and not last:
                        root(2)
                    hi(b + 23)

            def evac_ffn1(g):
                for i in range(4):
                    act.wait_ge(tile_summed, g * 7 + (M_FFN1 + 2 * i + 1))
                    A(SG[:, i, :], ps[2 * i][:, 0:T], ACT.Silu).then_inc(S("gate_act"), 1)

            def tail_ffn1(g, j):
                if j == 1:
                    act.wait_ge(bank_freed, g * 8 + (N_FFN1 + 8 + FREE_BANKS))
                    A(HID[:, 0, bass.ds(g * 4, 4), :], HS[:], ACT.Copy).then_inc(S("hid_hi"), 1)

            out_phase(U_OUT, N_OUT, 1)
            ffn_phase(U_FFN1, evac_ffn1, tail_ffn1)
            down(U_DOWN1, N_DOWN1)
            for f in range(KT):
                act.wait_ge(S("x_scaled"), f + 1)
                A(NSQ[:, f, :], X[:, f, :], ACT.Square).then_inc(S("squared"), 1)
            root(3)
            high_parts(3)
            hi(U_MISC2 + 2)
            hi(U_MISC2 + 3)
            hi(U_FOX)
            hi(U_FOX + 1)
            group_phase(U_FOX, 6)

            for part in range(2):
                got("att_in")
                A(ASQ[:], QKV[:, 16 * part:16 * part + 16, :], ACT.Square).then_inc(S("hr_sq"), 1)
                head_root()
            got("softplus_abs")
            A(FW[0:16, 1, :], FW[0:16, 1, :], ACT.Exp, scale=-1.0).then_inc(S("softplus_exp"), 1)
            got("softplus_plus1")
            A(FW[0:16, 1, :], FW[0:16, 1, :], ACT.Ln).then_inc(S("softplus_ln"), 1)
            for b in range(0, 8, 2):
                got("v_turned_a")
                A(VT[:, b // 4, (b % 4) * 512:(b % 4 + 1) * 512], ps[b][:, :], ACT.Copy).then_inc(S("vt_made_a"), 1)
            for h in range(A_HEADS):
                z = h % 2
                for n, c0, w in ((0, 0, P), (1, P, T)):
                    got("score_max")
                    A(SC[:, z, c0:c0 + w], SC[:, z, c0:c0 + w], ACT.Exp, bias=AST[:, z, n:n + 1],
                      accum_out=AST[:, z, 2 + n:3 + n]).then_inc(S("prob_made"), 1)
                got("pt_turned")
                A(PT[:, z, :], ps[2 + z][:, 0:384], ACT.Copy).then_inc(S("pt_made"), 1)
                got("att_summed")
                A(H[:, 0, h, :], ps[4 + z][:, 0:T], ACT.Copy).then_inc(S("att_hi"), 1)
            out_phase(U_OUT2, N_OUT2, 4)

            def evac_ffn2(g):
                for i in range(GROUP):
                    if i < GROUP - 1:
                        act.wait_ge(tile_summed, g * 7 + (M_FFN2 + i + 1))
                    else:
                        act.wait_ge(unit_used, g * UG + (U_FFN2 + UG + FREE_UNITS))
                    if i == 0:
                        act.wait_ge(S("hid_made"), g + 12)
                    A(UC[:, i, 2:2 + T], ps[i][:, 0:T], ACT.Copy).then_inc(bank_freed, 1)

            def tail_ffn2(g, j):
                if j == 3:
                    act.wait_ge(S("conv_step"), g * 3 + 3)
                    A(YG[:], YG[:], ACT.Silu).then_inc(S("conv_gate"), 1)
                elif j == 5:
                    act.wait_ge(S("hid_full"), g + 1)
                    A(HID[:, 0, bass.ds(g * 4, 4), :], YV[:], ACT.Copy).then_inc(S("hid_hi"), 1)
            ffn_phase(U_FFN2, evac_ffn2, tail_ffn2)
            down(U_DOWN2, last=True)
            for q in range(4):
                got("y_turned_a")
                A(OUTT[:, 0, q * 512:(q + 1) * 512], ps[q][:, :], ACT.Copy).then_inc(S("y_tokens_0"), 1)

        @block.vector
        def _(dve):
            V = nc.vector

            def step(ins):
                tick(ins, "dve_step")

            def settle():
                own(dve, "dve_step")

            def lo(u_const, g=None, stepu=0):
                v = u_const + 1
                dve.wait_ge(hi_made, v if g is None else g * stepu + v)
                n = unit_cols(u_const)
                V.tensor_tensor(LOW[:, u_const % 4, 0:n], RAW[:, u_const % 4, 0:n],
                                HIW[:, u_const % 2, 0:n].bitcast(F32), ALU.subtract).then_inc(lo_made, 1)

            def summed(n7, f, u_end, g=None, nf=8, stepu=UG):
                if f < nf - 1:
                    v = n7 + f + 1
                    dve.wait_ge(tile_summed, v if g is None else g * 7 + v)
                else:
                    v = u_end + FREE_UNITS
                    dve.wait_ge(unit_used, v if g is None else g * stepu + v)

            def group_phase(u0, groups, evac):
                with dve.Fori(0, groups) as g:
                    for j in range(2, UG):
                        lo(u0 + j, g, UG)
                    lo(u0 + UG, g, UG)
                    evac(g)
                    lo(u0 + UG + 1, g, UG)

            def inverse_root(k, eps):
                dve.wait_ge(S("squares_summed"), k + 1)
                V.tensor_scalar(rstd[:], ps[0][:, 0:T], 1.0 / D, eps, ALU.mult, ALU.add)\
                    .then_inc(S("variance"), 1)
                dve.wait_ge(S("rooted"), k + 1)
                step(V.reciprocal(rstd[:], rstd[:]))
                settle()

            def norm(k, gain, eps, between=None):
                inverse_root(k, eps)
                c = COL[gain]
                for e in range(9):
                    if e < 8:
                        for f in (2 * e, 2 * e + 1):
                            ins = V.scalar_tensor_tensor(NSQ[:, f, :], X[:, f, :], vec[:, c + f:c + f + 1], rstd[:],
                                                         ALU.mult, ALU.mult)
                        ins.then_inc(S("h_full"), 1)
                    if e == 2 and between:
                        between()
                    if e > 0:
                        dve.wait_ge(S("h_hi"), 8 * HN[k] + e)
                        s = slice(2 * e - 2, 2 * e)
                        V.tensor_tensor(H[:, 1, s, :], NSQ[:, s, :], H[:, 0, s, :].bitcast(F32), ALU.subtract)\
                            .then_inc(S("h_made"), 1)

            for q in range(4):
                dve.wait_ge(S("x_turned"), 5 + q)
                V.tensor_copy(X[:, 4 * q:4 * q + 4, P:T], ps[4 + q][:, :].rearrange("p (f t) -> p f t", f=4))\
                    .then_inc(S("x_tiles"), 1)
            c0 = 0
            for i, pack in enumerate(PACKS):
                r = sum(n for _, n in pack)
                dve.wait_ge(S("vecs_turned"), i + 1)
                V.tensor_copy(vec[:, c0:c0 + r], ps[i % 4][:, (i // 4) * P:(i // 4) * P + r])\
                    .then_inc(S("vecs_made"), 1)
                c0 += r
            dve.wait_ge(S("vecs_made"), len(PACKS))
            dve.wait_ge(S("masks_made"), 1)
            step(V.tensor_tensor(upper, upper, off[:, 5, :], ALU.mult))
            step(V.tensor_tensor(upper_eq, upper_eq, off[:, 5, :], ALU.mult))
            step(V.tensor_tensor(lower1[:], lower1[:], off[:, 0, :], ALU.mult))
            step(V.tensor_copy(headones[:], off[:, 5, :]))
            settle()
            for i in range(5, -1, -1):
                inner = off[:, i - 1, :] if i else ident[:]
                step(V.tensor_tensor(off[:, i, :], off[:, i, :], inner, ALU.subtract))
                settle()
                step(V.tensor_tensor(off[:, i, :], off[:, i, :], upper, ALU.mult))
            settle()
            dve.sem_inc(bank_freed, FREE_BANKS)
            lo(0)
            lo(1)
            norm(0, "attn_norm_w", 1e-5)
            dve.wait_ge(S("h_made"), 8)
            step(V.memset(PR[:, :, 0:PAD], 0.0))
            lo(2)
            lo(3)
            lo(4)
            for f in range(3):
                summed(0, f, U_IN, nf=3)
                V.tensor_copy(PR[:, f, PAD:TP], ps[f][:, 0:T]).then_inc(bank_freed, 6 if f == 2 else 1)
            lo(5)

            def evac_in(g):
                for f in range(GROUP):
                    summed(2, f, U_IN + UG, g)
                    V.tensor_copy(PR[:, bass.ds(g * 8 + (3 + f), 1), PAD:TP], ps[f][:, 0:T])\
                        .then_inc(bank_freed, 1)
            group_phase(U_IN, 6, evac_in)

            got = waiter(dve)

            def head_rsqrt(scale, eps, after=None):
                got("hr_sum")
                V.tensor_scalar(rstd[0:16], ps[0][0:16, 0:T], scale, eps, ALU.mult, ALU.add).then_inc(S("hr_var"), 1)
                got("hr_root")
                if after is None:
                    V.reciprocal(rstd[0:16], rstd[0:16]).then_inc(S("hr_inv"), 1)
                else:
                    step(V.reciprocal(rstd[0:16], rstd[0:16]))
                    settle()
                    after().then_inc(S("hr_inv"), 1)

            def pair_of(b):
                return ps[b][:, :].rearrange("p (a t) -> p a t", a=2)

            dve.wait_ge(bank_freed, FREE_BANKS + N_OUT)
            step(V.tensor_tensor(SHIFT[:], PR[:, 0:27, PAD - 1:TP - 1], PR[:, 0:27, PAD:TP], ALU.subtract))
            settle()
            mu = {T_WA: 24, T_G0: 25, T_G1: 26}
            for f in [0, 1, 2] + list(range(T_K, T_V)) + list(range(T_V, T_GQ)) + list(range(T_R, T_K)):
                c = COL["rwkv_mu"] + mu.get(f, f - 3)
                ins = V.scalar_tensor_tensor(PR[:, f, PAD:TP], SHIFT[:, f, :], vec[:, c:c + 1], PR[:, f, PAD:TP],
                                             ALU.mult, ALU.add)
                if f == T_G1:
                    ins.then_inc(S("lowrank_shifted"), 1)
                elif f == T_K - 1:
                    step(ins)
            settle()
            Rf, Kf, Vf = (PR[:, t:t + PAIRS, PAD:TP] for t in (T_R, T_K, T_V))
            for t in range(PAIRS):
                c = COL["rwkv_k_k"] + t
                ins = V.tensor_scalar(TMP[:, t, :], Kf[:, t, :], vec[:, c:c + 1], None, ALU.mult)
            ins.then_inc(S("kq_made"), 1)
            got("w_lora_sigmoid")
            for t in range(PAIRS):
                ins = V.tensor_tensor_scan(GS[:, t, :], chunk_go[:], EG[:, t, :], 0.0, ALU.mult, ALU.add)
            ins.then_inc(S("decay_summed"), 1)
            head_rsqrt(1.0, 1e-12)
            for q in range(4):
                got("hr_bc")
                step(V.tensor_tensor(KK[:, 2 * q:2 * q + 2, :], TMP[:, 2 * q:2 * q + 2, :], pair_of(q), ALU.mult))
            settle()
            got("a_lora_sigmoid")
            for t in range(PAIRS):
                c = COL["rwkv_k_a"] + t
                ins = V.tensor_scalar(TMP[:, t, :], BH[:, t, :], 1.0, vec[:, c:c + 1], ALU.subtract, ALU.mult)
            step(ins)
            settle()
            step(V.scalar_tensor_tensor(Kf, TMP[:], 1.0, Kf, ALU.add, ALU.mult))
            step(V.tensor_tensor(BH[:], KK[:], BH[:], ALU.mult))
            settle()
            for t in range(PAIRS):
                c = COL["rwkv_r_k"] + t
                ins = V.scalar_tensor_tensor(RN[:, t, :], Rf[:, t, :], vec[:, c:c + 1], Kf[:, t, :],
                                             ALU.mult, ALU.mult)
            ins.then_inc(S("bonus_terms"), 1)
            got("bonus_terms")
            got("decay_exp")
            step(V.tensor_copy(small[:, 0:32], EG[:].rearrange("p t (c j) -> p (t c) j", j=C)[:, :, C - 1]))
            got("decay_exp")
            step(V.tensor_tensor(BH[:], BH[:], ENG[:], ALU.mult))
            step(V.tensor_tensor(Kf, Kf, ENG[:], ALU.mult))
            for q in range(4):
                got("bonus_summed")
                step(V.tensor_tensor(BON[:, 2 * q:2 * q + 2, :], ps[4 + q][:, :].rearrange("p (a t) -> p a t", a=2),
                                     Vf[:, 2 * q:2 * q + 2, :], ALU.mult))
            step(V.tensor_tensor(AR[:, :, 1, :], Rf, EG[:], ALU.mult))
            for t in range(PAIRS):
                a_t = AR[:, t, 0, :].rearrange("p (c j) -> p c j", j=C)
                kk_t = KK[:, t, :].rearrange("p (c j) -> p c j", j=C)
                eg_t = EG[:, t, :].rearrange("p (c j) -> p c j", j=C)
                V.scalar_tensor_tensor(a_t[:, :, 1:C], kk_t[:, :, 1:C], -1.0, eg_t[:, :, 0:C - 1], ALU.mult, ALU.mult)
                ins = V.tensor_scalar(a_t[:, :, 0:1], kk_t[:, :, 0:1], -1.0, None, ALU.mult)
            step(ins)
            settle()
            step(V.memset(R1[:], 0.0))
            step(V.memset(UU[:], 0.0))
            settle()
            dve.sem_inc(S("hats_made"), 1)

            def bank(b):
                return ps[b][:, :].rearrange("p (h t) -> p h t", h=4)

            def many(m, n):
                return m.unsqueeze(1).broadcast_to([P, n, m.shape[-1]])

            def inversion(lt, LO, TM, TT):
                def lo_part(lev, b):
                    V.tensor_tensor(LO[:, 4 * b:4 * b + 4, :], lt(b), many(off[:, lev, :], 4), ALU.mult)\
                        .then_inc(S("inv_off"), 1)
                for b in range(2):
                    lo_part(1, b)
                for lev in range(1, 6):
                    for b in range(2):
                        s8 = slice(4 * b, 4 * b + 4)
                        got("inv_t")
                        if lev < 5:
                            V.tensor_tensor(TM[:, s8, :], TM[:, s8, :], bank(2 + 3 * b), ALU.add)
                        V.tensor_tensor(TT[:, s8, :], TT[:, s8, :], bank(3 + 3 * b), ALU.add)\
                            .then_inc(S("inv_added"), 1)
                        if lev < 5:
                            lo_part(lev + 1, b)

            for hb in range(2):
                step(V.memset(ST[:], 0.0))
                for n in range(NT):
                    got("ktok_turned")
                    V.tensor_copy(KTOK[:], bank(2)).then_inc(S("ktok_made"), 1)
                    for M in (LBR, LKR):
                        for q in range(4):
                            got("l_summed")
                            dst = M[:, 2 * q:2 * q + 2, :, :].rearrange("p h a t -> p h (a t)")
                            src = ps[3 + q][:, :].rearrange("p (h t) -> p h t", h=2)
                            tick(V.tensor_tensor(dst, src, many(upper2[:].rearrange("p a t -> p (a t)"), 2),
                                                 ALU.mult), "l_out")
                    for b in range(2):
                        got("l_plain")
                        tick(V.tensor_tensor(TM[:, 4 * b:4 * b + 4, :], bank((7, 0)[b]), many(lower1[:], 4), ALU.mult),
                             "l_out")
                    own(dve, "l_out")
                    step(V.tensor_tensor(TT[:], LBR[:, :, 0, :], many(off[:, 0, :], 8), ALU.mult))
                    step(V.tensor_tensor(TM[:], TM[:], many(ident[:], 8), ALU.add))
                    settle()
                    step(V.tensor_tensor(TT[:], TT[:], many(ident[:], 8), ALU.add))
                    settle()
                    dve.sem_inc(S("inv_start"), 1)
                    inversion(lambda b: LBR[:, 4 * b:4 * b + 4, 0, :], LO, TM, TT)
                    for c in (2 * n, 2 * n + 1):
                        r = slice(C * (c % 2), C * (c % 2) + C)
                        got("u_summed")
                        V.tensor_copy(UU[r], ps[0][r, :].rearrange("p (h t) -> p h t", h=4)).then_inc(S("u_out"), 1)
                        got("s_summed")
                        step(V.tensor_tensor(PM[:, 0:4, :], bank(2), many(headones[:], 4), ALU.mult))
                        settle()
                        step(V.tensor_tensor(ST[:], ST[:], PM[:, 0:4, :], ALU.add))
                        settle()
                        dc = small[:, 0:32].rearrange("p (t c) -> p t c", c=NCH)[:, 4 * hb:4 * hb + 4, c:c + 1]
                        step(V.tensor_tensor(ST[:], ST[:], dc.broadcast_to([P, 4, P]), ALU.mult))
                        settle()
                        dve.sem_inc(S("s_out"), 1)
            for q in range(4):
                got("y_mean")
                if q == 0:
                    dve.wait_ge(S("y_out"), 8)
                b2 = BH[:, 2 * q:2 * q + 2, :]
                ins = V.scalar_tensor_tensor(b2, ps[q][:, :].rearrange("p (a t) -> p a t", a=2), -1.0 / R_HEAD, b2,
                                             ALU.mult, ALU.add)
            ins.then_inc(S("y_centred"), 1)
            head_rsqrt(1.0 / R_HEAD, R_HEAD * 1e-5)
            for q in range(4):
                got("hr_bc")
                step(V.tensor_tensor(BH[:, 2 * q:2 * q + 2, :], BH[:, 2 * q:2 * q + 2, :], pair_of(q), ALU.mult))
            settle()
            dve.sem_inc(S("y_normed"), 1)
            for t in range(PAIRS):
                cw, cb = COL["rwkv_ln_w"] + t, COL["rwkv_ln_b"] + t
                ins = V.tensor_scalar(BH[:, t, :], BH[:, t, :], vec[:, cw:cw + 1], vec[:, cb:cb + 1],
                                      ALU.mult, ALU.add)
            step(ins)
            settle()
            step(V.tensor_tensor(BH[:], BH[:], BON[:], ALU.add))
            settle()
            for q in range(4):
                got("gate_summed")
                b2 = BH[:, 2 * q:2 * q + 2, :]
                ins = V.tensor_tensor(b2, b2, ps[q][:, :].rearrange("p (a t) -> p a t", a=2), ALU.mult)
            ins.then_inc(S("ya_full"), 1)
            got("mix_hi")
            V.tensor_tensor(H[:, 1, 0:PAIRS, :], BH[:], H[:, 0, 0:PAIRS, :].bitcast(F32), ALU.subtract)\
                .then_inc(S("mix_made"), 1)

            settle()
            step(V.memset(ROWS[:], 0.0))
            settle()
            dve.sem_inc(S("rows_zeroed"), 1)
            for tap in range(1, 4):
                for f in range(16):
                    if tap == 1:
                        got("tap0")
                    c = COL["gdn_conv_w"] + 16 * tap + f
                    ins = V.scalar_tensor_tensor(QKVC[:, f, :], PR[:, T_GQ + f, 1 + tap:1 + tap + T],
                                                 vec[:, c:c + 1], QKVC[:, f, :], ALU.mult, ALU.add)
                    if tap == 3 and f % 4 == 3:
                        ins.then_inc(S("conv_made"), 1)
                if tap < 3:
                    step(ins)
                    settle()
            dve.wait_ge(S("smalls_landed"), 48)
            g32 = slice(32, 40)
            step(V.tensor_scalar(RWK[g32, 0, :], PR[g32, T_G1, PAD:TP], dt_bias, None, ALU.add))
            settle()
            step(V.tensor_scalar(RWK[g32, 1, :], RWK[g32, 0, :], -1.0, None, ALU.mult))
            settle()
            step(V.tensor_tensor(RWK[g32, 1, :], RWK[g32, 1, :], RWK[g32, 0, :], ALU.max))
            settle()
            dve.sem_inc(S("softplus_abs"), 1)
            step(V.tensor_scalar(RWK[g32, 0, :], RWK[g32, 0, :], 0.0, None, ALU.max))
            got("softplus_exp")
            V.tensor_scalar(RWK[g32, 1, :], RWK[g32, 1, :], 1.0, None, ALU.add).then_inc(S("softplus_plus1"), 1)
            got("softplus_ln")
            step(V.tensor_tensor(RWK[g32, 0, :], RWK[g32, 0, :], RWK[g32, 1, :], ALU.add))
            settle()
            got("a_exp")
            step(V.tensor_scalar(RWK[g32, 0, :], RWK[g32, 0, :], a_log, -1.0, ALU.mult, ALU.mult))
            settle()
            step(V.tensor_tensor_scan(ROWS[g32, :], chunk_go[g32, :], RWK[g32, 0, :], 0.0, ALU.mult, ALU.add))
            settle()
            gc = ROWS[g32, :].rearrange("p (c j) -> p c j", j=C)
            V.tensor_tensor(ROWS[96:104, :].rearrange("p (c j) -> p c j", j=C),
                            gc[:, :, C - 1:C].broadcast_to([8, NCH, C]), gc, ALU.subtract).then_inc(S("rows_made"), 1)
            head_rsqrt(1.0, 1e-6)
            for q in range(4):
                got("hr_bc")
                s2 = QKVC[:, 2 * q:2 * q + 2, :]
                if q < 2:
                    ins = V.scalar_tensor_tensor(s2, s2, float(P) ** -0.5, pair_of(q), ALU.mult, ALU.mult)
                else:
                    ins = V.tensor_tensor(s2, s2, pair_of(q), ALU.mult)
            ins.then_inc(S("gqk_normed"), 1)
            got("cols_turned")
            V.tensor_copy(COLS[:], ps[4][:, 0:T].rearrange("p (n t) -> p n t", n=NT)).then_inc(S("cols_made"), 1)
            got("cols_exp")
            V.tensor_tensor(beta_exp, g_exp, COLS[:, :, 64:72], ALU.mult).then_inc(S("beta_exp_made"), 1)
            got("g_rows_exp", 4)
            got("gqk_normed")
            step(V.tensor_copy(gdecay, QG[:].rearrange("p h (c j) -> p (h c) j", j=C)[:, :, C - 1]))
            settle()
            step(V.tensor_tensor(QG[:].rearrange("p (a b) t -> p a b t", b=2),
                                 QC.unsqueeze(2).broadcast_to([P, 4, 2, T]),
                                 QG[:].rearrange("p (a b) t -> p a b t", b=2), ALU.mult))
            step(V.memset(gS[:], 0.0))
            step(V.memset(VN[:], 0.0))
            settle()
            for n in range(NT):
                for h in range(G_HEADS):
                    ins = V.tensor_scalar(GAM[:, h, :], ps[h // 2][:, (h % 2) * T + n * P:(h % 2) * T + n * P + P],
                                          COLS[:, n, 32 + h:33 + h], 0.0, ALU.subtract, ALU.min)
                ins.then_inc(S("gam_diff"), 1)
                got("beta_rows", 2)
                for b in range(2):
                    src = ps[4 + b][:, :].rearrange("p (h t) -> p h t", h=4)
                    ins = V.scalar_tensor_tensor(gBU[:, 4 * b:4 * b + 4, :], src, -1.0, many(upper, 4),
                                                 ALU.mult, ALU.mult)
                ins.then_inc(S("beta_rows_out"), 1)
                got("gam_exp")
                got("beta_rows_out")
                step(V.tensor_tensor(GAM[:], GAM[:], many(upper_eq, 8), ALU.mult))
                settle()

                def twice(b):
                    return ps[b][:, :].rearrange("p (a t) -> p a t", a=4).unsqueeze(2).broadcast_to([P, 4, 2, P])
                g4 = GAM[:].rearrange("p (a b) t -> p a b t", b=2)
                got("gkk_summed", 2)
                step(V.tensor_tensor(gLT[:].rearrange("p (a b) t -> p a b t", b=2), g4, twice(4), ALU.mult))
                step(V.tensor_tensor(AT[:].rearrange("p (a b) t -> p a b t", b=2), g4, twice(5), ALU.mult))
                settle()
                step(V.tensor_tensor(gLT[:], gLT[:], gBU[:], ALU.mult))
                settle()
                step(V.tensor_tensor(gTT[:], gLT[:], many(off[:, 0, :], 8), ALU.mult))
                settle()
                step(V.tensor_tensor(gTT[:], gTT[:], many(ident[:], 8), ALU.add))
                settle()
                dve.sem_inc(S("gtt_start"), 1)
                for b in range(2):
                    got("gtm_turned")
                    step(V.tensor_copy(gTM[:, 4 * b:4 * b + 4, :], bank((7, 4)[b])))
                settle()
                dve.sem_inc(S("inv_start"), 1)
                inversion(lambda b: gLT[:, 4 * b:4 * b + 4, :], gLO, gTM, gTT)
                for b in range(2):
                    got("wt_summed")
                    V.tensor_copy(WT[:, 4 * b:4 * b + 4, :], bank(2 + b)).then_inc(S("wt_out"), 1)
                got("u0_out", 2)
                for c in (2 * n, 2 * n + 1):
                    r = slice(C * (c % 2), C * (c % 2) + C)
                    for b in range(2):
                        got("ws_summed")
                        ins = V.tensor_tensor(VN[r, 4 * b:4 * b + 4, :], U0[r, 4 * b:4 * b + 4, :],
                                              ps[b][r, :].rearrange("p (h t) -> p h t", h=4), ALU.subtract)
                    ins.then_inc(S("vn_made"), 1)
                    got("gs_summed")
                    for h in range(G_HEADS):
                        k = 4 * h + c
                        ins = V.scalar_tensor_tensor(gS[:, h, :], gS[:, h, :], gdecay[:, k:k + 1],
                                                     ps[2 + h // 4][:, (h % 4) * P:(h % 4 + 1) * P],
                                                     ALU.mult, ALU.add)
                    ins.then_inc(S("gs_out"), 1)
                    got("gs_out")
                if n == 0:
                    got("g_rows_again", 4)
            head_rsqrt(1.0 / P, 1e-6)
            got("z_act")
            for q in range(4):
                got("hr_bc")
                s2 = slice(2 * q, 2 * q + 2)
                step(V.tensor_tensor(OG[:, s2, :], OG[:, s2, :], pair_of(q), ALU.mult))
            settle()
            c = COL["gdn_norm_w"]
            V.scalar_tensor_tensor(OG[:], OG[:], vec[:, c:c + 1], PR[:, T_Z:T_Z + 8, PAD:TP], ALU.mult, ALU.mult)\
                .then_inc(S("yb_full"), 1)
            got("mix_hi")
            V.tensor_tensor(H[:, 1, PAIRS:KT, :], OG[:], H[:, 0, PAIRS:KT, :].bitcast(F32), ALU.subtract)\
                .then_inc(S("mix_made"), 1)

            def residual(m0, u_end, half):
                for f in range(GROUP):
                    summed(m0, f, u_end)
                    x = X[:, half * 8 + f, :]
                    V.tensor_tensor(x, x, ps[f][:, 0:T], ALU.add).then_inc(bank_freed, 1)

            def out_phase(u0, n0, m0, norm_args):
                for g in range(2):
                    u = u0 + g * UG
                    for j in range(2, UG + 1):
                        lo(u + j)
                    residual(m0 + 7 * g, u + UG, g)
                    if g == 0:
                        lo(u + UG + 1)
                dve.wait_ge(bank_freed, n0 + 16 + FREE_BANKS)
                norm(*norm_args, between=lambda: lo(u0 + 2 * UG + 1))

            def down(u0, m0, last=False):
                for half in range(2):
                    b = u0 + half * (FT // 2)
                    with dve.Fori(0, 5) as i:
                        for j in range(4):
                            lo(b + 2 + j, i, 4)
                    if not (last and half):
                        lo(b + 22)
                    residual(m0 + 7 * half, b + 22, half)
                    if not half:
                        lo(b + 23)

            out_phase(U_OUT, N_OUT, M_OUT, (1, "ffn_norm_w", 1e-5))
            dve.sem_inc(S("hid_made"), 1)

            def ffn_phase(u0, evac, tail):
                for j in range(2, UG):
                    lo(u0 + j)
                with dve.Fori(0, 10) as g:
                    lo(u0 + UG, g, UG)
                    evac(g)
                    for j in range(1, UG):
                        lo(u0 + UG + j, g, UG)
                        tail(g, j)
                lo(u0 + 11 * UG)
                evac(10)
                lo(u0 + 11 * UG + 1)
                for j in range(1, UG):
                    tail(10, j)

            def evac_ffn1(g):
                for i in range(4):
                    dve.wait_ge(S("gate_act"), g * 4 + (i + 1))
                    if i == 0:
                        dve.wait_ge(S("hid_made"), g + 1)
                    summed(M_FFN1, 2 * i + 1, U_FFN1 + UG, g)
                    V.tensor_tensor(HS[:, i, :], SG[:, i, :], ps[2 * i + 1][:, 0:T], ALU.mult).then_inc(bank_freed, 2)

            def tail_ffn1(g, j):
                if j == 1:
                    dve.wait_ge(S("hid_hi"), g + 1)
                    V.tensor_tensor(HID[:, 1, bass.ds(g * 4, 4), :], HS[:],
                                    HID[:, 0, bass.ds(g * 4, 4), :].bitcast(F32), ALU.subtract)\
                        .then_inc(S("hid_made"), 1)
            ffn_phase(U_FFN1, evac_ffn1, tail_ffn1)
            down(U_DOWN1, M_DOWN1)
            dve.wait_ge(bank_freed, N_MISC2 + FREE_BANKS)
            inverse_root(2, 1e-5)
            c = COL["final_norm_w"]
            for f in range(KT):
                V.scalar_tensor_tensor(X[:, f, :], X[:, f, :], vec[:, c + f:c + f + 1], rstd[:], ALU.mult, ALU.mult)\
                    .then_inc(S("x_scaled"), 1)
            lo(U_MISC2 + 1)
            dve.wait_ge(S("x_scaled"), KT)
            norm(3, "mix_norm_2", 1e-6)
            lo(U_MISC2 + 2)
            lo(U_MISC2 + 3)
            lo(U_FOX)
            dve.wait_ge(unit_used, U_FOX + FREE_UNITS)
            V.tensor_copy(FM[:], ps[0][:, 0:T]).then_inc(bank_freed, 8)
            lo(U_FOX + 1)

            def evac_fox(g):
                for f in range(GROUP):
                    summed(M_FOX, f, U_FOX + UG, g)
                    V.tensor_copy(QKV[:, bass.ds(g * 8 + f, 1), :], ps[f][:, 0:T]).then_inc(bank_freed, 1)
            group_phase(U_FOX, 6, evac_fox)

            dve.wait_ge(bank_freed, N_OUT2 + FREE_BANKS)
            dve.sem_inc(S("att_in"), 1)
            got("f_rows")
            f16 = slice(0, 16)
            step(V.tensor_scalar(FW[f16, 0, :], ps[7][f16, 0:T], fox_bias, -1.0, ALU.add, ALU.mult))
            settle()
            step(V.tensor_scalar(FW[f16, 1, :], FW[f16, 0, :], -1.0, None, ALU.mult))
            settle()
            step(V.tensor_tensor(FW[f16, 1, :], FW[f16, 1, :], FW[f16, 0, :], ALU.max))
            step(V.tensor_scalar(FW[f16, 2, :], FW[f16, 0, :], 0.0, None, ALU.max))
            settle()
            for part, gain in enumerate(("fox_q_gain_2", "fox_k_gain_2")):
                c = COL[gain]
                head_rsqrt(1.0 / P, 1e-6)
                for q in range(8):
                    got("hr_bc")
                    s2 = QKV[:, 16 * part + 2 * q:16 * part + 2 * q + 2, :]
                    step(V.scalar_tensor_tensor(s2, s2, vec[:, c:c + 1], pair_of(q), ALU.mult, ALU.mult))
                settle()
                if part == 0:
                    step(V.tensor_scalar(QKV[:, 0:16, :], QKV[:, 0:16, :], float(P) ** -0.5, None, ALU.mult))
                    settle()
                    dve.sem_inc(S("att_in"), 1)
                    dve.sem_inc(S("softplus_abs"), 1)
            dve.sem_inc(S("qk_normed"), 1)
            got("softplus_exp")
            V.tensor_scalar(FW[f16, 1, :], FW[f16, 1, :], 1.0, None, ALU.add).then_inc(S("softplus_plus1"), 1)
            got("softplus_ln")
            step(V.tensor_tensor(FW[f16, 0, :], FW[f16, 1, :], FW[f16, 2, :], ALU.add))
            settle()
            step(V.memset(FW[f16, 1, :], 1.0))
            settle()
            V.tensor_tensor_scan(FW[f16, 2, :], FW[f16, 1, :], FW[f16, 0, :], 0.0, ALU.mult, ALU.add)\
                .then_inc(S("forget_summed"), 1)
            for b in range(1, 8, 2):
                got("v_turned_v")
                V.tensor_copy(VT[:, b // 4, (b % 4) * 512:(b % 4 + 1) * 512], ps[b][:, :]).then_inc(S("vt_made_v"), 1)
            got("forget_cols")
            V.tensor_copy(FQ[:], ps[0][:, 0:32].rearrange("p (n h) -> p n h", n=NT)).then_inc(S("forget_cols_out"), 1)
            for q in range(8):
                got("forget_rows")
                rows2 = ps[q][:, :].rearrange("p (h n t) -> p h n t", h=2, n=2)
                cb = CB[:, 2 * q:2 * q + 2, :, :]
                V.tensor_tensor(cb[:, :, 0, :], rows2[:, :, 0, :], many(causal[:], 2), ALU.add)
                V.tensor_copy(cb[:, :, 1, :], rows2[:, :, 0, :])
                V.tensor_tensor(cb[:, :, 2, :], rows2[:, :, 1, :], many(causal[:], 2), ALU.add)\
                    .then_inc(S("bias_made"), 1)
            got("bias_made", 8)

            def probs(h):
                z = h % 2
                got("scores_made")
                for n, c0, w, blk in ((0, 0, P, 0), (1, P, T, 1)):
                    src = CB[:, h, blk:blk + w // P, :].rearrange("p b t -> p (b t)")
                    step(V.scalar_tensor_tensor(SC[:, z, c0:c0 + w], src, FQ[:, n, h:h + 1], ps[z][:, c0:c0 + w],
                                                ALU.subtract, ALU.add))
                settle()
                for n, c0, w in ((0, 0, P), (1, P, T)):
                    V.tensor_reduce(AST[:, z, n:n + 1], SC[:, z, c0:c0 + w], AX_X, ALU.max, negate=True)\
                        .then_inc(S("score_max"), 1)
                got("prob_made", 2)
                step(V.reciprocal(AST[:, z, 4:6], AST[:, z, 2:4]))
                settle()
                for n, c0, w in ((0, 0, P), (1, P, T)):
                    ins = V.tensor_scalar(SC[:, z, c0:c0 + w], SC[:, z, c0:c0 + w], AST[:, z, 4 + n:5 + n], None,
                                          ALU.mult)
                ins.then_inc(S("prob_normed"), 1)

            def out_lo(h):
                got("att_hi")
                V.tensor_tensor(H[:, 1, h, :], ps[4 + h % 2][:, 0:T], H[:, 0, h, :].bitcast(F32), ALU.subtract)\
                    .then_inc(S("att_made"), 1)
            for h in range(A_HEADS):
                probs(h)
                if h:
                    out_lo(h - 1)
            out_lo(A_HEADS - 1)

            out_phase(U_OUT2, N_OUT2, M_OUT2, (4, "ffn_norm_2", 1e-6))
            step(V.memset(UC[:, :, 0:2], 0.0))
            settle()

            def y(i):
                return (YG, YV)[i % 2][:, i // 2, :]

            def tap(g, k, i):
                c = COL[f"conv{k}"] + (i % 2) * FT + i // 2
                return vec[:, bass.ds(g * 4 + c, 1)]

            def evac_ffn2(g):
                cb = COL["ffn_conv_b_2"]
                for i in range(GROUP):
                    dve.wait_ge(bank_freed, g * 8 + (N_FFN2 + i + 1 + FREE_BANKS))
                    if i == 0:
                        dve.wait_ge(S("hid_made"), g + 12)
                    ins = V.tensor_scalar(y(i), UC[:, i, 0:T], tap(g, 0, i),
                                          vec[:, bass.ds(g * 4 + (cb + (i % 2) * FT + i // 2), 1)], ALU.mult, ALU.add)
                ins.then_inc(S("conv_step"), 1)

            def tail_ffn2(g, j):
                if j in (1, 2):
                    dve.wait_ge(S("conv_step"), g * 3 + j)
                    for i in range(GROUP):
                        ins = V.scalar_tensor_tensor(y(i), UC[:, i, j:j + T], tap(g, j, i), y(i), ALU.mult, ALU.add)
                    ins.then_inc(S("conv_step"), 1)
                elif j == 4:
                    dve.wait_ge(S("conv_gate"), g + 1)
                    V.tensor_tensor(YV[:], YG[:], YV[:], ALU.mult).then_inc(S("hid_full"), 1)
                elif j == 6:
                    dve.wait_ge(S("hid_hi"), g + 12)
                    V.tensor_tensor(HID[:, 1, bass.ds(g * 4, 4), :], YV[:],
                                    HID[:, 0, bass.ds(g * 4, 4), :].bitcast(F32), ALU.subtract)\
                        .then_inc(S("hid_made"), 1)
            ffn_phase(U_FFN2, evac_ffn2, tail_ffn2)
            down(U_DOWN2, M_DOWN2, last=True)
            for q in range(4):
                got("y_turned_v")
                V.tensor_copy(OUTT[:, 1, q * 512:(q + 1) * 512], ps[4 + q][:, :]).then_inc(S("y_tokens_1"), 1)

        @block.tensor
        def _(pe):
            mm = nc.tensor.matmul

            def h_in(part, k):
                return H[:, part, k, :]

            def unit(u, tiles, nf, wcol, first=False, last=False, g=None, step=0, n0=None, hcol=h_in, h_wait=None):
                v = u + 1
                pe.wait_ge(lo_made, v if g is None else g * step + v)
                for kk, k in enumerate(tiles):
                    if h_wait is not None and kk == 0:
                        pe.wait_ge(*h_wait)
                    for f in range(nf):
                        if first and kk == 0:
                            bv = n0 + f + 1 - 8 + FREE_BANKS
                            pe.wait_ge(bank_freed, bv if g is None else g * 8 + bv)
                        c = wcol(kk, f)
                        hi_w, lo_w = HIW[:, u % 2, c:c + P], LOW[:, u % 4, c:c + P]
                        h_hi, h_lo = hcol(0, k), hcol(1, k)
                        start, stop = first and kk == 0, last and kk == len(tiles) - 1
                        o_ = ps[f][:, 0:T]
                        mm(o_, hi_w, h_hi, start=start, stop=False)
                        mm(o_, hi_w, h_lo, start=False, stop=False)
                        i = mm(o_, lo_w, h_hi, start=False, stop=stop)
                        if kk == len(tiles) - 1 and f == nf - 1:
                            i.then_inc(unit_used, 1)
                        elif stop:
                            i.then_inc(tile_summed, 1)

            def plain(kk, f):
                return kk * 1024 + f * P

            def gate_up_col(kk, i):
                return kk * 1024 + (i % 2) * 512 + (i // 2) * P

            def group_phase(u0, n0, groups, wcol=plain, k_norm=None):
                with pe.Fori(0, groups) as g:
                    for j in range(UG):
                        hw = None if k_norm is None else (S("h_made"), 8 * HN[k_norm] + j + 1)
                        unit(u0 + j, [2 * j, 2 * j + 1], GROUP, wcol, j == 0, j == UG - 1, g, UG, n0, h_wait=hw)

            def down(u0, n0, made0):
                for half in range(2):
                    b = u0 + half * (FT // 2)
                    for j in range(2):
                        unit(b + j, [2 * j, 2 * j + 1], GROUP, plain, j == 0, n0=n0 + 8 * half,
                             hcol=lambda part, k: HID[:, part, k, :], h_wait=(S("hid_made"), made0 + 10))
                    with pe.Fori(0, 4) as i:
                        for j in range(4):
                            unit(b + 2 + j, [4 + 2 * j, 5 + 2 * j], GROUP, plain, g=i, step=4,
                                 hcol=lambda part, k: HID[:, part, bass.ds(i * 8 + k, 1), :])
                    for j in range(18, 22):
                        unit(b + j, [2 * j, 2 * j + 1], GROUP, plain, last=j == 21,
                             hcol=lambda part, k: HID[:, part, k, :], h_wait=(S("hid_made"), made0 + 11))

            def norm(k, presummed=True):
                sq = NSQ_H if k == 2 else NSQ
                for f in range(8 if presummed else 0, KT):
                    pe.wait_ge(S("squared"), KT * k + f + 1)
                    i = mm(ps[0][:, 0:T], ones[:], sq[:, f, :], start=f == (8 if presummed else 0),
                           stop=f == KT - 1 and not presummed)
                if presummed:
                    pe.wait_ge(S("squares_presummed"), {1: 1, 2: 2, 4: 3}[k])
                    i = mm(ps[0][:, 0:T], ones[:], sq[:, 0, :], start=False, stop=True)
                i.then_inc(S("squares_summed"), 1)

            pe.sem_inc(unit_used, FREE_UNITS)
            pe.wait_ge(S("ident_made"), 1)
            for n in range(NT):
                pe.wait_ge(S(f"x_landed_{n}"), 16)
                for q in range(4):
                    for i in range(4):
                        f = 4 * q + i
                        ins = nc.tensor.transpose(ps[4 * n + q][:, i * P:(i + 1) * P], XIN[:, n, f * P:(f + 1) * P],
                                                  ident[:])
                    ins.then_inc(S("x_turned"), 1)
            pe.wait_ge(S("vecs_landed"), counts["vecs_landed"])
            pe.wait_ge(S("x_tiles"), 8)
            for i, pack in enumerate(PACKS):
                r = sum(n for _, n in pack)
                if i >= 4:
                    pe.wait_ge(S("vecs_made"), i - 3)
                nc.tensor.transpose(ps[i % 4][:, (i // 4) * P:(i // 4) * P + r], VPACK[0:r, i, :],
                                    ident[0:r, 0:r]).then_inc(S("vecs_turned"), 1)
            pe.wait_ge(S("vecs_made"), len(PACKS))
            norm(0, presummed=False)
            for j in range(4):
                unit(j, [4 * j + i for i in range(4)], 3, lambda kk, f: kk * 384 + f * P, j == 0, j == 3,
                     n0=N_MISC1, h_wait=(S("h_made"), 2 * j + 2))
            group_phase(U_IN, N_IN, 6)

            got = waiter(pe)
            got("loras_landed", 64)
            got("lowrank_ready")
            for name, r, b0 in (("w_lora", slice(0, 64), 0), ("a_lora", slice(64, 128), 4)):
                for t in range(PAIRS):
                    ins = mm(ps[b0 + t // 2][:, (t % 2) * T:(t % 2 + 1) * T], WA_UP[r, t * P:(t + 1) * P],
                             PR[r, T_WA, PAD:TP], start=True, stop=True)
                    if t % 2:
                        ins.then_inc(S(name), 1)

            def head_rsqrt(src, tiles, sel, width):
                got("hr_sq")
                for f in range(tiles):
                    ins = mm(ps[0][0:16, 0:T], sel[:, 15 - f * width - (width - 1):31 - f * width - (width - 1)],
                             src[:, f, :], start=f == 0, stop=f == tiles - 1)
                ins.then_inc(S("hr_sum"), 1)
                got("hr_inv")
                for f in range(tiles):
                    n = P // width
                    for e in range(width):
                        h = f * width + e
                        ins = mm(ps[f // 2][e * n:(e + 1) * n, (f % 2) * T:(f % 2 + 1) * T],
                                 ident[0:16, h:h + 1].broadcast_to([16, n]), rstd[0:16], start=True, stop=True)
                    if f % 2:
                        ins.then_inc(S("hr_bc"), 1)

            def head_sums(src, b0, name):
                for q in range(4):
                    mm(ps[b0 + q][:, :], headones[:], src[:, 2 * q:2 * q + 2, :], start=True, stop=True)\
                        .then_inc(S(name), 1)
            got("w_lora_sigmoid")
            head_rsqrt(KK, PAIRS, sel2, 2)
            got("bonus_terms")
            got("a_lora_sigmoid")
            head_sums(RN, 4, "bonus_summed")
            got("hats_made")

            def inversion(LO, TM, TT, PM):
                for lev in range(1, 6):
                    for b in range(2):
                        got("inv_off")
                        if lev > 1:
                            got("inv_added")
                        for h in range(4 * b, 4 * b + 4):
                            ins = mm(ps[1 + 3 * b][:, (h % 4) * P:(h % 4 + 1) * P], LO[:, h, :], TM[:, h, :],
                                     start=True, stop=True)
                        ins.then_inc(S("inv_p"), 1)
                    for b in range(2):
                        got("inv_pm")
                        if lev < 5:
                            for h in range(4 * b, 4 * b + 4):
                                mm(ps[2 + 3 * b][:, (h % 4) * P:(h % 4 + 1) * P], TT[:, h, :], PM[:, h, :],
                                   start=True, stop=True)
                        for h in range(4 * b, 4 * b + 4):
                            ins = mm(ps[3 + 3 * b][:, (h % 4) * P:(h % 4 + 1) * P], PM[:, h, :], TT[:, h, :],
                                     start=True, stop=True)
                        ins.then_inc(S("inv_t"), 1)
                for b in range(2):
                    got("inv_added")

            for hb in range(2):
                for n in range(NT):
                    tn = slice(n * P, n * P + P)
                    pn = slice(PAD + n * P, PAD + n * P + P)
                    for i in range(4):
                        nc.tensor.transpose(ps[0][:, i * P:(i + 1) * P], PR[:, T_V + 4 * hb + i, pn], ident[:])
                    for i in range(4):
                        ins = nc.tensor.transpose(ps[1][:, i * P:(i + 1) * P], BH[:, 4 * hb + i, tn], ident[:])
                    ins.then_inc(S("tok_turned"), 2)
                    for i in range(4):
                        ins = nc.tensor.transpose(ps[2][:, i * P:(i + 1) * P], PR[:, T_K + 4 * hb + i, pn], ident[:])
                    ins.then_inc(S("ktok_turned"), 1)
                    for which in range(2):
                        for hp in range(2):
                            rr = slice(64 * hp, 64 * hp + 64)
                            for i in range(4):
                                t = 4 * hb + i
                                w = BH[rr, t, tn] if which == 0 else PR[rr, T_K + t, pn]
                                if which and i % 2 == 0:
                                    got("l_out")
                                ins = mm(ps[3 + 2 * hp + i // 2][:, (i % 2) * T:(i % 2 + 1) * T], w,
                                         AR[rr, t, :, tn], start=True, stop=True)
                                if i % 2:
                                    ins.then_inc(S("l_summed"), 1)
                    got("tok_made", 2)
                    for hp in range(2):
                        rr = slice(64 * hp, 64 * hp + 64)
                        for i in range(4):
                            t = 4 * hb + i
                            ins = mm(ps[(7, 0)[hp]][:, i * P:(i + 1) * P], AR[rr, t, 0, tn], BH[rr, t, tn],
                                     start=True, stop=True)
                        ins.then_inc(S("l_plain"), 1)
                    got("l_out", 6)
                    got("ktok_made")
                    got("inv_start")
                    inversion(LO, TM, TT, PM)
                    for c in (2 * n, 2 * n + 1):
                        cp = c % 2
                        r = slice(C * cp, C * cp + C)
                        cc = slice(c * C, c * C + C)
                        if cp:
                            got("s_out")
                        for i in range(4):
                            mm(ps[7][r, i * P:(i + 1) * P], AR[:, 4 * hb + i, 0, cc], ST[:, i, :],
                               start=True, stop=False)
                            for hp in range(2):
                                v = slice(64 * hp, 64 * hp + 64)
                                ins = mm(ps[7][r, i * P + 64 * hp:i * P + 64 * hp + 64], LKR[:, 4 * hp + i, 0, r],
                                         VTOK[:, i, v], start=False, stop=hp == 1)
                        ins.then_inc(S("r1_summed"), 1)
                        got("r1_out")
                        for i in range(4):
                            for hp in range(2):
                                v = slice(64 * hp, 64 * hp + 64)
                                ins = mm(ps[0][r, i * P + 64 * hp:i * P + 64 * hp + 64], TT[:, 4 * hp + i, r],
                                         R1[:, i, v], start=True, stop=True)
                        ins.then_inc(S("u_summed"), 1)
                        got("u_out")
                        if c % 2:
                            got("y_out")
                        for i in range(4):
                            mm(ps[1][:, i * C:(i + 1) * C], ST[:, i, :], AR[:, 4 * hb + i, 1, cc],
                               start=True, stop=False)
                            for hp in range(2):
                                v = slice(64 * hp, 64 * hp + 64)
                                mm(ps[1][v, i * C:(i + 1) * C], UU[:, i, v], LBR[:, 4 * hp + i, 1, r],
                                   start=False, stop=False)
                                ins = mm(ps[1][v, i * C:(i + 1) * C], VTOK[:, i, v], LKR[:, 4 * hp + i, 1, r],
                                         start=False, stop=True)
                        ins.then_inc(S("y_summed"), 1)
                        for i in range(4):
                            mm(ps[2][:, i * P:(i + 1) * P], BTOK[r, i, :], UU[r, i, :], start=True, stop=False)
                            ins = mm(ps[2][:, i * P:(i + 1) * P], KTOK[r, i, :], VTOK[r, i, :],
                                     start=False, stop=True)
                        ins.then_inc(S("s_summed"), 1)
                    got("y_out")
                    got("s_out")
            head_sums(BH, 0, "y_mean")
            head_rsqrt(RN, PAIRS, sel2, 2)
            got("y_normed")
            for t in range(PAIRS):
                o_ = ps[t // 2][:, (t % 2) * T:(t % 2 + 1) * T]
                mm(o_, G_UP[:, 0, t * P:(t + 1) * P], PR[:, T_G0, PAD:TP], start=True, stop=False)
                ins = mm(o_, G_UP[0:32, 1, t * P:(t + 1) * P], PR[0:32, T_G1, PAD:TP], start=False, stop=True)
                if t % 2:
                    ins.then_inc(S("gate_summed"), 1)

            got("ya_full")
            head_rsqrt(GSQ, 8, sel1, 1)
            got("rows_made")
            got("beta_made")
            for n in range(NT):
                ins = nc.tensor.transpose(ps[4][:, n * P:(n + 1) * P], ROWS[:, n * P:(n + 1) * P], ident[:])
            ins.then_inc(S("cols_turned"), 1)
            got("gqk_normed")

            def g_rows(name):
                for h in range(G_HEADS):
                    ins = mm(ps[h // 2][:, (h % 2) * T:(h % 2 + 1) * T],
                             ident[32:40, 32 + h:33 + h].broadcast_to([8, P]), ROWS[32:40, :], start=True, stop=True)
                    if h % 2:
                        ins.then_inc(S(name), 1)
            g_rows("g_rows")
            got("cols_made")
            for n in range(NT):
                tn = slice(n * P, n * P + P)
                for h in range(G_HEADS):
                    ins = mm(ps[4 + h // 4][:, (h % 4) * P:(h % 4 + 1) * P],
                             ident[64:72, 64 + h:65 + h].broadcast_to([8, P]), ROWS[64:72, tn], start=True, stop=True)
                    if h % 4 == 3:
                        ins.then_inc(S("beta_rows"), 1)
                if n == 0:
                    got("gqk_normed", 0)
                for i in range(G_QK):
                    ins = nc.tensor.transpose(ps[6][:, i * P:(i + 1) * P], KC[:, i, tn], ident[:])
                ins.then_inc(S("gtok_turned"), 1)
                for i in range(4):
                    ins = nc.tensor.transpose(ps[7][:, i * P:(i + 1) * P], VC[:, i, tn], ident[:])
                ins.then_inc(S("gvtok_turned"), 1)
                got("beta_rows_out")
                for i in range(G_QK):
                    mm(ps[4][:, i * P:(i + 1) * P], KC[:, i, tn], KC[:, i, tn], start=True, stop=True)
                for i in range(G_QK):
                    ins = mm(ps[5][:, i * P:(i + 1) * P], KC[:, i, tn], QC[:, i, tn], start=True, stop=True)
                ins.then_inc(S("gkk_summed"), 2)
                got("gtt_start")
                for i in range(4):
                    ins = nc.tensor.transpose(ps[4][:, i * P:(i + 1) * P], VC[:, 4 + i, tn], ident[:])
                ins.then_inc(S("gvtok_turned"), 1)
                got("gtok_made")
                for b in range(2):
                    for i in range(4):
                        ins = nc.tensor.transpose(ps[(7, 4)[b]][:, i * P:(i + 1) * P], gTT[:, 4 * b + i, :], ident[:])
                    ins.then_inc(S("gtm_turned"), 1)
                got("inv_start")
                inversion(gLO, gTM, gTT, gPM)
                for b in range(2):
                    for i in range(4):
                        ins = mm(ps[b][:, i * P:(i + 1) * P], gTT[:, 4 * b + i, :], VB[:, 4 * b + i, :],
                                 start=True, stop=True)
                    ins.then_inc(S("u0_summed"), 1)
                for b in range(2):
                    for i in range(4):
                        ins = mm(ps[2 + b][:, i * P:(i + 1) * P], KBE[:, 4 * b + i, :], gTT[:, 4 * b + i, :],
                                 start=True, stop=True)
                    ins.then_inc(S("wt_summed"), 1)
                got("u0_out", 2)
                got("wt_out", 2)
                for c in (2 * n, 2 * n + 1):
                    r = slice(C * (c % 2), C * (c % 2) + C)
                    cc = slice(c * C, c * C + C)
                    if c % 2:
                        got("gs_out")
                    for h in range(G_HEADS):
                        ins = mm(ps[h // 4][r, (h % 4) * P:(h % 4 + 1) * P], WT[:, h, r], gS[:, h, :],
                                 start=True, stop=True)
                        if h % 4 == 3:
                            ins.then_inc(S("ws_summed"), 1)
                    got("vn_made")
                    if c % 2:
                        got("o_out")
                    for h in range(G_HEADS):
                        o_ = ps[4][:, h * C:(h + 1) * C]
                        mm(o_, gS[:, h, :], QG[:, h, cc], start=True, stop=False)
                        ins = mm(o_, VN[:, h, :], AT[:, h, r], start=False, stop=True)
                    ins.then_inc(S("o_summed"), 1)
                    for h in range(G_HEADS):
                        ins = mm(ps[2 + h // 4][:, (h % 4) * P:(h % 4 + 1) * P], KG[r, h, :], VN[r, h, :],
                                 start=True, stop=True)
                    ins.then_inc(S("gs_summed"), 1)
                got("gs_out")
                got("o_out")
                if n == 0:
                    g_rows("g_rows_again")
            head_rsqrt(GSQ, 8, sel1, 1)

            got("mix_made", 2)
            group_phase(U_OUT, N_OUT, 2)
            norm(1)
            group_phase(U_FFN1, N_FFN1, 11, gate_up_col, 1)
            down(U_DOWN1, N_DOWN1, 1)
            norm(2)
            norm(3, presummed=False)
            for j in range(4):
                unit(U_MISC2 + j, [4 * j + i for i in range(4)], 1, lambda kk, f: kk * P, j == 0, j == 3,
                     n0=N_MISC2, h_wait=(S("h_made"), 8 * HN[3] + 2 * j + 2))
            group_phase(U_FOX, N_FOX, 6)

            got("att_in")
            mm(ps[7][0:16, 0:T], ident[:, 112:128], FM[:], start=True, stop=True).then_inc(S("f_rows"), 1)
            head_rsqrt(ASQ, 16, sel1, 1)
            head_rsqrt(ASQ, 16, sel1, 1)
            got("qk_normed")
            for b in range(8):
                for i in range(4):
                    ins = nc.tensor.transpose(ps[b][:, i * P:(i + 1) * P],
                                              QKV[:, 32 + (b % 4) * 4 + i, (b // 4) * P:(b // 4 + 1) * P], ident[:])
                ins.then_inc(S("v_turned_v" if b % 2 else "v_turned_a"), 1)
            got("forget_summed")
            got("vt_made_a", 4)
            for n in range(NT):
                ins = nc.tensor.transpose(ps[0][:, n * 16:(n + 1) * 16], FW[0:16, 2, n * P:(n + 1) * P],
                                          ident[0:16, 0:16])
            ins.then_inc(S("forget_cols"), 1)
            got("vt_made_v", 4)
            got("forget_cols_out")
            for h in range(A_HEADS):
                ins = mm(ps[h // 2][:, (h % 2) * T:(h % 2 + 1) * T], ident[0:16, h:h + 1].broadcast_to([16, P]),
                         FW[0:16, 2, :], start=True, stop=True)
                if h % 2:
                    ins.then_inc(S("forget_rows"), 1)
            got("bias_made", 8)

            def scores(h):
                z = h % 2
                mm(ps[z][:, 0:P], QKV[:, h, 0:P], QKV[:, 16 + h, 0:P], start=True, stop=True)
                mm(ps[z][:, P:3 * P], QKV[:, h, P:T], QKV[:, 16 + h, :], start=True, stop=True)\
                    .then_inc(S("scores_made"), 1)

            def mix(h):
                z = h % 2
                got("prob_normed")
                for i in range(3):
                    ins = nc.tensor.transpose(ps[2 + z][:, i * P:(i + 1) * P], SC[:, z, i * P:(i + 1) * P], ident[:])
                ins.then_inc(S("pt_turned"), 1)
                got("pt_made")
                if h >= 2:
                    got("att_made")
                v0, v1 = (VT[:, n, h * P:(h + 1) * P] for n in range(NT))
                mm(ps[4 + z][:, 0:P], v0, PT[:, z, 0:P], start=True, stop=True)
                mm(ps[4 + z][:, P:T], v0, PT[:, z, P:2 * P], start=True, stop=False)
                mm(ps[4 + z][:, P:T], v1, PT[:, z, 2 * P:3 * P], start=False, stop=True)\
                    .then_inc(S("att_summed"), 1)
            for h in range(A_HEADS):
                scores(h)
                if h:
                    mix(h - 1)
            mix(A_HEADS - 1)

            got("att_made", 2)
            group_phase(U_OUT2, N_OUT2, 2)
            norm(4)
            group_phase(U_FFN2, N_FFN2, 11, gate_up_col, 4)
            down(U_DOWN2, N_DOWN2, 12)
            pe.wait_ge(bank_freed, N_END + FREE_BANKS)
            for n in range(NT):
                for q in range(4):
                    for i in range(4):
                        ins = nc.tensor.transpose(ps[4 * n + q][:, i * P:(i + 1) * P],
                                                  X[:, 4 * q + i, n * P:(n + 1) * P], ident[:])
                    ins.then_inc(S("y_turned_v" if n else "y_turned_a"), 1)


def kernel(**inputs):
    import numpy as np
    import concourse.bacc as bacc
    from concourse.bass_utils import run_bass_kernel_spmd

    nc = bacc.Bacc("TRN2", target_bir_lowering=False, num_devices=1)
    arrays, io = {}, {}
    for name in NAMES:
        a = np.ascontiguousarray(inputs[name])
        arrays[f"in_{name}"] = a
        io[name] = nc.dram_tensor(f"in_{name}", a.shape, mybir.dt.from_np(a.dtype), kind="ExternalInput").ap()
    out = nc.dram_tensor("out_y", (1, T, D), F32, kind="ExternalOutput").ap()
    build(nc, io, out)
    return run_bass_kernel_spmd(nc, [arrays], core_ids=[0]).results[0]["out_y"]
```

```python
from contextlib import ExitStack

import concourse.bass as bass
from concourse import mybir

F32 = mybir.dt.float32
F32R = mybir.dt.float32r
ALU = mybir.AluOpType
ACT = mybir.ActivationFunctionType
AX_X = mybir.AxisListType.X

P = 128
T = 256
D = 2048
KT = D // P
FT = 5632 // P
C = 64
NCH = T // C
NT = T // P
UNIT = 2048
RAW_SLOTS, HI_SLOTS = 4, 2
GROUP = 8
UG = KT // 2

R_DIM, R_HEADS, R_HEAD = 1024, 16, 64
PAIRS = R_HEADS // 2
G_HEADS, G_QK = 8, 4
A_HEADS = 16
N_RWKV = 3360
DECAY_RATE = 0.6065306597126334
TP = 260
PAD = TP - T
T_WA, T_G0, T_G1 = 0, 1, 2
T_R, T_K, T_V, T_GQ, T_GK, T_GV, T_Z = 3, 11, 19, 27, 31, 35, 43
NTILES = 51

WEIGHTS = ["w_in", "w_out", "ffn_w_gate", "ffn_w_up", "ffn_w_down", "fox_w_in_2", "fox_w_out_2",
           "ffn_w_up_2", "ffn_w_down_2"]
NAMES = ["x", "attn_norm_w", "w_in", "rwkv_mu", "rwkv_w0", "rwkv_w_up", "rwkv_a0", "rwkv_a_up", "rwkv_g_up",
         "rwkv_k_k", "rwkv_k_a", "rwkv_r_k", "rwkv_ln_w", "rwkv_ln_b", "gdn_conv_w", "gdn_A_log",
         "gdn_dt_bias", "gdn_norm_w", "w_out", "ffn_norm_w", "ffn_w_gate", "ffn_w_up", "ffn_w_down",
         "final_norm_w", "mix_norm_2", "ffn_norm_2", "fox_w_in_2", "fox_b_f_2", "fox_q_gain_2",
         "fox_k_gain_2", "fox_w_out_2", "ffn_w_up_2", "ffn_conv_w_2", "ffn_conv_b_2", "ffn_w_down_2"]

PACKS = [
    [("attn_norm_w", 16), ("ffn_norm_w", 16), ("final_norm_w", 16), ("mix_norm_2", 16), ("ffn_norm_2", 16),
     ("gdn_norm_w", 1), ("fox_q_gain_2", 1), ("fox_k_gain_2", 1)],
    [("rwkv_mu", 27), ("rwkv_w0", 8), ("rwkv_a0", 8), ("rwkv_k_k", 8), ("rwkv_k_a", 8), ("rwkv_r_k", 8),
     ("rwkv_ln_w", 8), ("rwkv_ln_b", 8)],
    [("gdn_conv_w", 64)],
    [("conv0", 88)], [("conv1", 88)], [("conv2", 88)], [("ffn_conv_b_2", 88)],
]
COL, _c = {}, 0
for _pack in PACKS:
    for _name, _rows in _pack:
        COL[_name] = _c
        _c += _rows
VEC_COLS = _c


def build(nc, io, out):
    with ExitStack() as ctx:
        sems, counts = {}, {}

        def S(name):
            if name not in sems:
                sems[name] = ctx.enter_context(nc.semaphore(name))
            return sems[name]

        def tick(ins, name, by=1):
            ins.then_inc(S(name), by)
            counts[name] = counts.get(name, 0) + by
            return counts[name]

        def waiter(engine):
            seen = {}

            def got(name, by=1):
                seen[name] = seen.get(name, 0) + by
                engine.wait_ge(S(name), seen[name])
            return got

        def own(engine, name):
            engine.wait_ge(S(name), counts[name])

        def at(name, shape, offset, dt=F32):
            return nc.alloc_sbuf_tensor_at(name, shape, dt, offset=offset)

        o = nc.sbuf_base if isinstance(nc.sbuf_base, int) else 0
        o = (o + 63) // 64 * 64
        base0 = o
        X = at("X", [P, KT, T], o); o += 16384
        w0 = o
        RAW = at("RAW", [P, RAW_SLOTS, UNIT], o)
        LOW = at("LOW", [P, RAW_SLOTS, UNIT], o, F32R); o += 32768
        HIW = at("HIW", [P, HI_SLOTS, UNIT], o, F32R); o += 16384
        ident = at("ident", [P, P], o); o += 512
        ones = at("ones", [P, P], o); o += 512
        headones = at("headones", [P, P], o); o += 512
        vec = at("vec", [P, VEC_COLS], o); o += (VEC_COLS * 4 + 63) // 64 * 64
        small = at("small", [P, 256], o); o += 1024
        causal = at("causal", [P, P], o); o += 512
        rstd = at("rstd", [P, T], o); o += 1024
        h0 = o
        H = at("H", [P, 2, KT, T], h0, F32R); o += 32768
        r2 = o
        end = base0 + 212800
        masks = end - 5632
        upper2 = at("upper2", [P, 2, P], masks)
        upper, upper_eq = upper2[:, 0, :], upper2[:, 1, :]
        lower1 = at("lower1", [P, P], masks + 1024)
        off = at("off", [P, 6, P], masks + 1536)
        chunk_go = at("chunk_go", [P, T], masks + 4608)
        assert r2 + 102192 <= masks and r2 + 90112 + 16600 <= end, (r2, masks, end)

        XIN = at("XIN", [P, NT, D], r2)
        VPACK = at("VPACK", [P, len(PACKS), P], r2 + 16384)
        NSQ = at("NSQ", [P, KT, T], r2)
        NSQ_H = at("NSQ_H", [P, KT, T], h0)
        PR = at("PR", [P, NTILES, TP], r2)
        a3 = r2 + 53056
        SHIFT = at("SHIFT", [P, 27, T], h0)
        GS = at("GS", [P, PAIRS, T], h0)
        ENG = at("ENG", [P, PAIRS, T], h0 + 8192)
        KK = at("KK", [P, PAIRS, T], h0 + 16384)
        TMP = at("TMP", [P, PAIRS, T], h0 + 24576)
        AR = at("AR", [P, PAIRS, 2, T], a3)
        RN = at("RN", [P, PAIRS, T], a3)
        RN2 = at("RN2", [P, PAIRS, T], a3 + 8192)
        BH = at("BH", [P, PAIRS, T], a3 + 16384)
        BON = at("BON", [P, PAIRS, T], a3 + 24576)
        WA_UP = at("WA_UP", [P, R_DIM], a3 + 24576)
        EG = at("EG", [P, PAIRS, T], a3 + 32768)
        G_UP = at("G_UP", [P, 2, R_DIM], a3 + 40960)
        VTOK = at("VTOK", [P, PAIRS, P], a3 + 32768)
        BTOK = at("BTOK", [P, PAIRS, P], a3 + 36864)
        R1 = at("R1", [P, PAIRS, P], r2 + T_R * TP * 4 + 16)
        UU = at("UU", [P, PAIRS, P], r2 + T_R * TP * 4 + 16 + 4096)
        LBR = at("LBR", [P, 16, 2, P], h0)
        LKR = at("LKR", [P, 16, 2, P], h0 + 16384)
        TT = at("TT", [P, 16, P], w0)
        TM = at("TM", [P, 16, P], w0 + 8192)
        PM = at("PM", [P, 16, P], w0 + 16384)
        LO = at("LO", [P, 16, P], w0 + 24576)
        KTOK = at("KTOK", [P, PAIRS, P], w0 + 32768)
        ST = at("ST", [P, 2, PAIRS, P], w0 + 36864)

        rdecay, gdecay = small[:, 0:32], small[:, 32:64]
        a_log, dt_bias, fox_bias = small[32:40, 64:65], small[32:40, 65:66], small[0:16, 66:67]
        sel1, sel2 = small[:, 80:111], small[:, 112:142]
        g_exp, k_left, beta_exp = (small[:, c:c + 16].rearrange("p (n h) -> p n h", n=NT) for c in (144, 160, 176))

        g1 = r2 + T_GQ * TP * 4 + 16
        QKVC = at("QKVC", [P, 16, T], a3)
        QC, KC, VC = QKVC[:, 0:4, :], QKVC[:, 4:8, :], QKVC[:, 8:16, :]
        QG = at("QG", [P, 8, T], a3 + 16384)
        KBE = at("KBE", [P, 16, P], a3 + 24576)
        KG = at("KG", [P, 16, P], a3 + 32768)
        U0 = at("U0", [P, 16, P], a3 + 40960)
        OG = at("OG", [P, 8, T], g1)
        WT = at("WT", [P, 16, P], g1 + 8192)
        GAM = at("GAM", [P, 16, P], r2)
        AT = at("AT", [P, 16, P], r2 + 8192)
        VB = at("VB", [P, 16, P], r2 + 16384)
        VN = at("VN", [P, 8, P], w0 + 45056)
        gTT = at("gTT", [P, 16, P], w0)
        gTM = at("gTM", [P, 16, P], w0 + 8192)
        gPM = at("gPM", [P, 16, P], w0 + 16384)
        gLO = at("gLO", [P, 16, P], w0 + 24576)
        gLT = at("gLT", [P, 16, P], w0 + 32768)
        gS = [at("gS0", [P, 8, P], w0 + 40960), at("gS1", [P, 8, P], h0 + 28672)]
        ROWS = at("ROWS", [P, T], h0 + 12288)
        RWK = at("RWK", [P, 2, T], h0 + 13312)
        COLS = at("COLS", [P, NT, P], h0 + 24576)
        GSQ = at("GSQ", [P, 8, T], r2)
        HID = at("HID", [P, 2, FT, T], r2, F32R)
        f0 = r2 + 2 * FT * T * 4
        SG = at("SG", [P, 4, T], f0)
        HS = at("HS", [P, 4, T], f0 + 4096)
        UC = at("UC", [P, 8, T + 2], f0)
        YG = at("YG", [P, 4, T], f0 + 8256)
        YV = at("YV", [P, 4, T], f0 + 12352)
        assert f0 + 16448 <= end
        QKV = at("QKV", [P, 48, T], r2)
        FM = at("FM", [P, T], r2 + 49152)
        VT = at("VT", [P, NT, D], r2 + 50176)
        ASQ = at("ASQ", [P, 16, T], r2 + 50176)
        CB = at("CB", [P, A_HEADS, 3, P], r2 + 66560)
        SC = at("SC", [P, 2, 384], r2 + 91136)
        PT = at("PT", [P, 2, 384], r2 + 94208)
        FW = at("FW", [P, 3, T], r2 + 97280)
        AST = at("AST", [P, 2, 8], r2 + 100352)
        FQ = at("FQ", [P, NT, A_HEADS], r2 + 100416)
        OUTT = at("OUTT", [P, NT, D], r2)

        ps = [ctx.enter_context(nc.psum_tensor(f"ps{i}", [P, 512], F32)) for i in range(8)]

        w_in, w_out = io["w_in"][0], io["w_out"][0]

        fox = io["fox_w_in_2"][0]
        wup2 = io["ffn_w_up_2"][0]
        U_MISC1, U_IN = 0, 4
        U_OUT = U_IN + 6 * UG
        U_FFN1 = U_OUT + 2 * UG
        U_DOWN1 = U_FFN1 + 11 * UG
        U_MISC2 = U_DOWN1 + FT
        U_FOX = U_MISC2 + 4
        U_OUT2 = U_FOX + 6 * UG
        U_FFN2 = U_OUT2 + 2 * UG
        U_DOWN2 = U_FFN2 + 11 * UG
        U_END = U_DOWN2 + FT
        N_MISC1, N_IN = 0, 8
        N_OUT = N_IN + 48
        N_FFN1 = N_OUT + 16
        N_DOWN1 = N_FFN1 + 88
        N_MISC2 = N_DOWN1 + 16
        N_FOX = N_MISC2 + 8
        N_OUT2 = N_FOX + 48
        N_FFN2 = N_OUT2 + 16
        N_DOWN2 = N_FFN2 + 88
        N_END = N_DOWN2 + 16

        M_IN, M_OUT, M_FFN1, M_DOWN1, M_FOX, M_OUT2, M_FFN2, M_DOWN2 = 2, 44, 58, 135, 149, 191, 205, 282

        landed = [S(f"weights_landed_{i}") for i in range(RAW_SLOTS)]
        unit_used = S("unit_used")
        hi_made, lo_made = S("hi_made"), S("lo_made")
        bank_freed = S("bank_freed")
        tile_summed = S("tile_summed")
        FREE_UNITS, FREE_BANKS = RAW_SLOTS, 8

        def rows(w, k, c0, n):
            return w[k * P:(k + 1) * P, c0:c0 + n]

        def unit_cols(u):
            return 1536 if u < U_IN else 512 if U_MISC2 <= u < U_FOX else UNIT

        HN = {0: 0, 1: 1, 3: 2, 4: 3}

        block = ctx.enter_context(nc.Block())

        @block.sync
        def _(sp):
            def slot_free(u):
                if isinstance(u, int) and u < RAW_SLOTS:
                    return
                sp.wait_ge(unit_used, u - RAW_SLOTS + 1 + FREE_UNITS)

            def load2(u, j, dsts, srcs):
                slot_free(u)
                for d, s in zip(dsts, srcs):
                    sp.dma_start(d, s).then_inc(landed[j % RAW_SLOTS], 16)

            def halves(j, cols=1024):
                s = RAW[:, j % RAW_SLOTS, :]
                return [s[:, 0:cols], s[:, cols:2 * cols]]

            def stream(u0, groups, sources):
                with sp.Fori(0, groups) as g:
                    for j in range(UG):
                        load2(g * UG + (u0 + j), u0 + j, halves(u0 + j), sources(g, j))

            def stream_down(u0, w):
                for half in range(2):
                    b = u0 + half * (FT // 2)

                    def srcs(k):
                        return [w[bass.ds(k * P + i * P, P) if not isinstance(k, int) else
                                  slice((k + i) * P, (k + i + 1) * P), half * 1024:half * 1024 + 1024]
                                for i in range(2)]
                    for j in range(2):
                        load2(b + j, b + j, halves(b + j), srcs(2 * j))
                    with sp.Fori(0, 5) as i:
                        for j in range(4):
                            load2(i * 4 + (b + 2 + j), b + 2 + j, halves(b + 2 + j), srcs(i * 8 + (4 + 2 * j)))

            for n in range(NT):
                sp.dma_start(XIN[:, n, :], io["x"][0, n * P:(n + 1) * P, :]).then_inc(S(f"x_landed_{n}"), 16)
            sp.wait_ge(S("vpack_zeroed"), 1)
            n_dma = 0
            for i, pack in enumerate(PACKS):
                r = 0
                for name, rows_ in pack:
                    if name.startswith("conv"):
                        src = io["ffn_conv_w_2"][0, int(name[4])].rearrange("(r q) -> r q", q=P)
                    elif name == "gdn_conv_w":
                        src = io[name][0].rearrange("k (r q) -> (k r) q", q=P)
                    elif name == "rwkv_r_k":
                        src = io[name][0].rearrange("(r e) q -> r (e q)", e=2)
                    elif name == "final_norm_w":
                        src = io[name].rearrange("(r q) -> r q", q=P)
                    elif name == "rwkv_mu":
                        src = io[name][0, 0:26 * P].rearrange("(r q) -> r q", q=P)
                        sp.dma_start(VPACK[r + 26:r + 27, i, 0:32], io[name][0:1, 26 * P:N_RWKV])\
                            .then_inc(S("vecs_landed"), 16)
                        n_dma += 1
                        rows_ = 26
                    else:
                        src = io[name][0].rearrange("(r q) -> r q", q=P)
                    sp.dma_start(VPACK[r:r + rows_, i, :], src).then_inc(S("vecs_landed"), 16)
                    n_dma += 1
                    r += 27 if name == "rwkv_mu" else rows_
            counts["vecs_landed"] = 16 * n_dma
            sp.wait_ge(S("misc_zeroed"), 1)
            for j in range(4):
                v = RAW[:, j, 0:1536].rearrange("p (k n) -> p k n", k=4)
                src = w_in[4 * j * P:4 * (j + 1) * P, :].rearrange("(k p) n -> p k n", p=P)
                slot_free(j)
                sp.dma_start(v[:, :, 0:288], src[:, :, 3072:3360]).then_inc(landed[j], 16)
                for e in range(2):
                    sp.dma_start(v[:, :, 288 + 32 * e:296 + 32 * e],
                                 src[:, :, 6432 + 8 * e:6440 + 8 * e]).then_inc(landed[j], 16)
            for part, c0 in ((0, 0), (1, N_RWKV)):
                stream(U_IN + part * 3 * UG, 3, lambda g, j, c0=c0: [
                    w_in[(2 * j + i) * P:(2 * j + i + 1) * P, bass.ds(g * 1024 + c0, 1024)] for i in range(2)])
            sp.wait_ge(S("weights_place_free"), 1)
            stream(U_OUT, 2, lambda g, j: [
                w_out[(2 * j + i) * P:(2 * j + i + 1) * P, bass.ds(g * 1024, 1024)] for i in range(2)])

            def gate_up(w_gate, w_up, shift):
                def sources(g, j):
                    return [w[2 * j * P:(2 * j + 2) * P, bass.ds(g * 512 + c, 512)]
                            .rearrange("(k p) n -> p k n", p=P) for w, c in ((w_gate, 0), (w_up, shift))]
                return sources

            def stream_gate_up(u0, sources):
                with sp.Fori(0, 11) as g:
                    for j in range(UG):
                        v = RAW[:, (u0 + j) % RAW_SLOTS, :].rearrange("p (k a n) -> p a k n", k=2, a=2)
                        load2(g * UG + (u0 + j), u0 + j, [v[:, 0], v[:, 1]], sources(g, j))

            stream_gate_up(U_FFN1, gate_up(io["ffn_w_gate"][0], io["ffn_w_up"][0], 0))
            stream_down(U_DOWN1, io["ffn_w_down"][0])
            for j in range(4):
                u = U_MISC2 + j
                v = RAW[:, j, 0:512].rearrange("p (k n) -> p k n", k=4)
                src = fox[4 * j * P:4 * (j + 1) * P, 6032:6160].rearrange("(k p) n -> p k n", p=P)
                load2(u, j, [v[:, 0:2], v[:, 2:4]], [src[:, 0:2], src[:, 2:4]])
            stream(U_FOX, 6, lambda g, j: [
                fox[(2 * j + i) * P:(2 * j + i + 1) * P, bass.ds(g * 1024, 1024)] for i in range(2)])
            fox_out = io["fox_w_out_2"][0]
            stream(U_OUT2, 2, lambda g, j: [
                fox_out[(2 * j + i) * P:(2 * j + i + 1) * P, bass.ds(g * 1024, 1024)] for i in range(2)])
            stream_gate_up(U_FFN2, gate_up(wup2, wup2, FT * P))
            stream_down(U_DOWN2, io["ffn_w_down_2"][0])
            for n in range(NT):
                for q in range(4):
                    sp.wait_ge(S(f"y_tokens_{n}"), q + 1)
                    sp.dma_start(out[0, n * P:(n + 1) * P, q * 512:(q + 1) * 512],
                                 OUTT[:, n, q * 512:(q + 1) * 512]).then_inc(S("y_stored"), 16)
            sp.wait_ge(S("y_stored"), 16 * 4 * NT)

        @block.gpsimd
        def _(pool):
            def sel(dst, pattern, base, mult, op=ALU.is_ge, fill=0.0):
                tick(nc.gpsimd.affine_select(out=dst, in_=dst, compare_op=op, fill=fill, base=base,
                                             pattern=pattern, channel_multiplier=mult), "pool_step")
                own(pool, "pool_step")

            nc.gpsimd.memset(VPACK[:], 0.0).then_inc(S("vpack_zeroed"), 1)
            for j in range(4):
                v = RAW[:, j, 0:1536].rearrange("p (k n) -> p k n", k=4)
                ins = nc.gpsimd.memset(v[:, :, 288:384], 0.0)
            ins.then_inc(S("misc_zeroed"), 1)
            tick(nc.gpsimd.memset(ident[:], 0.0), "pool_step")
            tick(nc.gpsimd.memset(ones[:], 1.0), "pool_step")
            own(pool, "pool_step")
            nc.gpsimd.affine_select(out=ident[:], in_=ident[:], compare_op=ALU.not_equal, fill=1.0, base=0,
                                    pattern=[[-1, P]], channel_multiplier=1).then_inc(S("ident_made"), 1)
            for i, m in enumerate((2, 4, 8, 16, 32, 64)):
                tick(nc.gpsimd.memset(off[:, i, :], 1.0), "pool_step")
            tick(nc.gpsimd.memset(upper, 1.0), "pool_step")
            tick(nc.gpsimd.memset(upper_eq, 1.0), "pool_step")
            tick(nc.gpsimd.memset(lower1[:], 1.0), "pool_step")
            tick(nc.gpsimd.memset(chunk_go[:], 1.0), "pool_step")
            own(pool, "pool_step")
            tick(nc.gpsimd.memset(chunk_go[:].rearrange("p (c t) -> p c t", t=C)[:, :, 0:1], 0.0), "pool_step")
            for i, m in enumerate((2, 4, 8, 16, 32, 64)):
                sel(off[:, i, :], [[-m, P // m], [0, m]], 0, 1)
                sel(off[:, i, :], [[m, P // m], [0, m]], m - 1, -1)
            sel(upper, [[1, P]], -1, -1)
            sel(upper_eq, [[1, P]], 0, -1)
            sel(lower1[:], [[-1, P]], -1, 1)
            tick(nc.gpsimd.memset(small[:, 80:144], 0.0), "pool_step")
            tick(nc.gpsimd.memset(causal[:], 0.0), "pool_step")
            own(pool, "pool_step")
            tick(nc.gpsimd.memset(small[:, 95:96], 1.0), "pool_step")
            own(pool, "pool_step")
            tick(nc.gpsimd.memset(small[0:64, 126:127], 1.0), "pool_step")
            own(pool, "pool_step")
            tick(nc.gpsimd.memset(small[64:128, 127:128], 1.0), "pool_step")
            own(pool, "pool_step")
            sel(causal[:], [[-1, P]], 0, 1, fill=-1e30)
            pool.sem_inc(S("masks_made"), 1)
            for k, sq in ((1, NSQ), (2, NSQ_H), (4, NSQ)):
                pool.wait_ge(S("squared"), KT * k + 8)
                for n in (4, 2):
                    tick(nc.gpsimd.tensor_tensor(sq[:, 0:n, :], sq[:, 0:n, :], sq[:, n:2 * n, :], ALU.add), "pool_step")
                    own(pool, "pool_step")
                nc.gpsimd.tensor_tensor(sq[:, 0, :], sq[:, 0, :], sq[:, 1, :], ALU.add)\
                    .then_inc(S("squares_presummed"), 1)

        @block.scalar
        def _(act):
            A = nc.scalar.activation

            def hi(u_const, g=None, step=0):
                lv = 32 * (u_const // 4 + 1)
                uv = u_const - HI_SLOTS + 1 + FREE_UNITS
                if g is not None:
                    lv = g * (8 * step) + lv
                    uv = g * step + uv
                if g is None and u_const < 4:
                    act.wait_ge(landed[u_const], 48)
                else:
                    act.wait_ge(landed[u_const % 4], lv + 16)
                act.wait_ge(unit_used, uv)
                n = unit_cols(u_const)
                A(HIW[:, u_const % 2, 0:n], RAW[:, u_const % 4, 0:n], ACT.Copy).then_inc(hi_made, 1)

            def summed(n0, f, u_end, g=None, nf=8, step=8):
                if f < nf - 1:
                    v = n0 // 8 * 7 + f + 1
                    act.wait_ge(tile_summed, v if g is None else g * 7 + v)
                else:
                    v = u_end + FREE_UNITS
                    act.wait_ge(unit_used, v if g is None else g * step + v)

            def group_phase(u0, groups, evac=None, n0=0):
                def rest(g):
                    for j in range(2, UG):
                        hi(u0 + j, g, UG)
                    hi(u0 + UG, g, UG)
                    if evac:
                        evac(g)
                    hi(u0 + UG + 1, g, UG)
                with act.Fori(0, groups) as g:
                    rest(g)

            def squares(n0, half, dst=None):
                for f in range(8 * half, 8 * half + 8):
                    act.wait_ge(bank_freed, n0 + f + 1 + FREE_BANKS)
                    A((dst or NSQ)[:, f, :], X[:, f, :], ACT.Square).then_inc(S("squared"), 1)

            def root(k):
                act.wait_ge(S("variance"), k + 1)
                A(rstd[:], rstd[:], ACT.Sqrt).then_inc(S("rooted"), 1)

            def high_parts(k):
                for e in range(8):
                    act.wait_ge(S("h_full"), 8 * HN[k] + e + 1)
                    A(H[:, 0, 2 * e:2 * e + 2, :], NSQ[:, 2 * e:2 * e + 2, :], ACT.Copy).then_inc(S("h_hi"), 1)

            def out_phase(u0, n0, k):
                for g in range(2):
                    u = u0 + g * UG
                    for j in range(2, UG + 1):
                        hi(u + j)
                    squares(n0, g)
                    if g == 1:
                        root(k)
                    hi(u + UG + 1)
                high_parts(k)

            got = waiter(act)
            for dst, src in ((WA_UP[0:64, :], io["rwkv_w_up"][0]), (WA_UP[64:128, :], io["rwkv_a_up"][0]),
                             (G_UP[:, 0, :], io["rwkv_g_up"][0, 0:P, :]),
                             (G_UP[0:32, 1, :], io["rwkv_g_up"][0, P:160, :])):
                act.dma_start(dst, src).then_inc(S("loras_landed"), 16)
            for dst, src in ((a_log, io["gdn_A_log"][0]), (dt_bias, io["gdn_dt_bias"][0]),
                             (fox_bias, io["fox_b_f_2"][0])):
                act.dma_start(dst, src.rearrange("(h a) -> h a", a=1)).then_inc(S("smalls_landed"), 16)
            for q in range(4):
                act.wait_ge(S("x_turned"), q + 1)
                A(X[:, 4 * q:4 * q + 4, 0:P], ps[q][:, :].rearrange("p (f t) -> p f t", f=4), ACT.Copy)\
                    .then_inc(S("x_tiles"), 1)
            hi(0)
            hi(1)
            act.wait_ge(S("x_tiles"), 8)
            for q in range(4):
                A(NSQ[:, 4 * q:4 * q + 4, :], X[:, 4 * q:4 * q + 4, :], ACT.Square).then_inc(S("squared"), 4)
            root(0)
            high_parts(0)
            hi(2)
            hi(3)
            hi(4)
            hi(5)
            group_phase(U_IN, 5)
            for j in range(2, UG):
                hi(U_IN + 5 * UG + j)

            def head_root():
                got("hr_var")
                A(rstd[0:16], rstd[0:16], ACT.Sqrt).then_inc(S("hr_root"), 1)

            got("lowrank_shifted")
            A(PR[0:64, T_WA, PAD:TP], PR[0:64, T_WA, PAD:TP], ACT.Tanh)
            A(PR[0:32, T_G1, PAD:TP], PR[0:32, T_G1, PAD:TP], ACT.Sigmoid)
            A(PR[:, T_G0, PAD:TP], PR[:, T_G0, PAD:TP], ACT.Sigmoid).then_inc(S("lowrank_ready"), 1)
            for name, dst, bias in (("w_lora", EG, "rwkv_w0"), ("a_lora", BH, "rwkv_a0")):
                for t in range(PAIRS):
                    if t % 2 == 0:
                        got(name)
                    b = (0 if dst is EG else 4) + t // 2
                    c = COL[bias] + t
                    ins = A(dst[:, t, :], ps[b][:, (t % 2) * T:(t % 2 + 1) * T], ACT.Sigmoid, bias=vec[:, c:c + 1])
                ins.then_inc(S(f"{name}_sigmoid"), 1)
            got("kq_made")
            A(KK[:], TMP[:], ACT.Square).then_inc(S("hr_sq"), 1)
            head_root()
            got("decay_summed")
            A(EG[:], GS[:], ACT.Exp, scale=-DECAY_RATE).then_inc(S("decay_exp"), 1)
            A(ENG[:], GS[:], ACT.Exp, scale=DECAY_RATE).then_inc(S("decay_exp"), 1)

            def heads4(b):
                return ps[b][:, :].rearrange("p (h t) -> p h t", h=4)

            def inversion(PM):
                for lev in range(1, 6):
                    for b in range(4):
                        got("inv_p")
                        A(PM[:, 4 * b:4 * b + 4, :], heads4(2 * b), ACT.Copy).then_inc(S("inv_pm"), 1)

            for n in range(NT):
                for i, dst in enumerate((VTOK, BTOK, KTOK)):
                    for hb in range(2):
                        got("tok_turned")
                        A(dst[:, 4 * hb:4 * hb + 4, :], heads4(2 * i + hb), ACT.Copy).then_inc(S("tok_made"), 1)
                inversion(PM)
                for c in (2 * n, 2 * n + 1):
                    r = slice(C * (c % 2), C * (c % 2) + C)
                    for hb in range(2):
                        got("r1_summed")
                        A(R1[r, 4 * hb:4 * hb + 4, :], ps[4 * hb][r, :].rearrange("p (h t) -> p h t", h=4), ACT.Copy)\
                            .then_inc(S("r1_out"), 1)
                    for hb in range(2):
                        got("y_summed")
                        A(BH[:, 4 * hb:4 * hb + 4, c * C:c * C + C],
                          ps[2 + 4 * hb][:, 0:256].rearrange("p (h t) -> p h t", h=4), ACT.Copy)\
                            .then_inc(S("y_out"), 1)
            got("y_centred")
            A(RN[:], BH[:], ACT.Square).then_inc(S("hr_sq"), 1)
            head_root()
            got("ya_full")
            A(H[:, 0, 0:PAIRS, :], BH[:], ACT.Copy).then_inc(S("mix_hi"), 1)

            for f in range(16):
                c = COL["gdn_conv_w"] + f
                A(QKVC[:, f, :], PR[:, T_GQ + f, 1:1 + T], ACT.Copy, scale=vec[:, c:c + 1]).then_inc(S("tap0"), 1)
            got("rows_zeroed")
            A(ROWS[64:72, :], PR[64:72, T_G1, PAD:TP], ACT.Sigmoid).then_inc(S("beta_made"), 1)
            for f in range(0, 16, 4):
                got("conv_made")
                A(QKVC[:, f:f + 4, :], QKVC[:, f:f + 4, :], ACT.Silu).then_inc(S("conv_act"), 1)
            A(PR[:, T_Z:T_Z + 8, PAD:TP], PR[:, T_Z:T_Z + 8, PAD:TP], ACT.Silu).then_inc(S("z_act"), 1)
            got("smalls_landed", 48)
            A(a_log, a_log, ACT.Exp).then_inc(S("a_exp"), 1)
            got("softplus_abs")
            A(RWK[32:40, 1, :], RWK[32:40, 1, :], ACT.Exp, scale=-1.0).then_inc(S("softplus_exp"), 1)
            got("conv_act", 2)
            A(GSQ[:], QKVC[:, 0:8, :], ACT.Square).then_inc(S("hr_sq"), 1)
            got("softplus_plus1")
            A(RWK[32:40, 1, :], RWK[32:40, 1, :], ACT.Ln).then_inc(S("softplus_ln"), 1)
            head_root()
            got("cols_made")
            A(g_exp, COLS[:, :, 32:40], ACT.Exp)
            A(k_left, COLS[:, :, 96:104], ACT.Exp).then_inc(S("cols_exp"), 1)
            for b in range(4):
                got("g_rows")
                A(QG[:, 2 * b:2 * b + 2, :], ps[b][:, :].rearrange("p (h t) -> p h t", h=2), ACT.Exp)\
                    .then_inc(S("g_rows_exp"), 1)
            got("beta_exp_made")
            for n in range(NT):
                n8 = slice(8 * n, 8 * n + 8)
                got("gam_diff")
                A(GAM[:, n8, :], GAM[:, n8, :], ACT.Exp).then_inc(S("gam_exp"), 1)
            for n in range(NT):
                got("gtok_turned")
                for h in range(G_HEADS):
                    kt = ps[n][:, (h // 2) * P:(h // 2 + 1) * P]
                    A(KBE[:, 8 * n + h, :], kt, ACT.Copy, scale=beta_exp[:, n, h:h + 1])
                    A(KG[:, 8 * n + h, :], kt, ACT.Copy, scale=k_left[:, n, h:h + 1])
                got("gvtok_turned")
                for h in range(G_HEADS):
                    vt = ps[2 + 2 * n + h // 4][:, (h % 4) * P:(h % 4 + 1) * P]
                    ins = A(VB[:, 8 * n + h, :], vt, ACT.Copy, scale=COLS[:, n, 64 + h:65 + h])
                ins.then_inc(S("gtok_made"), 1)
            inversion(gPM)
            for b in range(4):
                got("u0_summed")
                A(U0[:, 4 * b:4 * b + 4, :], heads4(b), ACT.Copy).then_inc(S("u0_out"), 1)
            for c in range(NCH):
                for hb in range(2):
                    got("o_summed")
                    A(OG[:, 4 * hb:4 * hb + 4, c * C:(c + 1) * C],
                      ps[4 + hb][:, 0:256].rearrange("p (h t) -> p h t", h=4), ACT.Copy).then_inc(S("o_out"), 1)
            got("o_out", 2 * NCH)
            A(GSQ[:], OG[:], ACT.Square).then_inc(S("hr_sq"), 1)
            head_root()
            got("yb_full")
            A(H[:, 0, PAIRS:KT, :], OG[:], ACT.Copy).then_inc(S("mix_hi"), 1)

            def ffn_phase(u0, evac, tail):
                for j in range(2, UG):
                    hi(u0 + j)
                with act.Fori(0, 10) as g:
                    hi(u0 + UG, g, UG)
                    evac(g)
                    for j in range(1, UG):
                        hi(u0 + UG + j, g, UG)
                        tail(g, j)
                hi(u0 + 11 * UG)
                evac(10)
                hi(u0 + 11 * UG + 1)
                for j in range(1, UG):
                    tail(10, j)

            def down(u0, n0=None, last=False):
                for half in range(2):
                    b = u0 + half * (FT // 2)
                    with act.Fori(0, 5) as i:
                        for j in range(4):
                            hi(b + 2 + j, i, 4)
                    if last and half:
                        return
                    hi(b + 22)
                    if not last:
                        squares(n0, half, NSQ_H)
                    if half and not last:
                        root(2)
                    hi(b + 23)

            def evac_ffn1(g):
                for i in range(4):
                    act.wait_ge(tile_summed, g * 7 + (M_FFN1 + 2 * i + 1))
                    A(SG[:, i, :], ps[2 * i][:, 0:T], ACT.Silu).then_inc(S("gate_act"), 1)

            def tail_ffn1(g, j):
                if j == 1:
                    act.wait_ge(bank_freed, g * 8 + (N_FFN1 + 8 + FREE_BANKS))
                    A(HID[:, 0, bass.ds(g * 4, 4), :], HS[:], ACT.Copy).then_inc(S("hid_hi"), 1)

            hi(U_OUT)
            hi(U_OUT + 1)
            out_phase(U_OUT, N_OUT, 1)
            ffn_phase(U_FFN1, evac_ffn1, tail_ffn1)
            down(U_DOWN1, N_DOWN1)
            for f in range(KT):
                act.wait_ge(S("x_scaled"), f + 1)
                A(NSQ[:, f, :], X[:, f, :], ACT.Square).then_inc(S("squared"), 1)
            root(3)
            high_parts(3)
            hi(U_MISC2 + 2)
            hi(U_MISC2 + 3)
            hi(U_FOX)
            hi(U_FOX + 1)
            group_phase(U_FOX, 6)

            for part in range(2):
                got("att_in")
                A(ASQ[:], QKV[:, 16 * part:16 * part + 16, :], ACT.Square).then_inc(S("hr_sq"), 1)
                head_root()
            got("softplus_abs")
            A(FW[0:16, 1, :], FW[0:16, 1, :], ACT.Exp, scale=-1.0).then_inc(S("softplus_exp"), 1)
            got("softplus_plus1")
            A(FW[0:16, 1, :], FW[0:16, 1, :], ACT.Ln).then_inc(S("softplus_ln"), 1)
            for b in range(0, 8, 2):
                got("v_turned_a")
                A(VT[:, b // 4, (b % 4) * 512:(b % 4 + 1) * 512], ps[b][:, :], ACT.Copy).then_inc(S("vt_made_a"), 1)
            for h in range(A_HEADS):
                z = h % 2
                for n, c0, w in ((0, 0, P), (1, P, T)):
                    got("score_max")
                    A(SC[:, z, c0:c0 + w], SC[:, z, c0:c0 + w], ACT.Exp, bias=AST[:, z, n:n + 1],
                      accum_out=AST[:, z, 2 + n:3 + n]).then_inc(S("prob_made"), 1)
                got("pt_turned")
                A(PT[:, z, :], ps[2 + z][:, 0:384], ACT.Copy).then_inc(S("pt_made"), 1)
                got("att_summed")
                A(H[:, 0, h, :], ps[4 + z][:, 0:T], ACT.Copy).then_inc(S("att_hi"), 1)
            out_phase(U_OUT2, N_OUT2, 4)

            def evac_ffn2(g):
                for i in range(GROUP):
                    if i < GROUP - 1:
                        act.wait_ge(tile_summed, g * 7 + (M_FFN2 + i + 1))
                    else:
                        act.wait_ge(unit_used, g * UG + (U_FFN2 + UG + FREE_UNITS))
                    if i == 0:
                        act.wait_ge(S("hid_made"), g + 12)
                    A(UC[:, i, 2:2 + T], ps[i][:, 0:T], ACT.Copy).then_inc(bank_freed, 1)

            def tail_ffn2(g, j):
                if j == 3:
                    act.wait_ge(S("conv_step"), g * 3 + 3)
                    A(YG[:], YG[:], ACT.Silu).then_inc(S("conv_gate"), 1)
                elif j == 5:
                    act.wait_ge(S("hid_full"), g + 1)
                    A(HID[:, 0, bass.ds(g * 4, 4), :], YV[:], ACT.Copy).then_inc(S("hid_hi"), 1)
            ffn_phase(U_FFN2, evac_ffn2, tail_ffn2)
            down(U_DOWN2, last=True)
            for q in range(4):
                got("y_turned_a")
                A(OUTT[:, 0, q * 512:(q + 1) * 512], ps[q][:, :], ACT.Copy).then_inc(S("y_tokens_0"), 1)

        @block.vector
        def _(dve):
            V = nc.vector

            def step(ins):
                tick(ins, "dve_step")

            def settle():
                own(dve, "dve_step")

            def lo(u_const, g=None, stepu=0):
                v = u_const + 1
                dve.wait_ge(hi_made, v if g is None else g * stepu + v)
                n = unit_cols(u_const)
                V.tensor_tensor(LOW[:, u_const % 4, 0:n], RAW[:, u_const % 4, 0:n],
                                HIW[:, u_const % 2, 0:n].bitcast(F32), ALU.subtract).then_inc(lo_made, 1)

            def summed(n7, f, u_end, g=None, nf=8, stepu=UG):
                if f < nf - 1:
                    v = n7 + f + 1
                    dve.wait_ge(tile_summed, v if g is None else g * 7 + v)
                else:
                    v = u_end + FREE_UNITS
                    dve.wait_ge(unit_used, v if g is None else g * stepu + v)

            def group_phase(u0, groups, evac):
                with dve.Fori(0, groups) as g:
                    for j in range(2, UG):
                        lo(u0 + j, g, UG)
                    lo(u0 + UG, g, UG)
                    evac(g)
                    lo(u0 + UG + 1, g, UG)

            def inverse_root(k, eps):
                dve.wait_ge(S("squares_summed"), k + 1)
                V.tensor_scalar(rstd[:], ps[0][:, 0:T], 1.0 / D, eps, ALU.mult, ALU.add)\
                    .then_inc(S("variance"), 1)
                dve.wait_ge(S("rooted"), k + 1)
                step(V.reciprocal(rstd[:], rstd[:]))
                settle()

            def norm(k, gain, eps, between=None):
                inverse_root(k, eps)
                c = COL[gain]
                for e in range(9):
                    if e < 8:
                        for f in (2 * e, 2 * e + 1):
                            ins = V.scalar_tensor_tensor(NSQ[:, f, :], X[:, f, :], vec[:, c + f:c + f + 1], rstd[:],
                                                         ALU.mult, ALU.mult)
                        ins.then_inc(S("h_full"), 1)
                    if e == 2 and between:
                        between()
                    if e > 0:
                        dve.wait_ge(S("h_hi"), 8 * HN[k] + e)
                        s = slice(2 * e - 2, 2 * e)
                        V.tensor_tensor(H[:, 1, s, :], NSQ[:, s, :], H[:, 0, s, :].bitcast(F32), ALU.subtract)\
                            .then_inc(S("h_made"), 1)

            for q in range(4):
                dve.wait_ge(S("x_turned"), 5 + q)
                V.tensor_copy(X[:, 4 * q:4 * q + 4, P:T], ps[4 + q][:, :].rearrange("p (f t) -> p f t", f=4))\
                    .then_inc(S("x_tiles"), 1)
            c0 = 0
            for i, pack in enumerate(PACKS):
                r = sum(n for _, n in pack)
                dve.wait_ge(S("vecs_turned"), i + 1)
                V.tensor_copy(vec[:, c0:c0 + r], ps[i % 4][:, (i // 4) * P:(i // 4) * P + r])\
                    .then_inc(S("vecs_made"), 1)
                c0 += r
            dve.wait_ge(S("vecs_made"), len(PACKS))
            dve.wait_ge(S("masks_made"), 1)
            step(V.tensor_tensor(upper, upper, off[:, 5, :], ALU.mult))
            step(V.tensor_tensor(upper_eq, upper_eq, off[:, 5, :], ALU.mult))
            step(V.tensor_tensor(lower1[:], lower1[:], off[:, 0, :], ALU.mult))
            step(V.tensor_copy(headones[:], off[:, 5, :]))
            settle()
            for i in range(5, -1, -1):
                inner = off[:, i - 1, :] if i else ident[:]
                step(V.tensor_tensor(off[:, i, :], off[:, i, :], inner, ALU.subtract))
                settle()
                step(V.tensor_tensor(off[:, i, :], off[:, i, :], upper, ALU.mult))
            settle()
            dve.sem_inc(bank_freed, FREE_BANKS)
            lo(0)
            lo(1)
            norm(0, "attn_norm_w", 1e-5)
            dve.wait_ge(S("h_made"), 8)
            step(V.memset(PR[:, :, 0:PAD], 0.0))
            lo(2)
            lo(3)
            lo(4)
            for f in range(3):
                summed(0, f, U_IN, nf=3)
                V.tensor_copy(PR[:, f, PAD:TP], ps[f][:, 0:T]).then_inc(bank_freed, 6 if f == 2 else 1)
            lo(5)

            def evac_in(g):
                for f in range(GROUP):
                    summed(2, f, U_IN + UG, g)
                    V.tensor_copy(PR[:, bass.ds(g * 8 + (3 + f), 1), PAD:TP], ps[f][:, 0:T])\
                        .then_inc(bank_freed, 1)
            group_phase(U_IN, 5, evac_in)
            for j in range(2, UG):
                lo(U_IN + 5 * UG + j)
            evac_in(5)

            got = waiter(dve)

            def head_rsqrt(scale, eps, after=None):
                got("hr_sum")
                V.tensor_scalar(rstd[0:16], ps[0][0:16, 0:T], scale, eps, ALU.mult, ALU.add).then_inc(S("hr_var"), 1)
                got("hr_root")
                if after is None:
                    V.reciprocal(rstd[0:16], rstd[0:16]).then_inc(S("hr_inv"), 1)
                else:
                    step(V.reciprocal(rstd[0:16], rstd[0:16]))
                    settle()
                    after().then_inc(S("hr_inv"), 1)

            def pair_of(b):
                return ps[b][:, :].rearrange("p (a t) -> p a t", a=2)

            dve.wait_ge(bank_freed, FREE_BANKS + N_OUT)
            step(V.tensor_tensor(SHIFT[:], PR[:, 0:27, PAD - 1:TP - 1], PR[:, 0:27, PAD:TP], ALU.subtract))
            settle()
            mu = {T_WA: 24, T_G0: 25, T_G1: 26}
            for f in [0, 1, 2] + list(range(T_K, T_V)) + list(range(T_V, T_GQ)) + list(range(T_R, T_K)):
                c = COL["rwkv_mu"] + mu.get(f, f - 3)
                ins = V.scalar_tensor_tensor(PR[:, f, PAD:TP], SHIFT[:, f, :], vec[:, c:c + 1], PR[:, f, PAD:TP],
                                             ALU.mult, ALU.add)
                if f == T_G1:
                    ins.then_inc(S("lowrank_shifted"), 1)
                elif f == T_K - 1:
                    step(ins)
            settle()
            Rf, Kf, Vf = (PR[:, t:t + PAIRS, PAD:TP] for t in (T_R, T_K, T_V))
            for t in range(PAIRS):
                c = COL["rwkv_k_k"] + t
                ins = V.tensor_scalar(TMP[:, t, :], Kf[:, t, :], vec[:, c:c + 1], None, ALU.mult)
            ins.then_inc(S("kq_made"), 1)
            got("w_lora_sigmoid")
            for t in range(PAIRS):
                ins = V.tensor_tensor_scan(GS[:, t, :], chunk_go[:], EG[:, t, :], 0.0, ALU.mult, ALU.add)
            ins.then_inc(S("decay_summed"), 1)
            head_rsqrt(1.0, 1e-12)
            for q in range(4):
                got("hr_bc")
                step(V.tensor_tensor(KK[:, 2 * q:2 * q + 2, :], TMP[:, 2 * q:2 * q + 2, :], pair_of(q), ALU.mult))
            settle()
            got("a_lora_sigmoid")
            for t in range(PAIRS):
                c = COL["rwkv_k_a"] + t
                ins = V.tensor_scalar(TMP[:, t, :], BH[:, t, :], 1.0, vec[:, c:c + 1], ALU.subtract, ALU.mult)
            step(ins)
            settle()
            step(V.scalar_tensor_tensor(Kf, TMP[:], 1.0, Kf, ALU.add, ALU.mult))
            step(V.tensor_tensor(BH[:], KK[:], BH[:], ALU.mult))
            settle()
            for t in range(PAIRS):
                c = COL["rwkv_r_k"] + t
                ins = V.scalar_tensor_tensor(RN[:, t, :], Rf[:, t, :], vec[:, c:c + 1], Kf[:, t, :],
                                             ALU.mult, ALU.mult)
            ins.then_inc(S("bonus_terms"), 1)
            got("bonus_terms")
            got("decay_exp")
            step(V.tensor_copy(small[:, 0:32], EG[:].rearrange("p t (c j) -> p (t c) j", j=C)[:, :, C - 1]))
            got("decay_exp")
            step(V.tensor_tensor(BH[:], BH[:], ENG[:], ALU.mult))
            step(V.tensor_tensor(Kf, Kf, ENG[:], ALU.mult))
            for q in range(4):
                got("bonus_summed")
                step(V.tensor_tensor(BON[:, 2 * q:2 * q + 2, :], ps[4 + q][:, :].rearrange("p (a t) -> p a t", a=2),
                                     Vf[:, 2 * q:2 * q + 2, :], ALU.mult))
            step(V.tensor_tensor(AR[:, :, 1, :], Rf, EG[:], ALU.mult))
            for t in range(PAIRS):
                a_t = AR[:, t, 0, :].rearrange("p (c j) -> p c j", j=C)
                kk_t = KK[:, t, :].rearrange("p (c j) -> p c j", j=C)
                eg_t = EG[:, t, :].rearrange("p (c j) -> p c j", j=C)
                V.scalar_tensor_tensor(a_t[:, :, 1:C], kk_t[:, :, 1:C], -1.0, eg_t[:, :, 0:C - 1], ALU.mult, ALU.mult)
                ins = V.tensor_scalar(a_t[:, :, 0:1], kk_t[:, :, 0:1], -1.0, None, ALU.mult)
            step(ins)
            settle()
            step(V.memset(R1[:], 0.0))
            step(V.memset(UU[:], 0.0))
            settle()
            dve.sem_inc(S("hats_made"), 1)

            def bank(b):
                return ps[b][:, :].rearrange("p (h t) -> p h t", h=4)

            def many(m, n):
                return m.unsqueeze(1).broadcast_to([P, n, m.shape[-1]])

            def inv_off(lev, b, lt, LO):
                V.tensor_tensor(LO[:, 4 * b:4 * b + 4, :], lt(b), many(off[:, lev, :], 4), ALU.mult)\
                    .then_inc(S("inv_off"), 1)

            def inversion(lt, LO, TM, TT):
                for lev in range(1, 6):
                    for b in range(4):
                        s4 = slice(4 * b, 4 * b + 4)
                        got("inv_t")
                        if lev < 5:
                            V.tensor_tensor(TM[:, s4, :], TM[:, s4, :], bank(2 * b), ALU.add)
                        V.tensor_tensor(TT[:, s4, :], TT[:, s4, :], bank(2 * b + 1), ALU.add)\
                            .then_inc(S("inv_added"), 1)
                        if lev < 5:
                            inv_off(lev + 1, b, lt, LO)

            step(V.memset(ST[:, 0], 0.0))
            for n in range(NT):
                b_out = 6
                for M in (LBR, LKR):
                    for q in range(8):
                        got("l_summed")
                        dst = M[:, 2 * q:2 * q + 2, :, :].rearrange("p h a t -> p h (a t)")
                        src = ps[b_out % 8][:, :].rearrange("p (h t) -> p h t", h=2)
                        tick(V.tensor_tensor(dst, src, many(upper2[:].rearrange("p a t -> p (a t)"), 2),
                                             ALU.mult), "l_out")
                        b_out += 1
                for b in range(4):
                    s4 = slice(4 * b, 4 * b + 4)
                    got("l_plain")
                    tick(V.tensor_tensor(TM[:, s4, :], bank(b_out % 8), many(lower1[:], 4), ALU.mult), "l_out")
                    step(V.tensor_tensor(TT[:, s4, :], LBR[:, s4, 0, :], many(off[:, 0, :], 4), ALU.mult))
                    own(dve, "l_out")
                    V.tensor_tensor(TM[:, s4, :], TM[:, s4, :], many(ident[:], 4), ALU.add)
                    settle()
                    step(V.tensor_tensor(TT[:, s4, :], TT[:, s4, :], many(ident[:], 4), ALU.add))
                    inv_off(1, b, lambda b: LBR[:, 4 * b:4 * b + 4, 0, :], LO)
                    b_out += 1
                inversion(lambda b: LBR[:, 4 * b:4 * b + 4, 0, :], LO, TM, TT)
                for c in (2 * n, 2 * n + 1):
                    r = slice(C * (c % 2), C * (c % 2) + C)
                    for hb in range(2):
                        h4 = slice(4 * hb, 4 * hb + 4)
                        got("u_summed")
                        V.tensor_copy(UU[r, h4, :], ps[1 + 4 * hb][r, :].rearrange("p (h t) -> p h t", h=4))\
                            .then_inc(S("u_out"), 1)
                    for hb in range(2):
                        h4 = slice(4 * hb, 4 * hb + 4)
                        before, after = ST[:, c % 2, h4, :], ST[:, (c + 1) % 2, h4, :]
                        got("s_summed")
                        step(V.tensor_tensor(PM[:, h4, :], bank(3 + 4 * hb), many(headones[:], 4), ALU.mult))
                        settle()
                        step(V.tensor_tensor(after, before, PM[:, h4, :], ALU.add))
                        settle()
                        dc = rdecay.rearrange("p (t c) -> p t c", c=NCH)[:, h4, c:c + 1]
                        tick(V.tensor_tensor(after, after, dc.broadcast_to([P, 4, P]), ALU.mult), "s_out")
                    own(dve, "s_out")
            for q in range(4):
                got("y_mean")
                if q == 0:
                    dve.wait_ge(S("y_out"), 8)
                b2 = BH[:, 2 * q:2 * q + 2, :]
                ins = V.scalar_tensor_tensor(b2, ps[q][:, :].rearrange("p (a t) -> p a t", a=2), -1.0 / R_HEAD, b2,
                                             ALU.mult, ALU.add)
            ins.then_inc(S("y_centred"), 1)
            head_rsqrt(1.0 / R_HEAD, R_HEAD * 1e-5)
            for q in range(4):
                got("hr_bc")
                step(V.tensor_tensor(BH[:, 2 * q:2 * q + 2, :], BH[:, 2 * q:2 * q + 2, :], pair_of(q), ALU.mult))
            settle()
            dve.sem_inc(S("y_normed"), 1)
            for t in range(PAIRS):
                cw, cb = COL["rwkv_ln_w"] + t, COL["rwkv_ln_b"] + t
                ins = V.tensor_scalar(BH[:, t, :], BH[:, t, :], vec[:, cw:cw + 1], vec[:, cb:cb + 1],
                                      ALU.mult, ALU.add)
            step(ins)
            settle()
            step(V.tensor_tensor(BH[:], BH[:], BON[:], ALU.add))
            settle()
            for q in range(4):
                got("gate_summed")
                b2 = BH[:, 2 * q:2 * q + 2, :]
                ins = V.tensor_tensor(b2, b2, ps[q][:, :].rearrange("p (a t) -> p a t", a=2), ALU.mult)
            ins.then_inc(S("ya_full"), 1)
            got("mix_hi")
            V.tensor_tensor(H[:, 1, 0:PAIRS, :], BH[:], H[:, 0, 0:PAIRS, :].bitcast(F32), ALU.subtract)\
                .then_inc(S("mix_made"), 1)

            settle()
            step(V.memset(ROWS[:], 0.0))
            settle()
            dve.sem_inc(S("rows_zeroed"), 1)
            for tap in range(1, 4):
                for f in range(16):
                    if tap == 1:
                        got("tap0")
                    c = COL["gdn_conv_w"] + 16 * tap + f
                    ins = V.scalar_tensor_tensor(QKVC[:, f, :], PR[:, T_GQ + f, 1 + tap:1 + tap + T],
                                                 vec[:, c:c + 1], QKVC[:, f, :], ALU.mult, ALU.add)
                    if tap == 3 and f % 4 == 3:
                        ins.then_inc(S("conv_made"), 1)
                if tap < 3:
                    step(ins)
                    settle()
            dve.wait_ge(S("smalls_landed"), 48)
            g32 = slice(32, 40)
            step(V.tensor_scalar(RWK[g32, 0, :], PR[g32, T_G1, PAD:TP], dt_bias, None, ALU.add))
            settle()
            step(V.tensor_scalar(RWK[g32, 1, :], RWK[g32, 0, :], -1.0, None, ALU.mult))
            settle()
            step(V.tensor_tensor(RWK[g32, 1, :], RWK[g32, 1, :], RWK[g32, 0, :], ALU.max))
            settle()
            dve.sem_inc(S("softplus_abs"), 1)
            step(V.tensor_scalar(RWK[g32, 0, :], RWK[g32, 0, :], 0.0, None, ALU.max))
            got("softplus_exp")
            V.tensor_scalar(RWK[g32, 1, :], RWK[g32, 1, :], 1.0, None, ALU.add).then_inc(S("softplus_plus1"), 1)
            got("softplus_ln")
            step(V.tensor_tensor(RWK[g32, 0, :], RWK[g32, 0, :], RWK[g32, 1, :], ALU.add))
            settle()
            got("a_exp")
            step(V.tensor_scalar(RWK[g32, 0, :], RWK[g32, 0, :], a_log, -1.0, ALU.mult, ALU.mult))
            settle()
            step(V.tensor_tensor_scan(ROWS[g32, :], chunk_go[g32, :], RWK[g32, 0, :], 0.0, ALU.mult, ALU.add))
            settle()
            gc = ROWS[g32, :].rearrange("p (c j) -> p c j", j=C)
            V.tensor_tensor(ROWS[96:104, :].rearrange("p (c j) -> p c j", j=C),
                            gc[:, :, C - 1:C].broadcast_to([8, NCH, C]), gc, ALU.subtract).then_inc(S("rows_made"), 1)
            head_rsqrt(1.0, 1e-6)
            for q in range(4):
                got("hr_bc")
                s2 = QKVC[:, 2 * q:2 * q + 2, :]
                if q < 2:
                    ins = V.scalar_tensor_tensor(s2, s2, float(P) ** -0.5, pair_of(q), ALU.mult, ALU.mult)
                else:
                    ins = V.tensor_tensor(s2, s2, pair_of(q), ALU.mult)
            ins.then_inc(S("gqk_normed"), 1)
            got("cols_turned")
            V.tensor_copy(COLS[:], ps[4][:, 0:T].rearrange("p (n t) -> p n t", n=NT)).then_inc(S("cols_made"), 1)
            got("cols_exp")
            V.tensor_tensor(beta_exp, g_exp, COLS[:, :, 64:72], ALU.mult).then_inc(S("beta_exp_made"), 1)
            got("g_rows_exp", 4)
            got("gqk_normed")
            step(V.tensor_copy(gdecay, QG[:].rearrange("p h (c j) -> p (h c) j", j=C)[:, :, C - 1]))
            settle()
            step(V.tensor_tensor(QG[:].rearrange("p (a b) t -> p a b t", b=2),
                                 QC.unsqueeze(2).broadcast_to([P, 4, 2, T]),
                                 QG[:].rearrange("p (a b) t -> p a b t", b=2), ALU.mult))
            step(V.memset(gS[0][:], 0.0))
            step(V.memset(VN[:], 0.0))
            settle()
            for n in range(NT):
                for h in range(G_HEADS):
                    ins = V.tensor_scalar(GAM[:, 8 * n + h, :],
                                          ps[h // 2][:, (h % 2) * T + n * P:(h % 2) * T + n * P + P],
                                          COLS[:, n, 32 + h:33 + h], 0.0, ALU.subtract, ALU.min)
                ins.then_inc(S("gam_diff"), 1)
            for b in range(4):
                got("beta_rows")
                V.scalar_tensor_tensor(gPM[:, 4 * b:4 * b + 4, :], bank(4 + b), -1.0, many(upper, 4),
                                       ALU.mult, ALU.mult).then_inc(S("beta_rows_out"), 1)
            got("beta_rows_out", 4)

            def twice(b):
                return ps[b][:, :].rearrange("p (a t) -> p a t", a=4).unsqueeze(2).broadcast_to([P, 4, 2, P])

            def two_by_two(x):
                return x.rearrange("p (a b) t -> p a b t", b=2)
            for n in range(NT):
                n8 = slice(8 * n, 8 * n + 8)
                got("gam_exp")
                step(V.tensor_tensor(GAM[:, n8, :], GAM[:, n8, :], many(upper_eq, 8), ALU.mult))
                settle()
                got("gkk_summed")
                g4 = two_by_two(GAM[:, n8, :])
                step(V.tensor_tensor(two_by_two(gLT[:, n8, :]), g4, twice(4 + 2 * n), ALU.mult))
                V.tensor_tensor(two_by_two(AT[:, n8, :]), g4, twice(5 + 2 * n), ALU.mult).then_inc(S("gkk_out"), 1)
                settle()
                step(V.tensor_tensor(gLT[:, n8, :], gLT[:, n8, :], gPM[:, n8, :], ALU.mult))
                settle()
                step(V.tensor_tensor(gTT[:, n8, :], gLT[:, n8, :], many(off[:, 0, :], 8), ALU.mult))
                settle()
                V.tensor_tensor(gTT[:, n8, :], gTT[:, n8, :], many(ident[:], 8), ALU.add).then_inc(S("gtt_start"), 1)
            got("gtt_start", 2)
            for b in range(4):
                got("gtm_turned")
                V.tensor_copy(gTM[:, 4 * b:4 * b + 4, :], bank((0, 2, 6, 7)[b]))
                inv_off(1, b, lambda b: gLT[:, 4 * b:4 * b + 4, :], gLO)
            inversion(lambda b: gLT[:, 4 * b:4 * b + 4, :], gLO, gTM, gTT)
            for b in range(4):
                got("wt_summed")
                V.tensor_copy(WT[:, 4 * b:4 * b + 4, :], bank(4 + b)).then_inc(S("wt_out"), 1)
            got("u0_out", 4)
            for c in range(NCH):
                n, r = c // 2, slice(C * (c % 2), C * (c % 2) + C)
                for hb in range(2):
                    got("ws_summed")
                    V.tensor_tensor(VN[r, 4 * hb:4 * hb + 4, :], U0[r, 8 * n + 4 * hb:8 * n + 4 * hb + 4, :],
                                    ps[hb][r, :].rearrange("p (h t) -> p h t", h=4), ALU.subtract)\
                        .then_inc(S("vn_made"), 1)
                for hb in range(2):
                    got("gs_summed")
                    for i in range(4):
                        h = 4 * hb + i
                        k = 4 * h + c
                        ins = V.scalar_tensor_tensor(gS[(c + 1) % 2][:, h, :], gS[c % 2][:, h, :], gdecay[:, k:k + 1],
                                                     ps[2 + hb][:, i * P:(i + 1) * P], ALU.mult, ALU.add)
                    ins.then_inc(S("gs_out"), 1)
                got("gs_out", 2)
            head_rsqrt(1.0 / P, 1e-6)
            got("z_act")
            for q in range(4):
                got("hr_bc")
                s2 = slice(2 * q, 2 * q + 2)
                step(V.tensor_tensor(OG[:, s2, :], OG[:, s2, :], pair_of(q), ALU.mult))
            settle()
            c = COL["gdn_norm_w"]
            V.scalar_tensor_tensor(OG[:], OG[:], vec[:, c:c + 1], PR[:, T_Z:T_Z + 8, PAD:TP], ALU.mult, ALU.mult)\
                .then_inc(S("yb_full"), 1)
            got("mix_hi")
            V.tensor_tensor(H[:, 1, PAIRS:KT, :], OG[:], H[:, 0, PAIRS:KT, :].bitcast(F32), ALU.subtract)\
                .then_inc(S("mix_made"), 1)

            def residual(m0, u_end, half):
                for f in range(GROUP):
                    summed(m0, f, u_end)
                    x = X[:, half * 8 + f, :]
                    V.tensor_tensor(x, x, ps[f][:, 0:T], ALU.add).then_inc(bank_freed, 1)

            def out_phase(u0, n0, m0, norm_args):
                for g in range(2):
                    u = u0 + g * UG
                    for j in range(2, UG + 1):
                        lo(u + j)
                    residual(m0 + 7 * g, u + UG, g)
                    if g == 0:
                        lo(u + UG + 1)
                dve.wait_ge(bank_freed, n0 + 16 + FREE_BANKS)
                norm(*norm_args, between=lambda: lo(u0 + 2 * UG + 1))

            def down(u0, m0, last=False):
                for half in range(2):
                    b = u0 + half * (FT // 2)
                    with dve.Fori(0, 5) as i:
                        for j in range(4):
                            lo(b + 2 + j, i, 4)
                    if not (last and half):
                        lo(b + 22)
                    residual(m0 + 7 * half, b + 22, half)
                    if not half:
                        lo(b + 23)

            lo(U_OUT)
            lo(U_OUT + 1)
            out_phase(U_OUT, N_OUT, M_OUT, (1, "ffn_norm_w", 1e-5))
            dve.sem_inc(S("hid_made"), 1)

            def ffn_phase(u0, evac, tail):
                for j in range(2, UG):
                    lo(u0 + j)
                with dve.Fori(0, 10) as g:
                    lo(u0 + UG, g, UG)
                    evac(g)
                    for j in range(1, UG):
                        lo(u0 + UG + j, g, UG)
                        tail(g, j)
                lo(u0 + 11 * UG)
                evac(10)
                lo(u0 + 11 * UG + 1)
                for j in range(1, UG):
                    tail(10, j)

            def evac_ffn1(g):
                for i in range(4):
                    dve.wait_ge(S("gate_act"), g * 4 + (i + 1))
                    if i == 0:
                        dve.wait_ge(S("hid_made"), g + 1)
                    summed(M_FFN1, 2 * i + 1, U_FFN1 + UG, g)
                    V.tensor_tensor(HS[:, i, :], SG[:, i, :], ps[2 * i + 1][:, 0:T], ALU.mult).then_inc(bank_freed, 2)

            def tail_ffn1(g, j):
                if j == 1:
                    dve.wait_ge(S("hid_hi"), g + 1)
                    V.tensor_tensor(HID[:, 1, bass.ds(g * 4, 4), :], HS[:],
                                    HID[:, 0, bass.ds(g * 4, 4), :].bitcast(F32), ALU.subtract)\
                        .then_inc(S("hid_made"), 1)
            ffn_phase(U_FFN1, evac_ffn1, tail_ffn1)
            down(U_DOWN1, M_DOWN1)
            dve.wait_ge(bank_freed, N_MISC2 + FREE_BANKS)
            inverse_root(2, 1e-5)
            c = COL["final_norm_w"]
            for f in range(KT):
                V.scalar_tensor_tensor(X[:, f, :], X[:, f, :], vec[:, c + f:c + f + 1], rstd[:], ALU.mult, ALU.mult)\
                    .then_inc(S("x_scaled"), 1)
            lo(U_MISC2 + 1)
            dve.wait_ge(S("x_scaled"), KT)
            norm(3, "mix_norm_2", 1e-6)
            lo(U_MISC2 + 2)
            lo(U_MISC2 + 3)
            lo(U_FOX)
            dve.wait_ge(unit_used, U_FOX + FREE_UNITS)
            V.tensor_copy(FM[:], ps[0][:, 0:T]).then_inc(bank_freed, 8)
            lo(U_FOX + 1)

            def evac_fox(g):
                for f in range(GROUP):
                    summed(M_FOX, f, U_FOX + UG, g)
                    V.tensor_copy(QKV[:, bass.ds(g * 8 + f, 1), :], ps[f][:, 0:T]).then_inc(bank_freed, 1)
            group_phase(U_FOX, 6, evac_fox)

            dve.wait_ge(bank_freed, N_OUT2 + FREE_BANKS)
            dve.sem_inc(S("att_in"), 1)
            got("f_rows")
            f16 = slice(0, 16)
            step(V.tensor_scalar(FW[f16, 0, :], ps[7][f16, 0:T], fox_bias, -1.0, ALU.add, ALU.mult))
            settle()
            step(V.tensor_scalar(FW[f16, 1, :], FW[f16, 0, :], -1.0, None, ALU.mult))
            settle()
            step(V.tensor_tensor(FW[f16, 1, :], FW[f16, 1, :], FW[f16, 0, :], ALU.max))
            step(V.tensor_scalar(FW[f16, 2, :], FW[f16, 0, :], 0.0, None, ALU.max))
            settle()
            for part, gain in enumerate(("fox_q_gain_2", "fox_k_gain_2")):
                c = COL[gain]
                head_rsqrt(1.0 / P, 1e-6)
                for q in range(8):
                    got("hr_bc")
                    s2 = QKV[:, 16 * part + 2 * q:16 * part + 2 * q + 2, :]
                    step(V.scalar_tensor_tensor(s2, s2, vec[:, c:c + 1], pair_of(q), ALU.mult, ALU.mult))
                settle()
                if part == 0:
                    step(V.tensor_scalar(QKV[:, 0:16, :], QKV[:, 0:16, :], float(P) ** -0.5, None, ALU.mult))
                    settle()
                    dve.sem_inc(S("att_in"), 1)
                    dve.sem_inc(S("softplus_abs"), 1)
            dve.sem_inc(S("qk_normed"), 1)
            got("softplus_exp")
            V.tensor_scalar(FW[f16, 1, :], FW[f16, 1, :], 1.0, None, ALU.add).then_inc(S("softplus_plus1"), 1)
            got("softplus_ln")
            step(V.tensor_tensor(FW[f16, 0, :], FW[f16, 1, :], FW[f16, 2, :], ALU.add))
            settle()
            step(V.memset(FW[f16, 1, :], 1.0))
            settle()
            V.tensor_tensor_scan(FW[f16, 2, :], FW[f16, 1, :], FW[f16, 0, :], 0.0, ALU.mult, ALU.add)\
                .then_inc(S("forget_summed"), 1)
            for b in range(1, 8, 2):
                got("v_turned_v")
                V.tensor_copy(VT[:, b // 4, (b % 4) * 512:(b % 4 + 1) * 512], ps[b][:, :]).then_inc(S("vt_made_v"), 1)
            got("forget_cols")
            V.tensor_copy(FQ[:], ps[0][:, 0:32].rearrange("p (n h) -> p n h", n=NT)).then_inc(S("forget_cols_out"), 1)
            for q in range(8):
                got("forget_rows")
                rows2 = ps[q][:, :].rearrange("p (h n t) -> p h n t", h=2, n=2)
                cb = CB[:, 2 * q:2 * q + 2, :, :]
                V.tensor_tensor(cb[:, :, 0, :], rows2[:, :, 0, :], many(causal[:], 2), ALU.add)
                V.tensor_copy(cb[:, :, 1, :], rows2[:, :, 0, :])
                V.tensor_tensor(cb[:, :, 2, :], rows2[:, :, 1, :], many(causal[:], 2), ALU.add)\
                    .then_inc(S("bias_made"), 1)
            got("bias_made", 8)

            def probs(h):
                z = h % 2
                got("scores_made")
                for n, c0, w, blk in ((0, 0, P, 0), (1, P, T, 1)):
                    src = CB[:, h, blk:blk + w // P, :].rearrange("p b t -> p (b t)")
                    step(V.scalar_tensor_tensor(SC[:, z, c0:c0 + w], src, FQ[:, n, h:h + 1], ps[z][:, c0:c0 + w],
                                                ALU.subtract, ALU.add))
                settle()
                for n, c0, w in ((0, 0, P), (1, P, T)):
                    V.tensor_reduce(AST[:, z, n:n + 1], SC[:, z, c0:c0 + w], AX_X, ALU.max, negate=True)\
                        .then_inc(S("score_max"), 1)
                got("prob_made", 2)
                step(V.reciprocal(AST[:, z, 4:6], AST[:, z, 2:4]))
                settle()
                for n, c0, w in ((0, 0, P), (1, P, T)):
                    ins = V.tensor_scalar(SC[:, z, c0:c0 + w], SC[:, z, c0:c0 + w], AST[:, z, 4 + n:5 + n], None,
                                          ALU.mult)
                ins.then_inc(S("prob_normed"), 1)

            def out_lo(h):
                got("att_hi")
                V.tensor_tensor(H[:, 1, h, :], ps[4 + h % 2][:, 0:T], H[:, 0, h, :].bitcast(F32), ALU.subtract)\
                    .then_inc(S("att_made"), 1)
            for h in range(A_HEADS):
                probs(h)
                if h:
                    out_lo(h - 1)
            out_lo(A_HEADS - 1)

            out_phase(U_OUT2, N_OUT2, M_OUT2, (4, "ffn_norm_2", 1e-6))
            step(V.memset(UC[:, :, 0:2], 0.0))
            settle()

            def y(i):
                return (YG, YV)[i % 2][:, i // 2, :]

            def tap(g, k, i):
                c = COL[f"conv{k}"] + (i % 2) * FT + i // 2
                return vec[:, bass.ds(g * 4 + c, 1)]

            def evac_ffn2(g):
                cb = COL["ffn_conv_b_2"]
                for i in range(GROUP):
                    dve.wait_ge(bank_freed, g * 8 + (N_FFN2 + i + 1 + FREE_BANKS))
                    if i == 0:
                        dve.wait_ge(S("hid_made"), g + 12)
                    ins = V.tensor_scalar(y(i), UC[:, i, 0:T], tap(g, 0, i),
                                          vec[:, bass.ds(g * 4 + (cb + (i % 2) * FT + i // 2), 1)], ALU.mult, ALU.add)
                ins.then_inc(S("conv_step"), 1)

            def tail_ffn2(g, j):
                if j in (1, 2):
                    dve.wait_ge(S("conv_step"), g * 3 + j)
                    for i in range(GROUP):
                        ins = V.scalar_tensor_tensor(y(i), UC[:, i, j:j + T], tap(g, j, i), y(i), ALU.mult, ALU.add)
                    ins.then_inc(S("conv_step"), 1)
                elif j == 4:
                    dve.wait_ge(S("conv_gate"), g + 1)
                    V.tensor_tensor(YV[:], YG[:], YV[:], ALU.mult).then_inc(S("hid_full"), 1)
                elif j == 6:
                    dve.wait_ge(S("hid_hi"), g + 12)
                    V.tensor_tensor(HID[:, 1, bass.ds(g * 4, 4), :], YV[:],
                                    HID[:, 0, bass.ds(g * 4, 4), :].bitcast(F32), ALU.subtract)\
                        .then_inc(S("hid_made"), 1)
            ffn_phase(U_FFN2, evac_ffn2, tail_ffn2)
            down(U_DOWN2, M_DOWN2, last=True)
            for q in range(4):
                got("y_turned_v")
                V.tensor_copy(OUTT[:, 1, q * 512:(q + 1) * 512], ps[4 + q][:, :]).then_inc(S("y_tokens_1"), 1)

        @block.tensor
        def _(pe):
            mm = nc.tensor.matmul

            def h_in(part, k):
                return H[:, part, k, :]

            def unit(u, tiles, nf, wcol, first=False, last=False, g=None, step=0, n0=None, hcol=h_in, h_wait=None):
                v = u + 1
                pe.wait_ge(lo_made, v if g is None else g * step + v)
                for kk, k in enumerate(tiles):
                    if h_wait is not None and kk == 0:
                        pe.wait_ge(*h_wait)
                    for f in range(nf):
                        if first and kk == 0:
                            bv = n0 + f + 1 - 8 + FREE_BANKS
                            pe.wait_ge(bank_freed, bv if g is None else g * 8 + bv)
                        c = wcol(kk, f)
                        hi_w, lo_w = HIW[:, u % 2, c:c + P], LOW[:, u % 4, c:c + P]
                        h_hi, h_lo = hcol(0, k), hcol(1, k)
                        start, stop = first and kk == 0, last and kk == len(tiles) - 1
                        o_ = ps[f][:, 0:T]
                        mm(o_, hi_w, h_hi, start=start, stop=False)
                        mm(o_, hi_w, h_lo, start=False, stop=False)
                        i = mm(o_, lo_w, h_hi, start=False, stop=stop)
                        if kk == len(tiles) - 1 and f == nf - 1:
                            i.then_inc(unit_used, 1)
                        elif stop:
                            i.then_inc(tile_summed, 1)

            def plain(kk, f):
                return kk * 1024 + f * P

            def gate_up_col(kk, i):
                return kk * 1024 + (i % 2) * 512 + (i // 2) * P

            def group_phase(u0, n0, groups, wcol=plain, k_norm=None):
                with pe.Fori(0, groups) as g:
                    for j in range(UG):
                        hw = None if k_norm is None else (S("h_made"), 8 * HN[k_norm] + j + 1)
                        unit(u0 + j, [2 * j, 2 * j + 1], GROUP, wcol, j == 0, j == UG - 1, g, UG, n0, h_wait=hw)

            def down(u0, n0, made0):
                for half in range(2):
                    b = u0 + half * (FT // 2)
                    for j in range(2):
                        unit(b + j, [2 * j, 2 * j + 1], GROUP, plain, j == 0, n0=n0 + 8 * half,
                             hcol=lambda part, k: HID[:, part, k, :], h_wait=(S("hid_made"), made0 + 10))
                    with pe.Fori(0, 4) as i:
                        for j in range(4):
                            unit(b + 2 + j, [4 + 2 * j, 5 + 2 * j], GROUP, plain, g=i, step=4,
                                 hcol=lambda part, k: HID[:, part, bass.ds(i * 8 + k, 1), :])
                    for j in range(18, 22):
                        unit(b + j, [2 * j, 2 * j + 1], GROUP, plain, last=j == 21,
                             hcol=lambda part, k: HID[:, part, k, :], h_wait=(S("hid_made"), made0 + 11))

            def norm(k, presummed=True):
                sq = NSQ_H if k == 2 else NSQ
                for f in range(8 if presummed else 0, KT):
                    pe.wait_ge(S("squared"), KT * k + f + 1)
                    i = mm(ps[0][:, 0:T], ones[:], sq[:, f, :], start=f == (8 if presummed else 0),
                           stop=f == KT - 1 and not presummed)
                if presummed:
                    pe.wait_ge(S("squares_presummed"), {1: 1, 2: 2, 4: 3}[k])
                    i = mm(ps[0][:, 0:T], ones[:], sq[:, 0, :], start=False, stop=True)
                i.then_inc(S("squares_summed"), 1)

            pe.sem_inc(unit_used, FREE_UNITS)
            pe.wait_ge(S("ident_made"), 1)
            for n in range(NT):
                pe.wait_ge(S(f"x_landed_{n}"), 16)
                for q in range(4):
                    for i in range(4):
                        f = 4 * q + i
                        ins = nc.tensor.transpose(ps[4 * n + q][:, i * P:(i + 1) * P], XIN[:, n, f * P:(f + 1) * P],
                                                  ident[:])
                    ins.then_inc(S("x_turned"), 1)
            pe.wait_ge(S("vecs_landed"), counts["vecs_landed"])
            pe.wait_ge(S("x_tiles"), 8)
            for i, pack in enumerate(PACKS):
                r = sum(n for _, n in pack)
                if i >= 4:
                    pe.wait_ge(S("vecs_made"), i - 3)
                nc.tensor.transpose(ps[i % 4][:, (i // 4) * P:(i // 4) * P + r], VPACK[0:r, i, :],
                                    ident[0:r, 0:r]).then_inc(S("vecs_turned"), 1)
            pe.wait_ge(S("vecs_made"), len(PACKS))
            norm(0, presummed=False)
            for j in range(4):
                unit(j, [4 * j + i for i in range(4)], 3, lambda kk, f: kk * 384 + f * P, j == 0, j == 3,
                     n0=N_MISC1, h_wait=(S("h_made"), 2 * j + 2))
            group_phase(U_IN, N_IN, 6)

            got = waiter(pe)
            got("loras_landed", 64)
            got("lowrank_ready")
            for name, r, b0 in (("w_lora", slice(0, 64), 0), ("a_lora", slice(64, 128), 4)):
                for t in range(PAIRS):
                    ins = mm(ps[b0 + t // 2][:, (t % 2) * T:(t % 2 + 1) * T], WA_UP[r, t * P:(t + 1) * P],
                             PR[r, T_WA, PAD:TP], start=True, stop=True)
                    if t % 2:
                        ins.then_inc(S(name), 1)

            def head_rsqrt(src, tiles, sel, width):
                got("hr_sq")
                for f in range(tiles):
                    ins = mm(ps[0][0:16, 0:T], sel[:, 15 - f * width - (width - 1):31 - f * width - (width - 1)],
                             src[:, f, :], start=f == 0, stop=f == tiles - 1)
                ins.then_inc(S("hr_sum"), 1)
                got("hr_inv")
                for f in range(tiles):
                    n = P // width
                    for e in range(width):
                        h = f * width + e
                        ins = mm(ps[f // 2][e * n:(e + 1) * n, (f % 2) * T:(f % 2 + 1) * T],
                                 ident[0:16, h:h + 1].broadcast_to([16, n]), rstd[0:16], start=True, stop=True)
                    if f % 2:
                        ins.then_inc(S("hr_bc"), 1)

            def head_sums(src, b0, name):
                for q in range(4):
                    mm(ps[b0 + q][:, :], headones[:], src[:, 2 * q:2 * q + 2, :], start=True, stop=True)\
                        .then_inc(S(name), 1)
            got("w_lora_sigmoid")
            head_rsqrt(KK, PAIRS, sel2, 2)
            got("bonus_terms")
            got("a_lora_sigmoid")
            head_sums(RN, 4, "bonus_summed")
            got("hats_made")

            def inversion(LO, TM, TT, PM):
                for lev in range(1, 6):
                    for b in range(4):
                        got("inv_off")
                        if lev > 1:
                            got("inv_added")
                        for h in range(4 * b, 4 * b + 4):
                            ins = mm(ps[2 * b][:, (h % 4) * P:(h % 4 + 1) * P], LO[:, h, :], TM[:, h, :],
                                     start=True, stop=True)
                        ins.then_inc(S("inv_p"), 1)
                    for b in range(4):
                        got("inv_pm")
                        if lev < 5:
                            for h in range(4 * b, 4 * b + 4):
                                mm(ps[2 * b][:, (h % 4) * P:(h % 4 + 1) * P], TT[:, h, :], PM[:, h, :],
                                   start=True, stop=True)
                        for h in range(4 * b, 4 * b + 4):
                            ins = mm(ps[2 * b + 1][:, (h % 4) * P:(h % 4 + 1) * P], PM[:, h, :], TT[:, h, :],
                                     start=True, stop=True)
                        ins.then_inc(S("inv_t"), 1)
                got("inv_added", 4)

            for n in range(NT):
                tn = slice(n * P, n * P + P)
                pn = slice(PAD + n * P, PAD + n * P + P)
                for i, src in enumerate((lambda t: PR[:, T_V + t, pn], lambda t: BH[:, t, tn],
                                         lambda t: PR[:, T_K + t, pn])):
                    for t in range(PAIRS):
                        ins = nc.tensor.transpose(ps[2 * i + t // 4][:, (t % 4) * P:(t % 4 + 1) * P], src(t), ident[:])
                        if t % 4 == 3:
                            ins.then_inc(S("tok_turned"), 1)
                fill = 6
                for which in range(2):
                    for hp in range(2):
                        rr = slice(64 * hp, 64 * hp + 64)
                        for t in range(PAIRS):
                            if t % 2 == 0 and fill >= 8:
                                got("tok_made" if fill < 14 else "l_out")
                            w = BH[rr, t, tn] if which == 0 else PR[rr, T_K + t, pn]
                            ins = mm(ps[fill % 8][:, (t % 2) * T:(t % 2 + 1) * T], w,
                                     AR[rr, t, :, tn], start=True, stop=True)
                            if t % 2:
                                ins.then_inc(S("l_summed"), 1)
                                fill += 1
                for b in range(4):
                    got("l_out")
                    rr = slice(64 * (b // 2), 64 * (b // 2) + 64)
                    for i in range(4):
                        t = 4 * (b % 2) + i
                        ins = mm(ps[fill % 8][:, i * P:(i + 1) * P], AR[rr, t, 0, tn], BH[rr, t, tn],
                                 start=True, stop=True)
                    ins.then_inc(S("l_plain"), 1)
                    fill += 1
                got("l_out", 8)
                inversion(LO, TM, TT, PM)
                for c in (2 * n, 2 * n + 1):
                    r = slice(C * (c % 2), C * (c % 2) + C)
                    cc = slice(c * C, c * C + C)
                    s0 = ST[:, c % 2]
                    for hb in range(2):
                        if c % 2:
                            got("s_out")
                        for i in range(4):
                            t = 4 * hb + i
                            mm(ps[4 * hb][r, i * P:(i + 1) * P], AR[:, t, 0, cc], s0[:, t, :], start=True, stop=False)
                            for hp in range(2):
                                v = slice(64 * hp, 64 * hp + 64)
                                ins = mm(ps[4 * hb][r, i * P + 64 * hp:i * P + 64 * hp + 64],
                                         LKR[:, 8 * hp + t, 0, r], VTOK[:, t, v], start=False, stop=hp == 1)
                        ins.then_inc(S("r1_summed"), 1)
                    for hb in range(2):
                        got("r1_out")
                        for i in range(4):
                            t = 4 * hb + i
                            for hp in range(2):
                                v = slice(64 * hp, 64 * hp + 64)
                                ins = mm(ps[1 + 4 * hb][r, i * P + 64 * hp:i * P + 64 * hp + 64],
                                         TT[:, 8 * hp + t, r], R1[:, t, v], start=True, stop=True)
                        ins.then_inc(S("u_summed"), 1)
                    for hb in range(2):
                        got("u_out")
                        for i in range(4):
                            t = 4 * hb + i
                            o_ = ps[3 + 4 * hb][:, i * P:(i + 1) * P]
                            mm(o_, BTOK[r, t, :], UU[r, t, :], start=True, stop=False)
                            ins = mm(o_, KTOK[r, t, :], VTOK[r, t, :], start=False, stop=True)
                        ins.then_inc(S("s_summed"), 1)
                    for hb in range(2):
                        if c % 2:
                            got("y_out")
                        for i in range(4):
                            t = 4 * hb + i
                            o_ = ps[2 + 4 * hb]
                            mm(o_[:, i * C:(i + 1) * C], s0[:, t, :], AR[:, t, 1, cc], start=True, stop=False)
                            for hp in range(2):
                                v = slice(64 * hp, 64 * hp + 64)
                                mm(o_[v, i * C:(i + 1) * C], UU[:, t, v], LBR[:, 8 * hp + t, 1, r],
                                   start=False, stop=False)
                                ins = mm(o_[v, i * C:(i + 1) * C], VTOK[:, t, v], LKR[:, 8 * hp + t, 1, r],
                                         start=False, stop=True)
                        ins.then_inc(S("y_summed"), 1)
                got("y_out", 2)
                got("s_out", 2)
            head_sums(BH, 0, "y_mean")
            head_rsqrt(RN, PAIRS, sel2, 2)
            got("y_normed")
            for t in range(PAIRS):
                o_ = ps[t // 2][:, (t % 2) * T:(t % 2 + 1) * T]
                mm(o_, G_UP[:, 0, t * P:(t + 1) * P], PR[:, T_G0, PAD:TP], start=True, stop=False)
                ins = mm(o_, G_UP[0:32, 1, t * P:(t + 1) * P], PR[0:32, T_G1, PAD:TP], start=False, stop=True)
                if t % 2:
                    ins.then_inc(S("gate_summed"), 1)

            got("ya_full")
            head_rsqrt(GSQ, 8, sel1, 1)
            got("rows_made")
            got("beta_made")
            for n in range(NT):
                ins = nc.tensor.transpose(ps[4][:, n * P:(n + 1) * P], ROWS[:, n * P:(n + 1) * P], ident[:])
            ins.then_inc(S("cols_turned"), 1)
            got("gqk_normed")

            def g_rows(name):
                for h in range(G_HEADS):
                    ins = mm(ps[h // 2][:, (h % 2) * T:(h % 2 + 1) * T],
                             ident[32:40, 32 + h:33 + h].broadcast_to([8, P]), ROWS[32:40, :], start=True, stop=True)
                    if h % 2:
                        ins.then_inc(S(name), 1)
            g_rows("g_rows")
            got("cols_made")
            for n in range(NT):
                for h in range(G_HEADS):
                    ins = mm(ps[4 + 2 * n + h // 4][:, (h % 4) * P:(h % 4 + 1) * P],
                             ident[64:72, 64 + h:65 + h].broadcast_to([8, P]), ROWS[64:72, n * P:(n + 1) * P],
                             start=True, stop=True)
                    if h % 4 == 3:
                        ins.then_inc(S("beta_rows"), 1)
            got("g_rows_exp", 4)
            got("gam_diff", 2)

            def key_tokens(n):
                for i in range(G_QK):
                    ins = nc.tensor.transpose(ps[n][:, i * P:(i + 1) * P], KC[:, i, n * P:(n + 1) * P], ident[:])
                ins.then_inc(S("gtok_turned"), 1)

            def value_tokens(n):
                for h in range(G_HEADS):
                    ins = nc.tensor.transpose(ps[2 + 2 * n + h // 4][:, (h % 4) * P:(h % 4 + 1) * P],
                                              VC[:, h, n * P:(n + 1) * P], ident[:])
                ins.then_inc(S("gvtok_turned"), 1)
            key_tokens(0)
            value_tokens(0)
            key_tokens(1)
            for n in range(NT):
                tn = slice(n * P, n * P + P)
                got("beta_rows_out", 2)
                for i in range(G_QK):
                    mm(ps[4 + 2 * n][:, i * P:(i + 1) * P], KC[:, i, tn], KC[:, i, tn], start=True, stop=True)
                for i in range(G_QK):
                    ins = mm(ps[5 + 2 * n][:, i * P:(i + 1) * P], KC[:, i, tn], QC[:, i, tn], start=True, stop=True)
                ins.then_inc(S("gkk_summed"), 1)
            got("gkk_out")
            value_tokens(1)
            for b in range(4):
                if b % 2 == 0:
                    got("gtok_made")
                    got("gtt_start")
                for i in range(4):
                    ins = nc.tensor.transpose(ps[(0, 2, 6, 7)[b]][:, i * P:(i + 1) * P], gTT[:, 4 * b + i, :], ident[:])
                ins.then_inc(S("gtm_turned"), 1)
            inversion(gLO, gTM, gTT, gPM)
            for b in range(4):
                for i in range(4):
                    ins = mm(ps[b][:, i * P:(i + 1) * P], gTT[:, 4 * b + i, :], VB[:, 4 * b + i, :],
                             start=True, stop=True)
                ins.then_inc(S("u0_summed"), 1)
            for b in range(4):
                for i in range(4):
                    ins = mm(ps[4 + b][:, i * P:(i + 1) * P], KBE[:, 4 * b + i, :], gTT[:, 4 * b + i, :],
                             start=True, stop=True)
                ins.then_inc(S("wt_summed"), 1)
            got("u0_out", 4)
            got("wt_out", 4)
            for c in range(NCH):
                n, r = c // 2, slice(C * (c % 2), C * (c % 2) + C)
                cc = slice(c * C, c * C + C)
                s0 = gS[c % 2]
                for hb in range(2):
                    if c:
                        got("gs_out")
                    for h in range(4 * hb, 4 * hb + 4):
                        ins = mm(ps[hb][r, (h % 4) * P:(h % 4 + 1) * P], WT[:, 8 * n + h, r], s0[:, h, :],
                                 start=True, stop=True)
                    ins.then_inc(S("ws_summed"), 1)
                for hb in range(2):
                    got("vn_made")
                    for h in range(4 * hb, 4 * hb + 4):
                        ins = mm(ps[2 + hb][:, (h % 4) * P:(h % 4 + 1) * P], KG[r, 8 * n + h, :], VN[r, h, :],
                                 start=True, stop=True)
                    ins.then_inc(S("gs_summed"), 1)
                for hb in range(2):
                    if c:
                        got("o_out")
                    for h in range(4 * hb, 4 * hb + 4):
                        o_ = ps[4 + hb][:, (h % 4) * C:(h % 4 + 1) * C]
                        mm(o_, s0[:, h, :], QG[:, h, cc], start=True, stop=False)
                        ins = mm(o_, VN[:, h, :], AT[:, 8 * n + h, r], start=False, stop=True)
                    ins.then_inc(S("o_summed"), 1)
            got("o_out", 2)
            got("gs_out", 2)
            pe.sem_inc(S("weights_place_free"), 1)
            head_rsqrt(GSQ, 8, sel1, 1)

            got("mix_made", 2)
            group_phase(U_OUT, N_OUT, 2)
            norm(1)
            group_phase(U_FFN1, N_FFN1, 11, gate_up_col, 1)
            down(U_DOWN1, N_DOWN1, 1)
            norm(2)
            norm(3, presummed=False)
            for j in range(4):
                unit(U_MISC2 + j, [4 * j + i for i in range(4)], 1, lambda kk, f: kk * P, j == 0, j == 3,
                     n0=N_MISC2, h_wait=(S("h_made"), 8 * HN[3] + 2 * j + 2))
            group_phase(U_FOX, N_FOX, 6)

            got("att_in")
            mm(ps[7][0:16, 0:T], ident[:, 112:128], FM[:], start=True, stop=True).then_inc(S("f_rows"), 1)
            head_rsqrt(ASQ, 16, sel1, 1)
            head_rsqrt(ASQ, 16, sel1, 1)
            got("qk_normed")
            for b in range(8):
                for i in range(4):
                    ins = nc.tensor.transpose(ps[b][:, i * P:(i + 1) * P],
                                              QKV[:, 32 + (b % 4) * 4 + i, (b // 4) * P:(b // 4 + 1) * P], ident[:])
                ins.then_inc(S("v_turned_v" if b % 2 else "v_turned_a"), 1)
            got("forget_summed")
            got("vt_made_a", 4)
            for n in range(NT):
                ins = nc.tensor.transpose(ps[0][:, n * 16:(n + 1) * 16], FW[0:16, 2, n * P:(n + 1) * P],
                                          ident[0:16, 0:16])
            ins.then_inc(S("forget_cols"), 1)
            got("vt_made_v", 4)
            got("forget_cols_out")
            for h in range(A_HEADS):
                ins = mm(ps[h // 2][:, (h % 2) * T:(h % 2 + 1) * T], ident[0:16, h:h + 1].broadcast_to([16, P]),
                         FW[0:16, 2, :], start=True, stop=True)
                if h % 2:
                    ins.then_inc(S("forget_rows"), 1)
            got("bias_made", 8)

            def scores(h):
                z = h % 2
                mm(ps[z][:, 0:P], QKV[:, h, 0:P], QKV[:, 16 + h, 0:P], start=True, stop=True)
                mm(ps[z][:, P:3 * P], QKV[:, h, P:T], QKV[:, 16 + h, :], start=True, stop=True)\
                    .then_inc(S("scores_made"), 1)

            def mix(h):
                z = h % 2
                got("prob_normed")
                for i in range(3):
                    ins = nc.tensor.transpose(ps[2 + z][:, i * P:(i + 1) * P], SC[:, z, i * P:(i + 1) * P], ident[:])
                ins.then_inc(S("pt_turned"), 1)
                got("pt_made")
                if h >= 2:
                    got("att_made")
                v0, v1 = (VT[:, n, h * P:(h + 1) * P] for n in range(NT))
                mm(ps[4 + z][:, 0:P], v0, PT[:, z, 0:P], start=True, stop=True)
                mm(ps[4 + z][:, P:T], v0, PT[:, z, P:2 * P], start=True, stop=False)
                mm(ps[4 + z][:, P:T], v1, PT[:, z, 2 * P:3 * P], start=False, stop=True)\
                    .then_inc(S("att_summed"), 1)
            for h in range(A_HEADS):
                scores(h)
                if h:
                    mix(h - 1)
            mix(A_HEADS - 1)

            got("att_made", 2)
            group_phase(U_OUT2, N_OUT2, 2)
            norm(4)
            group_phase(U_FFN2, N_FFN2, 11, gate_up_col, 4)
            down(U_DOWN2, N_DOWN2, 12)
            pe.wait_ge(bank_freed, N_END + FREE_BANKS)
            for n in range(NT):
                for q in range(4):
                    for i in range(4):
                        ins = nc.tensor.transpose(ps[4 * n + q][:, i * P:(i + 1) * P],
                                                  X[:, 4 * q + i, n * P:(n + 1) * P], ident[:])
                    ins.then_inc(S("y_turned_v" if n else "y_turned_a"), 1)


def kernel(**inputs):
    import numpy as np
    import concourse.bacc as bacc
    from concourse.bass_utils import run_bass_kernel_spmd

    nc = bacc.Bacc("TRN2", target_bir_lowering=False, num_devices=1)
    arrays, io = {}, {}
    for name in NAMES:
        a = np.ascontiguousarray(inputs[name])
        arrays[f"in_{name}"] = a
        io[name] = nc.dram_tensor(f"in_{name}", a.shape, mybir.dt.from_np(a.dtype), kind="ExternalInput").ap()
    out = nc.dram_tensor("out_y", (1, T, D), F32, kind="ExternalOutput").ap()
    build(nc, io, out)
    return run_bass_kernel_spmd(nc, [arrays], core_ids=[0]).results[0]["out_y"]
```

```python
from contextlib import ExitStack

import concourse.bass as bass
from concourse import mybir

F32 = mybir.dt.float32
F32R = mybir.dt.float32r
ALU = mybir.AluOpType
ACT = mybir.ActivationFunctionType
AX_X = mybir.AxisListType.X

P = 128
T = 256
D = 2048
KT = D // P
FT = 5632 // P
C = 64
NCH = T // C
NT = T // P
UNIT = 2048
RAW_SLOTS, HI_SLOTS = 4, 2
GROUP = 8
UG = KT // 2

R_DIM, R_HEADS, R_HEAD = 1024, 16, 64
PAIRS = R_HEADS // 2
G_HEADS, G_QK = 8, 4
A_HEADS = 16
SCORE_BANKS = (0, 1, 6)
N_RWKV = 3360
DECAY_RATE = 0.6065306597126334
TP = 260
PAD = TP - T
T_WA, T_G0, T_G1 = 0, 1, 2
T_R, T_K, T_V, T_GQ, T_GK, T_GV, T_Z = 3, 11, 19, 27, 31, 35, 43
NTILES = 51

NAMES = ["x", "attn_norm_w", "w_in", "rwkv_mu", "rwkv_w0", "rwkv_w_up", "rwkv_a0", "rwkv_a_up", "rwkv_g_up",
         "rwkv_k_k", "rwkv_k_a", "rwkv_r_k", "rwkv_ln_w", "rwkv_ln_b", "gdn_conv_w", "gdn_A_log",
         "gdn_dt_bias", "gdn_norm_w", "w_out", "ffn_norm_w", "ffn_w_gate", "ffn_w_up", "ffn_w_down",
         "final_norm_w", "mix_norm_2", "ffn_norm_2", "fox_w_in_2", "fox_b_f_2", "fox_q_gain_2",
         "fox_k_gain_2", "fox_w_out_2", "ffn_w_up_2", "ffn_conv_w_2", "ffn_conv_b_2", "ffn_w_down_2"]

PACKS = [
    [("attn_norm_w", 16), ("ffn_norm_w", 16), ("final_norm_w", 16), ("mix_norm_2", 16), ("ffn_norm_2", 16),
     ("gdn_norm_w", 1), ("fox_q_gain_2", 1), ("fox_k_gain_2", 1)],
    [("rwkv_mu", 27), ("rwkv_w0", 8), ("rwkv_a0", 8), ("rwkv_k_k", 8), ("rwkv_k_a", 8), ("rwkv_r_k", 8),
     ("rwkv_ln_w", 8), ("rwkv_ln_b", 8)],
    [("gdn_conv_w", 64)],
    [("conv0", 88)], [("conv1", 88)], [("conv2", 88)], [("ffn_conv_b_2", 88)],
]
COL, _c = {}, 0
for _pack in PACKS:
    for _name, _rows in _pack:
        COL[_name] = _c
        _c += _rows
VEC_COLS = _c


def build(nc, io, out):
    with ExitStack() as ctx:
        sems, counts = {}, {}

        def S(name):
            if name not in sems:
                sems[name] = ctx.enter_context(nc.semaphore(name))
            return sems[name]

        def tick(ins, name, by=1):
            ins.then_inc(S(name), by)
            counts[name] = counts.get(name, 0) + by
            return counts[name]

        def waiter(engine):
            seen = {}

            def got(name, by=1):
                seen[name] = seen.get(name, 0) + by
                engine.wait_ge(S(name), seen[name])
            return got

        def own(engine, name):
            engine.wait_ge(S(name), counts[name])

        def at(name, shape, offset, dt=F32):
            return nc.alloc_sbuf_tensor_at(name, shape, dt, offset=offset)

        o = nc.sbuf_base if isinstance(nc.sbuf_base, int) else 0
        o = (o + 63) // 64 * 64
        base0 = o
        X = at("X", [P, KT, T], o); o += 16384
        w0 = o
        RAW = at("RAW", [P, RAW_SLOTS, UNIT], o)
        LOW = at("LOW", [P, RAW_SLOTS, UNIT], o, F32R); o += 32768
        HIW = at("HIW", [P, HI_SLOTS, UNIT], o, F32R); o += 16384
        ident = at("ident", [P, P], o); o += 512
        ones = at("ones", [P, P], o); o += 512
        headones = at("headones", [P, P], o); o += 512
        vec = at("vec", [P, VEC_COLS], o); o += (VEC_COLS * 4 + 63) // 64 * 64
        small = at("small", [P, 256], o); o += 1024
        causal = at("causal", [P, P], o); o += 512
        rstd = at("rstd", [P, T], o); o += 1024
        h0 = o
        H = at("H", [P, 2, KT, T], h0, F32R); o += 32768
        r2 = o
        end = base0 + 212800
        masks = end - 5632
        upper2 = at("upper2", [P, 2, P], masks)
        upper, upper_eq = upper2[:, 0, :], upper2[:, 1, :]
        lower1 = at("lower1", [P, P], masks + 1024)
        off = at("off", [P, 6, P], masks + 1536)
        chunk_go = at("chunk_go", [P, T], masks + 4608)
        assert r2 + 102192 <= masks and r2 + 90112 + 16600 <= end, (r2, masks, end)

        XIN = at("XIN", [P, NT, D], r2)
        VPACK = at("VPACK", [P, len(PACKS), P], r2 + 16384)
        NSQ = at("NSQ", [P, KT, T], r2)
        NSQ_H = at("NSQ_H", [P, KT, T], h0)
        PR = at("PR", [P, NTILES, TP], r2)
        a3 = r2 + 53056
        KQ = at("KQ", [P, PAIRS, T], a3)
        KSQ = at("KSQ", [P, PAIRS, T], a3 + 8192)
        SHIFT = at("SHIFT", [P, 2, 3, T], a3 + 16384)
        GS = at("GS", [P, PAIRS, T], h0)
        ENG = at("ENG", [P, PAIRS, T], h0 + 8192)
        KK = at("KK", [P, PAIRS, T], h0 + 16384)
        TMP = at("TMP", [P, PAIRS, T], h0 + 24576)
        AR = at("AR", [P, PAIRS, 2, T], a3)
        RN = at("RN", [P, PAIRS, T], a3)
        RN2 = at("RN2", [P, PAIRS, T], a3 + 8192)
        BH = at("BH", [P, PAIRS, T], a3 + 16384)
        BON = at("BON", [P, PAIRS, T], a3 + 24576)
        WA_UP = at("WA_UP", [P, R_DIM], a3 + 24576)
        EG = at("EG", [P, PAIRS, T], a3 + 32768)
        G_UP = at("G_UP", [P, 2, R_DIM], a3 + 40960)
        VTOK = at("VTOK", [P, PAIRS, P], a3 + 32768)
        BTOK = at("BTOK", [P, PAIRS, P], a3 + 36864)
        R1 = at("R1", [P, PAIRS, P], r2 + T_R * TP * 4 + 16)
        UU = at("UU", [P, PAIRS, P], r2 + T_R * TP * 4 + 16 + 4096)
        LBR = at("LBR", [P, 16, 2, P], h0)
        LKR = at("LKR", [P, 16, 2, P], h0 + 16384)
        TT = at("TT", [P, 16, P], w0)
        TM = at("TM", [P, 16, P], w0 + 8192)
        PM = at("PM", [P, 16, P], w0 + 16384)
        LO = at("LO", [P, 16, P], w0 + 24576)
        KTOK = at("KTOK", [P, PAIRS, P], w0 + 32768)
        ST = at("ST", [P, 2, PAIRS, P], w0 + 36864)

        rdecay, gdecay = small[:, 0:32], small[:, 32:64]
        a_log, dt_bias, fox_bias = small[32:40, 64:65], small[32:40, 65:66], small[96:128, 66:67]
        sel1, sel2 = small[:, 80:111], small[:, 112:142]
        g_exp, k_left, beta_exp = (small[:, c:c + 16].rearrange("p (n h) -> p n h", n=NT) for c in (144, 160, 176))

        QKVC = PR[:, T_GQ:T_GQ + 16, PAD:TP]
        CV = at("CV", [P, 4, T], w0 + 45056)
        QC, KC, VC = QKVC[:, 0:4, :], QKVC[:, 4:8, :], QKVC[:, 8:16, :]
        QG = at("QG", [P, 8, T], a3 + 16384)
        KBE = at("KBE", [P, 16, P], a3 + 24576)
        KG = at("KG", [P, 16, P], a3 + 32768)
        U0 = at("U0", [P, 16, P], a3 + 40960)
        OG = at("OG", [P, 8, T], a3)
        WT = at("WT", [P, 16, P], a3 + 8192)
        GAM = at("GAM", [P, 16, P], r2)
        AT = at("AT", [P, 16, P], r2 + 8192)
        VB = at("VB", [P, 16, P], r2 + 16384)
        VN = at("VN", [P, 8, P], w0 + 45056)
        gTT = at("gTT", [P, 16, P], w0)
        gTM = at("gTM", [P, 16, P], w0 + 8192)
        gPM = at("gPM", [P, 16, P], w0 + 16384)
        gLO = at("gLO", [P, 16, P], w0 + 24576)
        gLT = at("gLT", [P, 16, P], w0 + 32768)
        gS = [at("gS0", [P, 8, P], w0 + 40960), at("gS1", [P, 8, P], h0 + 28672)]
        ROWS = at("ROWS", [P, T], h0 + 12288)
        RWK = at("RWK", [P, 2, T], h0 + 13312)
        COLS = at("COLS", [P, NT, P], h0 + 24576)
        QKSQ = at("QKSQ", [P, 8, T], h0 + 16384)
        GSQ = at("GSQ", [P, 8, T], a3 + 24576)
        HID = at("HID", [P, 2, FT, T], r2, F32R)
        f0 = r2 + 2 * FT * T * 4
        SG = at("SG", [P, 4, T], f0)
        HS = at("HS", [P, 4, T], f0 + 4096)
        UC = at("UC", [P, 8, T + 2], f0)
        YG = at("YG", [P, 4, T], f0 + 8256)
        YV = at("YV", [P, 4, T], f0 + 12352)
        assert f0 + 16448 <= end
        QKV = at("QKV", [P, 48, T], r2)
        FM = at("FM", [P, T], r2 + 49152)
        VT = at("VT", [P, NT, D], r2 + 50176)
        ASQ = at("ASQ", [P, 32, T], r2 + 50176)
        CB = at("CB", [P, A_HEADS, 3, P], r2 + 66560)
        SC = at("SC", [P, 3, 384], r2 + 91136)
        PT = at("PT", [P, 2, 384], r2 + 95744)
        FW = at("FW", [P, 3, T], r2 + 98816)
        f_in = slice(96, 128)
        AST = at("AST", [P, 3, 8], r2 + 101888)
        FQ = at("FQ", [P, NT, A_HEADS], r2 + 101984)
        OUTT = at("OUTT", [P, NT, D], r2)

        ps = [ctx.enter_context(nc.psum_tensor(f"ps{i}", [P, 512], F32)) for i in range(8)]

        w_in, w_out = io["w_in"][0], io["w_out"][0]

        fox = io["fox_w_in_2"][0]
        wup2 = io["ffn_w_up_2"][0]
        U_MISC1, U_IN = 0, 4
        U_OUT = U_IN + 6 * UG
        U_FFN1 = U_OUT + 2 * UG
        U_DOWN1 = U_FFN1 + 11 * UG
        U_MISC2 = U_DOWN1 + FT
        U_FOX = U_MISC2 + 4
        U_OUT2 = U_FOX + 6 * UG
        U_FFN2 = U_OUT2 + 2 * UG
        U_DOWN2 = U_FFN2 + 11 * UG
        U_END = U_DOWN2 + FT
        N_MISC1, N_IN = 0, 8
        N_OUT = N_IN + 48
        N_FFN1 = N_OUT + 16
        N_DOWN1 = N_FFN1 + 88
        N_MISC2 = N_DOWN1 + 16
        N_FOX = N_MISC2 + 8
        N_OUT2 = N_FOX + 48
        N_FFN2 = N_OUT2 + 16
        N_DOWN2 = N_FFN2 + 88
        N_END = N_DOWN2 + 16

        M_IN, M_OUT, M_FFN1, M_DOWN1, M_FOX, M_OUT2, M_FFN2, M_DOWN2 = 2, 44, 58, 135, 149, 191, 205, 282

        landed = [S(f"weights_landed_{i}") for i in range(RAW_SLOTS)]
        unit_used = S("unit_used")
        hi_made, lo_made = S("hi_made"), S("lo_made")
        bank_freed = S("bank_freed")
        tile_summed = S("tile_summed")
        FREE_UNITS, FREE_BANKS = RAW_SLOTS, 8

        def rows(w, k, c0, n):
            return w[k * P:(k + 1) * P, c0:c0 + n]

        def unit_cols(u):
            return 1536 if u < U_IN else 512 if U_MISC2 <= u < U_FOX else UNIT

        HN = {0: 0, 1: 1, 3: 2, 4: 3}

        block = ctx.enter_context(nc.Block())

        @block.sync
        def _(sp):
            def slot_free(u):
                if isinstance(u, int) and u < RAW_SLOTS:
                    return
                sp.wait_ge(unit_used, u - RAW_SLOTS + 1 + FREE_UNITS)

            def load2(u, j, dsts, srcs):
                slot_free(u)
                for d, s in zip(dsts, srcs):
                    sp.dma_start(d, s).then_inc(landed[j % RAW_SLOTS], 16)

            def halves(j, cols=1024):
                s = RAW[:, j % RAW_SLOTS, :]
                return [s[:, 0:cols], s[:, cols:2 * cols]]

            def stream(u0, groups, sources):
                with sp.Fori(0, groups) as g:
                    for j in range(UG):
                        load2(g * UG + (u0 + j), u0 + j, halves(u0 + j), sources(g, j))

            def stream_down(u0, w):
                for half in range(2):
                    b = u0 + half * (FT // 2)

                    def srcs(k):
                        return [w[bass.ds(k * P + i * P, P) if not isinstance(k, int) else
                                  slice((k + i) * P, (k + i + 1) * P), half * 1024:half * 1024 + 1024]
                                for i in range(2)]
                    for j in range(2):
                        load2(b + j, b + j, halves(b + j), srcs(2 * j))
                    with sp.Fori(0, 5) as i:
                        for j in range(4):
                            load2(i * 4 + (b + 2 + j), b + 2 + j, halves(b + 2 + j), srcs(i * 8 + (4 + 2 * j)))

            for n in range(NT):
                sp.dma_start(XIN[:, n, :], io["x"][0, n * P:(n + 1) * P, :]).then_inc(S(f"x_landed_{n}"), 16)
            sp.wait_ge(S("vpack_zeroed"), 1)
            n_dma = 0
            for i, pack in enumerate(PACKS):
                r = 0
                for name, rows_ in pack:
                    if name.startswith("conv"):
                        src = io["ffn_conv_w_2"][0, int(name[4])].rearrange("(r q) -> r q", q=P)
                    elif name == "gdn_conv_w":
                        src = io[name][0].rearrange("k (r q) -> (k r) q", q=P)
                    elif name == "rwkv_r_k":
                        src = io[name][0].rearrange("(r e) q -> r (e q)", e=2)
                    elif name == "final_norm_w":
                        src = io[name].rearrange("(r q) -> r q", q=P)
                    elif name == "rwkv_mu":
                        src = io[name][0, 0:26 * P].rearrange("(r q) -> r q", q=P)
                        sp.dma_start(VPACK[r + 26:r + 27, i, 0:32], io[name][0:1, 26 * P:N_RWKV])\
                            .then_inc(S("vecs_landed"), 16)
                        n_dma += 1
                        rows_ = 26
                    else:
                        src = io[name][0].rearrange("(r q) -> r q", q=P)
                    sp.dma_start(VPACK[r:r + rows_, i, :], src).then_inc(S("vecs_landed"), 16)
                    n_dma += 1
                    r += 27 if name == "rwkv_mu" else rows_
            counts["vecs_landed"] = 16 * n_dma
            sp.wait_ge(S("misc_zeroed"), 1)
            for j in range(4):
                v = RAW[:, j, 0:1536].rearrange("p (k n) -> p k n", k=4)
                src = w_in[4 * j * P:4 * (j + 1) * P, :].rearrange("(k p) n -> p k n", p=P)
                slot_free(j)
                sp.dma_start(v[:, :, 0:288], src[:, :, 3072:3360]).then_inc(landed[j], 16)
                for e in range(2):
                    sp.dma_start(v[:, :, 288 + 32 * e:296 + 32 * e],
                                 src[:, :, 6432 + 8 * e:6440 + 8 * e]).then_inc(landed[j], 16)
            for part, c0 in ((0, 0), (1, N_RWKV)):
                stream(U_IN + part * 3 * UG, 3, lambda g, j, c0=c0: [
                    w_in[(2 * j + i) * P:(2 * j + i + 1) * P, bass.ds(g * 1024 + c0, 1024)] for i in range(2)])
            sp.wait_ge(S("weights_place_free"), 1)
            stream(U_OUT, 2, lambda g, j: [
                w_out[(2 * j + i) * P:(2 * j + i + 1) * P, bass.ds(g * 1024, 1024)] for i in range(2)])

            def gate_up(w_gate, w_up, shift):
                def sources(g, j):
                    return [w[2 * j * P:(2 * j + 2) * P, bass.ds(g * 512 + c, 512)]
                            .rearrange("(k p) n -> p k n", p=P) for w, c in ((w_gate, 0), (w_up, shift))]
                return sources

            def stream_gate_up(u0, sources):
                with sp.Fori(0, 11) as g:
                    for j in range(UG):
                        v = RAW[:, (u0 + j) % RAW_SLOTS, :].rearrange("p (k a n) -> p a k n", k=2, a=2)
                        load2(g * UG + (u0 + j), u0 + j, [v[:, 0], v[:, 1]], sources(g, j))

            stream_gate_up(U_FFN1, gate_up(io["ffn_w_gate"][0], io["ffn_w_up"][0], 0))
            stream_down(U_DOWN1, io["ffn_w_down"][0])
            for j in range(4):
                u = U_MISC2 + j
                v = RAW[:, j, 0:512].rearrange("p (k n) -> p k n", k=4)
                src = fox[4 * j * P:4 * (j + 1) * P, 6032:6160].rearrange("(k p) n -> p k n", p=P)
                load2(u, j, [v[:, 0:2], v[:, 2:4]], [src[:, 0:2], src[:, 2:4]])
            stream(U_FOX, 6, lambda g, j: [
                fox[(2 * j + i) * P:(2 * j + i + 1) * P, bass.ds(g * 1024, 1024)] for i in range(2)])
            fox_out = io["fox_w_out_2"][0]
            stream(U_OUT2, 2, lambda g, j: [
                fox_out[(2 * j + i) * P:(2 * j + i + 1) * P, bass.ds(g * 1024, 1024)] for i in range(2)])
            stream_gate_up(U_FFN2, gate_up(wup2, wup2, FT * P))
            stream_down(U_DOWN2, io["ffn_w_down_2"][0])
            for n in range(NT):
                for q in range(4):
                    sp.wait_ge(S(f"y_tokens_{n}"), q + 1)
                    sp.dma_start(out[0, n * P:(n + 1) * P, q * 512:(q + 1) * 512],
                                 OUTT[:, n, q * 512:(q + 1) * 512]).then_inc(S("y_stored"), 16)
            sp.wait_ge(S("y_stored"), 16 * 4 * NT)

        @block.gpsimd
        def _(pool):
            def sel(dst, pattern, base, mult, op=ALU.is_ge, fill=0.0):
                tick(nc.gpsimd.affine_select(out=dst, in_=dst, compare_op=op, fill=fill, base=base,
                                             pattern=pattern, channel_multiplier=mult), "pool_step")
                own(pool, "pool_step")

            tick(nc.gpsimd.memset(small[:, 66:67], 0.0), "pool_step")
            nc.gpsimd.memset(VPACK[:], 0.0).then_inc(S("vpack_zeroed"), 1)
            for j in range(4):
                v = RAW[:, j, 0:1536].rearrange("p (k n) -> p k n", k=4)
                ins = nc.gpsimd.memset(v[:, :, 288:384], 0.0)
            ins.then_inc(S("misc_zeroed"), 1)
            tick(nc.gpsimd.memset(ident[:], 0.0), "pool_step")
            tick(nc.gpsimd.memset(ones[:], 1.0), "pool_step")
            own(pool, "pool_step")
            nc.gpsimd.affine_select(out=ident[:], in_=ident[:], compare_op=ALU.not_equal, fill=1.0, base=0,
                                    pattern=[[-1, P]], channel_multiplier=1).then_inc(S("ident_made"), 1)
            for i, m in enumerate((2, 4, 8, 16, 32, 64)):
                tick(nc.gpsimd.memset(off[:, i, :], 1.0), "pool_step")
            tick(nc.gpsimd.memset(upper, 1.0), "pool_step")
            tick(nc.gpsimd.memset(upper_eq, 1.0), "pool_step")
            tick(nc.gpsimd.memset(lower1[:], 1.0), "pool_step")
            tick(nc.gpsimd.memset(chunk_go[:], 1.0), "pool_step")
            own(pool, "pool_step")
            tick(nc.gpsimd.memset(chunk_go[:].rearrange("p (c t) -> p c t", t=C)[:, :, 0:1], 0.0), "pool_step")
            for i, m in enumerate((2, 4, 8, 16, 32, 64)):
                sel(off[:, i, :], [[-m, P // m], [0, m]], 0, 1)
                sel(off[:, i, :], [[m, P // m], [0, m]], m - 1, -1)
            sel(upper, [[1, P]], -1, -1)
            sel(upper_eq, [[1, P]], 0, -1)
            sel(lower1[:], [[-1, P]], -1, 1)
            tick(nc.gpsimd.memset(small[:, 80:144], 0.0), "pool_step")
            tick(nc.gpsimd.memset(causal[:], 0.0), "pool_step")
            own(pool, "pool_step")
            tick(nc.gpsimd.memset(small[:, 95:96], 1.0), "pool_step")
            own(pool, "pool_step")
            tick(nc.gpsimd.memset(small[0:64, 126:127], 1.0), "pool_step")
            own(pool, "pool_step")
            tick(nc.gpsimd.memset(small[64:128, 127:128], 1.0), "pool_step")
            own(pool, "pool_step")
            sel(causal[:], [[-1, P]], 0, 1, fill=-1e30)
            pool.sem_inc(S("masks_made"), 1)
            pool.wait_ge(S("decay_exp"), 2)
            pool.wait_ge(S("rate_read"), 1)
            nc.gpsimd.tensor_tensor(BH[:], BH[:], ENG[:], ALU.mult).then_inc(S("rate_grown"), 1)
            pool.wait_ge(S("bonus_terms"), 1)
            pool.wait_ge(S("hr_bc_read"), 1)
            tick(nc.gpsimd.tensor_tensor(AR[:, :, 1, :], PR[:, T_R:T_R + PAIRS, PAD:TP], EG[:], ALU.mult), "pool_step")
            own(pool, "pool_step")
            tick(nc.gpsimd.memset(R1[:], 0.0), "pool_step")
            tick(nc.gpsimd.memset(UU[:], 0.0), "pool_step")
            own(pool, "pool_step")
            pool.sem_inc(S("r_hat_made"), 1)
            for n in range(NT):
                if n:
                    pool.wait_ge(S("inv_added"), 20)
                for b in range(4):
                    pool.wait_ge(S("lbr_out"), 8 * n + 2 * b + 2)
                    s4 = slice(4 * b, 4 * b + 4)
                    lt = LBR[:, s4, 0, :]

                    def each(m):
                        return m.unsqueeze(1).broadcast_to([P, 4, P])
                    tick(nc.gpsimd.tensor_tensor(TT[:, s4, :], lt, each(off[:, 0, :]), ALU.mult), "pool_step")
                    tick(nc.gpsimd.tensor_tensor(LO[:, s4, :], lt, each(off[:, 1, :]), ALU.mult), "pool_step")
                    own(pool, "pool_step")
                    nc.gpsimd.tensor_tensor(TT[:, s4, :], TT[:, s4, :], each(ident[:]), ALU.add)\
                        .then_inc(S("tt_started"), 1)
            for k, sq in ((1, NSQ), (2, NSQ_H), (4, NSQ)):
                pool.wait_ge(S("squared"), KT * k + 8)
                for n in (4, 2):
                    tick(nc.gpsimd.tensor_tensor(sq[:, 0:n, :], sq[:, 0:n, :], sq[:, n:2 * n, :], ALU.add), "pool_step")
                    own(pool, "pool_step")
                nc.gpsimd.tensor_tensor(sq[:, 0, :], sq[:, 0, :], sq[:, 1, :], ALU.add)\
                    .then_inc(S("squares_presummed"), 1)

        @block.scalar
        def _(act):
            A = nc.scalar.activation

            def hi(u_const, g=None, step=0):
                lv = 32 * (u_const // 4 + 1)
                uv = u_const - HI_SLOTS + 1 + FREE_UNITS
                if g is not None:
                    lv = g * (8 * step) + lv
                    uv = g * step + uv
                if g is None and u_const < 4:
                    act.wait_ge(landed[u_const], 48)
                else:
                    act.wait_ge(landed[u_const % 4], lv + 16)
                act.wait_ge(unit_used, uv)
                n = unit_cols(u_const)
                A(HIW[:, u_const % 2, 0:n], RAW[:, u_const % 4, 0:n], ACT.Copy).then_inc(hi_made, 1)

            def summed(n0, f, u_end, g=None, nf=8, step=8):
                if f < nf - 1:
                    v = n0 // 8 * 7 + f + 1
                    act.wait_ge(tile_summed, v if g is None else g * 7 + v)
                else:
                    v = u_end + FREE_UNITS
                    act.wait_ge(unit_used, v if g is None else g * step + v)

            def group_phase(u0, groups, evac=None, n0=0):
                def rest(g):
                    for j in range(2, UG):
                        hi(u0 + j, g, UG)
                    hi(u0 + UG, g, UG)
                    if evac:
                        evac(g)
                    hi(u0 + UG + 1, g, UG)
                with act.Fori(0, groups) as g:
                    rest(g)

            def squares(n0, half, dst=None):
                for f in range(8 * half, 8 * half + 8):
                    act.wait_ge(bank_freed, n0 + f + 1 + FREE_BANKS)
                    A((dst or NSQ)[:, f, :], X[:, f, :], ACT.Square).then_inc(S("squared"), 1)

            def root(k):
                act.wait_ge(S("variance"), k + 1)
                A(rstd[:], rstd[:], ACT.Sqrt).then_inc(S("rooted"), 1)

            def high_parts(k):
                for e in range(8):
                    act.wait_ge(S("h_full"), 8 * HN[k] + e + 1)
                    A(H[:, 0, 2 * e:2 * e + 2, :], NSQ[:, 2 * e:2 * e + 2, :], ACT.Copy).then_inc(S("h_hi"), 1)

            def out_phase(u0, n0, k):
                for g in range(2):
                    u = u0 + g * UG
                    for j in range(2, UG + 1):
                        hi(u + j)
                    squares(n0, g)
                    if g == 1:
                        root(k)
                    hi(u + UG + 1)
                high_parts(k)

            got = waiter(act)
            for dst, src in ((WA_UP[0:64, :], io["rwkv_w_up"][0]), (WA_UP[64:128, :], io["rwkv_a_up"][0]),
                             (G_UP[:, 0, :], io["rwkv_g_up"][0, 0:P, :]),
                             (G_UP[0:32, 1, :], io["rwkv_g_up"][0, P:160, :])):
                act.dma_start(dst, src).then_inc(S("loras_landed"), 16)
            act.wait_ge(S("vpack_zeroed"), 1)
            for dst, src in ((a_log, io["gdn_A_log"][0]), (dt_bias, io["gdn_dt_bias"][0]),
                             (fox_bias[16:32], io["fox_b_f_2"][0])):
                act.dma_start(dst, src.rearrange("(h a) -> h a", a=1)).then_inc(S("smalls_landed"), 16)
            for q in range(4):
                act.wait_ge(S("x_turned"), q + 1)
                A(X[:, 4 * q:4 * q + 4, 0:P], ps[q][:, :].rearrange("p (f t) -> p f t", f=4), ACT.Copy)\
                    .then_inc(S("x_tiles"), 1)
            act.wait_ge(S("x_tiles"), 8)
            for q in range(4):
                A(NSQ[:, 4 * q:4 * q + 4, :], X[:, 4 * q:4 * q + 4, :], ACT.Square).then_inc(S("squared"), 4)
            hi(0)
            root(0)
            hi(1)
            high_parts(0)
            hi(2)
            hi(3)
            hi(4)
            hi(5)
            group_phase(U_IN, 3)
            for g in (3, 4, 5):
                for j in range(2, UG + 2 if g < 5 else UG):
                    hi(U_IN + g * UG + j)
                    if (g, j) == (3, 6):
                        got("lowrank_shifted")
                        A(PR[0:64, T_WA, PAD:TP], PR[0:64, T_WA, PAD:TP], ACT.Tanh)
                        A(PR[0:32, T_G1, PAD:TP], PR[0:32, T_G1, PAD:TP], ACT.Sigmoid)
                        A(PR[:, T_G0, PAD:TP], PR[:, T_G0, PAD:TP], ACT.Sigmoid).then_inc(S("lowrank_ready"), 1)
                    if (g, j) == (5, 4):
                        got("kq_made")
                        A(KSQ[:], KQ[:], ACT.Square).then_inc(S("hr_sq"), 1)

            def head_root(buf=None):
                got("hr_var")
                r = rstd[0:16] if buf is None else buf
                A(r, r, ACT.Sqrt).then_inc(S("hr_root"), 1)

            for name, dst, bias in (("w_lora", EG, "rwkv_w0"), ("a_lora", BH, "rwkv_a0")):
                for t in range(PAIRS):
                    if t % 2 == 0:
                        got(name)
                    b = (0 if dst is EG else 4) + t // 2
                    c = COL[bias] + t
                    ins = A(dst[:, t, :], ps[b][:, (t % 2) * T:(t % 2 + 1) * T], ACT.Sigmoid, bias=vec[:, c:c + 1])
                ins.then_inc(S(f"{name}_sigmoid"), 1)
            head_root()
            got("decay_summed")
            A(EG[:], GS[:], ACT.Exp, scale=-DECAY_RATE).then_inc(S("decay_exp"), 1)
            A(ENG[:], GS[:], ACT.Exp, scale=DECAY_RATE).then_inc(S("decay_exp"), 1)

            def heads4(b):
                return ps[b][:, :].rearrange("p (h t) -> p h t", h=4)

            def inversion(PM, beside=None):
                for lev in range(1, 6):
                    for b in range(4):
                        got("inv_p")
                        A(PM[:, 4 * b:4 * b + 4, :], heads4(2 * b), ACT.Copy).then_inc(S("inv_pm"), 1)
                        if beside and (b == 3 or (b, lev) == (1, 5)):
                            beside(lev - 1 + (b // 3) * (lev // 5))

            def conv_step(i):
                q, k = i // 3, i % 3
                if k == 0 and 0 < q <= 4:
                    got("conv_made")
                    tick(A(QKVC[:, 4 * q - 4:4 * q, :], CV[:], ACT.Silu), "conv_act")
                if k == 0 and q < 4:
                    if q > 0:
                        own(act, "conv_act")
                    for f in range(4 * q, 4 * q + 4):
                        c = COL["gdn_conv_w"] + f
                        ins = A(CV[:, f % 4, :], PR[:, T_GQ + f, 1:1 + T], ACT.Copy, scale=vec[:, c:c + 1])
                    ins.then_inc(S("tap0"), 1)
                if i == 12:
                    A(PR[:, T_Z:T_Z + 8, PAD:TP], PR[:, T_Z:T_Z + 8, PAD:TP], ACT.Silu).then_inc(S("z_act"), 1)

            for n in range(NT):
                for i, dst in enumerate((VTOK, BTOK, KTOK)):
                    for hb in range(2):
                        got("tok_turned")
                        A(dst[:, 4 * hb:4 * hb + 4, :], heads4(2 * i + hb), ACT.Copy).then_inc(S("tok_made"), 1)
                inversion(PM, lambda i: conv_step(6 * n + i))
                for c in (2 * n, 2 * n + 1):
                    r = slice(C * (c % 2), C * (c % 2) + C)
                    for hb in range(2):
                        got("r1_summed")
                        A(R1[r, 4 * hb:4 * hb + 4, :], ps[4 * hb][r, :].rearrange("p (h t) -> p h t", h=4), ACT.Copy)\
                            .then_inc(S("r1_out"), 1)
                    for hb in range(2):
                        got("y_summed")
                        A(BH[:, 4 * hb:4 * hb + 4, c * C:c * C + C],
                          ps[2 + 4 * hb][:, 0:256].rearrange("p (h t) -> p h t", h=4), ACT.Copy)\
                            .then_inc(S("y_out"), 1)
            conv_step(12)
            own(act, "conv_act")
            A(QKSQ[:], QKVC[:, 0:8, :], ACT.Square).then_inc(S("hr_sq"), 1)
            head_root(RWK[0:16, 0, :])
            got("y_centred")
            A(RN[:], BH[:], ACT.Square).then_inc(S("hr_sq"), 1)
            got("smalls_landed", 48)
            A(a_log, a_log, ACT.Exp).then_inc(S("a_exp"), 1)
            got("rows_zeroed")
            A(ROWS[64:72, :], PR[64:72, T_G1, PAD:TP], ACT.Sigmoid).then_inc(S("beta_made"), 1)
            got("softplus_abs")
            A(RWK[32:40, 1, :], RWK[32:40, 1, :], ACT.Exp, scale=-1.0).then_inc(S("softplus_exp"), 1)
            got("softplus_plus1")
            A(RWK[32:40, 1, :], RWK[32:40, 1, :], ACT.Ln).then_inc(S("softplus_ln"), 1)
            head_root()
            got("ya_full")
            A(H[:, 0, 0:PAIRS, :], BH[:], ACT.Copy).then_inc(S("mix_hi"), 1)

            got("cols_made")
            A(g_exp, COLS[:, :, 32:40], ACT.Exp)
            A(k_left, COLS[:, :, 96:104], ACT.Exp).then_inc(S("cols_exp"), 1)
            for b in range(4):
                got("g_rows")
                A(QG[:, 2 * b:2 * b + 2, :], ps[b][:, :].rearrange("p (h t) -> p h t", h=2), ACT.Exp)\
                    .then_inc(S("g_rows_exp"), 1)
            got("beta_exp_made")
            for n in range(NT):
                n8 = slice(8 * n, 8 * n + 8)
                got("gam_diff")
                A(GAM[:, n8, :], GAM[:, n8, :], ACT.Exp).then_inc(S("gam_exp"), 1)
            for n in range(NT):
                got("tok_turned")
                for h in range(G_HEADS):
                    kt = ps[n][:, (h // 2) * P:(h // 2 + 1) * P]
                    A(KBE[:, 8 * n + h, :], kt, ACT.Copy, scale=beta_exp[:, n, h:h + 1])
                    A(KG[:, 8 * n + h, :], kt, ACT.Copy, scale=k_left[:, n, h:h + 1])
                got("tok_turned")
                for h in range(G_HEADS):
                    vt = ps[2 + 2 * n + h // 4][:, (h % 4) * P:(h % 4 + 1) * P]
                    ins = A(VB[:, 8 * n + h, :], vt, ACT.Copy, scale=COLS[:, n, 64 + h:65 + h])
                ins.then_inc(S("gtok_made"), 1)
            inversion(gPM)
            for b in range(4):
                got("u0_summed")
                A(U0[:, 4 * b:4 * b + 4, :], heads4(b), ACT.Copy).then_inc(S("u0_out"), 1)
            for c in range(NCH):
                for hb in range(2):
                    got("o_summed")
                    A(OG[:, 4 * hb:4 * hb + 4, c * C:(c + 1) * C],
                      ps[4 + hb][:, 0:256].rearrange("p (h t) -> p h t", h=4), ACT.Copy).then_inc(S("o_out"), 1)
            got("o_out", 2 * NCH)
            A(GSQ[:], OG[:], ACT.Square).then_inc(S("hr_sq"), 1)
            head_root()
            hi(U_OUT)
            hi(U_OUT + 1)
            got("yb_full")
            A(H[:, 0, PAIRS:KT, :], OG[:], ACT.Copy).then_inc(S("mix_hi"), 1)

            def ffn_phase(u0, evac, tail):
                for j in range(2, UG):
                    hi(u0 + j)
                with act.Fori(0, 10) as g:
                    hi(u0 + UG, g, UG)
                    evac(g)
                    for j in range(1, UG):
                        hi(u0 + UG + j, g, UG)
                        tail(g, j)
                hi(u0 + 11 * UG)
                evac(10)
                for j in range(1, UG):
                    if j < 6:
                        hi(u0 + 11 * UG + j)
                    tail(10, j)

            def down(u0, n0=None, last=False):
                for half in range(2):
                    b = u0 + half * (FT // 2)
                    done = 2 if half else 6
                    with act.Fori(0, (22 - done) // 4) as i:
                        for j in range(4):
                            hi(b + done + j, i, 4)
                    if last and half:
                        return
                    hi(b + 22)
                    if not last:
                        squares(n0, half, NSQ_H)
                    if half and not last:
                        root(2)
                    hi(b + 23)

            def evac_ffn1(g):
                for i in range(4):
                    act.wait_ge(tile_summed, g * 7 + (M_FFN1 + 2 * i + 1))
                    A(SG[:, i, :], ps[2 * i][:, 0:T], ACT.Silu).then_inc(S("gate_act"), 1)

            def tail_ffn1(g, j):
                if j == 1:
                    act.wait_ge(bank_freed, g * 8 + (N_FFN1 + 8 + FREE_BANKS))
                    A(HID[:, 0, bass.ds(g * 4, 4), :], HS[:], ACT.Copy).then_inc(S("hid_hi"), 1)

            out_phase(U_OUT, N_OUT, 1)
            ffn_phase(U_FFN1, evac_ffn1, tail_ffn1)
            down(U_DOWN1, N_DOWN1)
            for f in range(KT):
                act.wait_ge(S("x_scaled"), f + 1)
                A(NSQ[:, f, :], X[:, f, :], ACT.Square).then_inc(S("squared"), 1)
            root(3)
            high_parts(3)
            hi(U_MISC2 + 2)
            hi(U_MISC2 + 3)
            hi(U_FOX)
            hi(U_FOX + 1)
            group_phase(U_FOX, 4)
            for g in (4, 5):
                for j in range(2, UG + 2):
                    hi(U_FOX + g * UG + j)
                    if (g, j) == (4, 3):
                        got("softplus_abs")
                        A(FW[f_in, 1, :], FW[f_in, 1, :], ACT.Exp, scale=-1.0).then_inc(S("softplus_exp"), 1)
                    if (g, j) == (4, 5):
                        got("softplus_plus1")
                        A(FW[f_in, 1, :], FW[f_in, 1, :], ACT.Ln).then_inc(S("softplus_ln"), 1)
                    if g == 5 and j < UG:
                        sets = (0, 2, 4, 5, 6, 7, 8)
                        for q in range(sets[j - 2], sets[j - 1]):
                            if q == 0:
                                act.wait_ge(bank_freed, N_FOX + 32 + FREE_BANKS)
                            ins = A(ASQ[:, 4 * q:4 * q + 4, :], QKV[:, 4 * q:4 * q + 4, :], ACT.Square)
                            if q == 7:
                                ins.then_inc(S("hr_sq"), 1)

            got("hr_var")
            A(FW[0:16, 0:2, :], FW[0:16, 0:2, :], ACT.Sqrt).then_inc(S("hr_root"), 1)
            for i in range(8):
                got("turned_a")
                A(VT[:, i // 4, (i % 4) * 512:(i % 4 + 1) * 512], ps[1 + (8 + i) % 7][:, :], ACT.Copy)\
                    .then_inc(S("vt_made"), 1)
            for h in range(A_HEADS + 2):
                z = h % 2
                if h < A_HEADS:
                    for n, c0, w in ((0, 0, P), (1, P, T)):
                        got("score_max")
                        A(SC[:, h % 3, c0:c0 + w], SC[:, h % 3, c0:c0 + w], ACT.Exp, bias=AST[:, h % 3, n:n + 1],
                          accum_out=AST[:, h % 3, 2 + n:3 + n]).then_inc(S("prob_made"), 1)
                if 0 < h <= A_HEADS:
                    got("pt_turned")
                    A(PT[:, 1 - z, :], ps[3 - z][:, 0:384], ACT.Copy).then_inc(S("pt_made"), 1)
                if h > 1:
                    got("att_summed")
                    A(H[:, 0, h - 2, :], ps[4 + z][:, 0:T], ACT.Copy).then_inc(S("att_hi"), 1)
            out_phase(U_OUT2, N_OUT2, 4)

            def evac_ffn2(g):
                for i in range(GROUP):
                    if i < GROUP - 1:
                        act.wait_ge(tile_summed, g * 7 + (M_FFN2 + i + 1))
                    else:
                        act.wait_ge(unit_used, g * UG + (U_FFN2 + UG + FREE_UNITS))
                    if i == 0:
                        act.wait_ge(S("hid_made"), g + 12)
                    A(UC[:, i, 2:2 + T], ps[i][:, 0:T], ACT.Copy).then_inc(bank_freed, 1)

            def tail_ffn2(g, j):
                if j == 3:
                    act.wait_ge(S("conv_step"), g * 3 + 3)
                    A(YG[:], YG[:], ACT.Silu).then_inc(S("conv_gate"), 1)
                elif j == 5:
                    act.wait_ge(S("hid_full"), g + 1)
                    A(HID[:, 0, bass.ds(g * 4, 4), :], YV[:], ACT.Copy).then_inc(S("hid_hi"), 1)
            ffn_phase(U_FFN2, evac_ffn2, tail_ffn2)
            down(U_DOWN2, last=True)
            for q in range(4):
                got("turned_a")
                A(OUTT[:, 0, q * 512:(q + 1) * 512], ps[q][:, :], ACT.Copy).then_inc(S("y_tokens_0"), 1)

        @block.vector
        def _(dve):
            V = nc.vector

            def step(ins):
                tick(ins, "dve_step")

            def settle():
                own(dve, "dve_step")

            def lo(u_const, g=None, stepu=0):
                v = u_const + 1
                dve.wait_ge(hi_made, v if g is None else g * stepu + v)
                n = unit_cols(u_const)
                V.tensor_tensor(LOW[:, u_const % 4, 0:n], RAW[:, u_const % 4, 0:n],
                                HIW[:, u_const % 2, 0:n].bitcast(F32), ALU.subtract).then_inc(lo_made, 1)

            def summed(n7, f, u_end, g=None, nf=8, stepu=UG):
                if f < nf - 1:
                    v = n7 + f + 1
                    dve.wait_ge(tile_summed, v if g is None else g * 7 + v)
                else:
                    v = u_end + FREE_UNITS
                    dve.wait_ge(unit_used, v if g is None else g * stepu + v)

            def group_phase(u0, groups, evac):
                with dve.Fori(0, groups) as g:
                    for j in range(2, UG):
                        lo(u0 + j, g, UG)
                    lo(u0 + UG, g, UG)
                    evac(g)
                    lo(u0 + UG + 1, g, UG)

            def inverse_root(k, eps):
                dve.wait_ge(S("squares_summed"), k + 1)
                V.tensor_scalar(rstd[:], ps[0][:, 0:T], 1.0 / D, eps, ALU.mult, ALU.add)\
                    .then_inc(S("variance"), 1)
                dve.wait_ge(S("rooted"), k + 1)
                step(V.reciprocal(rstd[:], rstd[:]))
                settle()

            def norm(k, gain, eps, between=None):
                inverse_root(k, eps)
                c = COL[gain]
                for e in range(9):
                    if e < 8:
                        for f in (2 * e, 2 * e + 1):
                            ins = V.scalar_tensor_tensor(NSQ[:, f, :], X[:, f, :], vec[:, c + f:c + f + 1], rstd[:],
                                                         ALU.mult, ALU.mult)
                        ins.then_inc(S("h_full"), 1)
                    if e == 2 and between:
                        between()
                    if e > 0:
                        dve.wait_ge(S("h_hi"), 8 * HN[k] + e)
                        s = slice(2 * e - 2, 2 * e)
                        V.tensor_tensor(H[:, 1, s, :], NSQ[:, s, :], H[:, 0, s, :].bitcast(F32), ALU.subtract)\
                            .then_inc(S("h_made"), 1)

            for q in range(4):
                dve.wait_ge(S("x_turned"), 5 + q)
                V.tensor_copy(X[:, 4 * q:4 * q + 4, P:T], ps[4 + q][:, :].rearrange("p (f t) -> p f t", f=4))\
                    .then_inc(S("x_tiles"), 1)
            c0 = 0
            for i, pack in enumerate(PACKS):
                r = sum(n for _, n in pack)
                dve.wait_ge(S("vecs_turned"), i + 1)
                V.tensor_copy(vec[:, c0:c0 + r], ps[i % 4][:, (i // 4) * P:(i // 4) * P + r])\
                    .then_inc(S("vecs_made"), 1)
                c0 += r
            dve.wait_ge(S("vecs_made"), len(PACKS))
            dve.sem_inc(bank_freed, FREE_BANKS)
            lo(0)
            norm(0, "attn_norm_w", 1e-5, between=lambda: lo(1))
            dve.wait_ge(S("h_made"), 8)
            step(V.memset(PR[:, :, 0:PAD], 0.0))
            lo(2)
            lo(3)
            lo(4)
            for f in range(3):
                summed(0, f, U_IN, nf=3)
                V.tensor_copy(PR[:, f, PAD:TP], ps[f][:, 0:T]).then_inc(bank_freed, 6 if f == 2 else 1)
            lo(5)
            dve.wait_ge(S("masks_made"), 1)
            step(V.tensor_tensor(upper, upper, off[:, 5, :], ALU.mult))
            step(V.tensor_tensor(upper_eq, upper_eq, off[:, 5, :], ALU.mult))
            step(V.tensor_tensor(lower1[:], lower1[:], off[:, 0, :], ALU.mult))
            step(V.tensor_copy(headones[:], off[:, 5, :]))
            settle()
            for i in range(5, -1, -1):
                inner = off[:, i - 1, :] if i else ident[:]
                step(V.tensor_tensor(off[:, i, :], off[:, i, :], inner, ALU.subtract))
                settle()
                step(V.tensor_tensor(off[:, i, :], off[:, i, :], upper, ALU.mult))
            settle()

            def evac_in(g):
                for f in range(GROUP):
                    summed(2, f, U_IN + UG, g)
                    V.tensor_copy(PR[:, bass.ds(g * 8 + (3 + f), 1), PAD:TP], ps[f][:, 0:T])\
                        .then_inc(bank_freed, 1)
            group_phase(U_IN, 3, evac_in)

            got = waiter(dve)
            mu_col = {T_WA: 24, T_G0: 25, T_G1: 26}
            shifted = [[T_WA, T_G0, T_G1]] + [[t, t + 1] for t0 in (T_K, T_V, T_R) for t in range(t0, t0 + PAIRS, 2)]

            def shift_step(i):
                if i > 0:
                    settle()
                    for e, f in enumerate(shifted[i - 1]):
                        c = COL["rwkv_mu"] + mu_col.get(f, f - 3)
                        ins = V.scalar_tensor_tensor(PR[:, f, PAD:TP], SHIFT[:, (i - 1) % 2, e, :], vec[:, c:c + 1],
                                                     PR[:, f, PAD:TP], ALU.mult, ALU.add)
                    if i == 1:
                        ins.then_inc(S("lowrank_shifted"), 1)
                    else:
                        step(ins)
                if i < len(shifted):
                    for e, f in enumerate(shifted[i]):
                        ins = V.tensor_tensor(SHIFT[:, i % 2, e, :], PR[:, f, PAD - 1:TP - 1], PR[:, f, PAD:TP],
                                              ALU.subtract)
                    step(ins)

            Rf, Kf, Vf = (PR[:, t:t + PAIRS, PAD:TP] for t in (T_R, T_K, T_V))

            def kq_step(t):
                c = COL["rwkv_k_k"] + t
                ins = V.tensor_scalar(KQ[:, t, :], Kf[:, t, :], vec[:, c:c + 1], None, ALU.mult)
                if t == PAIRS - 1:
                    ins.then_inc(S("kq_made"), 1)
            dve.wait_ge(bank_freed, N_IN + 24 + FREE_BANKS)
            slot = 0
            for g in (3, 4, 5):
                for j in range(2, UG + 2 if g < 5 else UG):
                    lo(U_IN + g * UG + j)
                    if j == UG:
                        evac_in(g)
                        continue
                    if slot <= len(shifted):
                        shift_step(slot)
                    if 6 <= slot < 6 + PAIRS:
                        kq_step(slot - 6)
                    slot += 1
            evac_in(5)

            def head_rsqrt(scale, eps, meanwhile=None, buf=None, b=0):
                r = rstd[0:16] if buf is None else buf
                got("hr_sum")
                V.tensor_scalar(r, ps[b][0:16, 0:T], scale, eps, ALU.mult, ALU.add).then_inc(S("hr_var"), 1)
                if meanwhile:
                    meanwhile()
                got("hr_root")
                V.reciprocal(r, r).then_inc(S("hr_inv"), 1)

            def pair_of(b):
                return ps[b][:, :].rearrange("p (a t) -> p a t", a=2)

            got("w_lora_sigmoid")
            for t in range(PAIRS):
                ins = V.tensor_tensor_scan(GS[:, t, :], chunk_go[:], EG[:, t, :], 0.0, ALU.mult, ALU.add)
            ins.then_inc(S("decay_summed"), 1)

            def rates():
                got("a_lora_sigmoid")
                for t in range(PAIRS):
                    c = COL["rwkv_k_a"] + t
                    ins = V.tensor_scalar(TMP[:, t, :], BH[:, t, :], 1.0, vec[:, c:c + 1], ALU.subtract, ALU.mult)
                ins.then_inc(S("rate_read"), 1)
                got("rate_read")
                step(V.scalar_tensor_tensor(Kf, TMP[:], 1.0, Kf, ALU.add, ALU.mult))
                settle()
            head_rsqrt(1.0, 1e-12, rates)
            for t in range(PAIRS):
                c = COL["rwkv_r_k"] + t
                ins = V.scalar_tensor_tensor(TMP[:, t, :], Rf[:, t, :], vec[:, c:c + 1], Kf[:, t, :],
                                             ALU.mult, ALU.mult)
            ins.then_inc(S("bonus_terms"), 1)
            got("bonus_terms")
            for q in range(4):
                got("hr_bc")
                ins = V.tensor_tensor(KK[:, 2 * q:2 * q + 2, :], KQ[:, 2 * q:2 * q + 2, :], pair_of(q), ALU.mult)
                if q < 3:
                    step(ins)
                else:
                    ins.then_inc(S("hr_bc_read"), 1)
            got("hr_bc_read")
            got("decay_exp", 2)
            step(V.tensor_copy(small[:, 0:32], EG[:].rearrange("p t (c j) -> p (t c) j", j=C)[:, :, C - 1]))
            step(V.tensor_tensor(Kf, Kf, ENG[:], ALU.mult))
            settle()
            got("rate_grown")
            step(V.tensor_tensor(BH[:], BH[:], KK[:], ALU.mult))
            for t in range(PAIRS):
                a_t = AR[:, t, 0, :].rearrange("p (c j) -> p c j", j=C)
                kk_t = KK[:, t, :].rearrange("p (c j) -> p c j", j=C)
                eg_t = EG[:, t, :].rearrange("p (c j) -> p c j", j=C)
                V.scalar_tensor_tensor(a_t[:, :, 1:C], kk_t[:, :, 1:C], -1.0, eg_t[:, :, 0:C - 1], ALU.mult, ALU.mult)
                ins = V.tensor_scalar(a_t[:, :, 0:1], kk_t[:, :, 0:1], -1.0, None, ALU.mult)
            step(ins)
            settle()
            dve.sem_inc(S("hats_made"), 1)
            for q in range(4):
                got("heads_summed")
                V.tensor_tensor(BON[:, 2 * q:2 * q + 2, :], pair_of(4 + q), Vf[:, 2 * q:2 * q + 2, :], ALU.mult)\
                    .then_inc(S("bonus_out"), 1)

            def bank(b):
                return ps[b][:, :].rearrange("p (h t) -> p h t", h=4)

            def many(m, n):
                return m.unsqueeze(1).broadcast_to([P, n, m.shape[-1]])

            def inv_off(lev, b, lt, LO):
                V.tensor_tensor(LO[:, 4 * b:4 * b + 4, :], lt(b), many(off[:, lev, :], 4), ALU.mult)\
                    .then_inc(S("inv_off"), 1)

            def inversion(lt, LO, TM, TT, beside=None):
                for lev in range(1, 6):
                    for b in range(4):
                        s4 = slice(4 * b, 4 * b + 4)
                        got("inv_t")
                        if lev < 5:
                            V.tensor_tensor(TM[:, s4, :], TM[:, s4, :], bank(2 * b), ALU.add)
                        V.tensor_tensor(TT[:, s4, :], TT[:, s4, :], bank(2 * b + 1), ALU.add)\
                            .then_inc(S("inv_added"), 1)
                        if lev < 5:
                            inv_off(lev + 1, b, lt, LO)
                        if beside and (b == 3 or (b, lev) == (1, 5)):
                            beside(lev - 1 + (b // 3) * (lev // 5))

            def conv_step(i):
                q, tap = i // 3, i % 3 + 1
                if q > 3:
                    return
                if tap == 1:
                    got("tap0")
                else:
                    settle()
                for f in range(4 * q, 4 * q + 4):
                    c = COL["gdn_conv_w"] + 16 * tap + f
                    ins = V.scalar_tensor_tensor(CV[:, f % 4, :], PR[:, T_GQ + f, 1 + tap:1 + tap + T],
                                                 vec[:, c:c + 1], CV[:, f % 4, :], ALU.mult, ALU.add)
                if tap == 3:
                    ins.then_inc(S("conv_made"), 1)
                else:
                    step(ins)

            step(V.memset(ST[:, 0], 0.0))
            for n in range(NT):
                def l_evac(M, fill):
                    for q in range(8):
                        got("l_summed")
                        dst = M[:, 2 * q:2 * q + 2, :, :].rearrange("p h a t -> p h (a t)")
                        src = ps[(fill + q) % 8][:, :].rearrange("p (h t) -> p h t", h=2)
                        V.tensor_tensor(dst, src, many(upper2[:].rearrange("p a t -> p (a t)"), 2), ALU.mult)\
                            .then_inc(S("lbr_out" if M is LBR else "lkr_out"), 1)
                l_evac(LBR, 6)
                for b in range(4):
                    s4 = slice(4 * b, 4 * b + 4)
                    got("l_plain")
                    tick(V.tensor_tensor(TM[:, s4, :], bank((14 + b) % 8), many(lower1[:], 4), ALU.mult), "l_out")
                    own(dve, "l_out")
                    V.tensor_tensor(TM[:, s4, :], TM[:, s4, :], many(ident[:], 4), ALU.add)
                l_evac(LKR, 18)
                inversion(lambda b: LBR[:, 4 * b:4 * b + 4, 0, :], LO, TM, TT, lambda i: conv_step(6 * n + i))
                for c in (2 * n, 2 * n + 1):
                    r = slice(C * (c % 2), C * (c % 2) + C)
                    for hb in range(2):
                        h4 = slice(4 * hb, 4 * hb + 4)
                        got("u_summed")
                        V.tensor_copy(UU[r, h4, :], ps[1 + 4 * hb][r, :].rearrange("p (h t) -> p h t", h=4))\
                            .then_inc(S("u_out"), 1)
                    for hb in range(2):
                        h4 = slice(4 * hb, 4 * hb + 4)
                        before, after = ST[:, c % 2, h4, :], ST[:, (c + 1) % 2, h4, :]
                        got("s_summed")
                        step(V.tensor_tensor(PM[:, h4, :], bank(3 + 4 * hb), many(headones[:], 4), ALU.mult))
                        settle()
                        step(V.tensor_tensor(after, before, PM[:, h4, :], ALU.add))
                        settle()
                        dc = rdecay.rearrange("p (t c) -> p t c", c=NCH)[:, h4, c:c + 1]
                        tick(V.tensor_tensor(after, after, dc.broadcast_to([P, 4, P]), ALU.mult), "s_out")
                    own(dve, "s_out")
            g32 = slice(32, 40)

            def centre():
                for q in range(4):
                    got("heads_summed")
                    if q == 0:
                        dve.wait_ge(S("y_out"), 8)
                    b2 = BH[:, 2 * q:2 * q + 2, :]
                    ins = V.scalar_tensor_tensor(b2, pair_of(q), -1.0 / R_HEAD, b2, ALU.mult, ALU.add)
                ins.then_inc(S("y_centred"), 1)
                settle()
                step(V.memset(ROWS[:], 0.0))
                settle()
                dve.sem_inc(S("rows_zeroed"), 1)
                dve.wait_ge(S("smalls_landed"), 48)
                step(V.tensor_scalar(RWK[g32, 0, :], PR[g32, T_G1, PAD:TP], dt_bias, None, ALU.add))
                settle()
                step(V.tensor_scalar(RWK[g32, 1, :], RWK[g32, 0, :], -1.0, None, ALU.mult))
                settle()
                step(V.tensor_tensor(RWK[g32, 1, :], RWK[g32, 1, :], RWK[g32, 0, :], ALU.max))
                settle()
                dve.sem_inc(S("softplus_abs"), 1)
                step(V.tensor_scalar(RWK[g32, 0, :], RWK[g32, 0, :], 0.0, None, ALU.max))

            def gates():
                got("softplus_ln")
                step(V.tensor_tensor(RWK[g32, 0, :], RWK[g32, 0, :], RWK[g32, 1, :], ALU.add))
                settle()
                got("a_exp")
                step(V.tensor_scalar(RWK[g32, 0, :], RWK[g32, 0, :], a_log, -1.0, ALU.mult, ALU.mult))
                settle()
                step(V.tensor_tensor_scan(ROWS[g32, :], chunk_go[g32, :], RWK[g32, 0, :], 0.0, ALU.mult, ALU.add))
                settle()
                gc = ROWS[g32, :].rearrange("p (c j) -> p c j", j=C)
                V.tensor_tensor(ROWS[96:104, :].rearrange("p (c j) -> p c j", j=C),
                                gc[:, :, C - 1:C].broadcast_to([8, NCH, C]), gc, ALU.subtract).then_inc(S("rows_made"), 1)
            head_rsqrt(1.0, 1e-6, centre, RWK[0:16, 0, :], 4)
            for q in range(4):
                got("hr_bc")
                s2 = QKVC[:, 2 * q:2 * q + 2, :]
                if q < 2:
                    ins = V.scalar_tensor_tensor(s2, s2, float(P) ** -0.5, pair_of(4 + q), ALU.mult, ALU.mult)
                else:
                    ins = V.tensor_tensor(s2, s2, pair_of(4 + q), ALU.mult)
            ins.then_inc(S("gqk_normed"), 1)
            got("softplus_exp")
            V.tensor_scalar(RWK[g32, 1, :], RWK[g32, 1, :], 1.0, None, ALU.add).then_inc(S("softplus_plus1"), 1)
            head_rsqrt(1.0 / R_HEAD, R_HEAD * 1e-5, gates)
            for q in range(4):
                got("hr_bc")
                step(V.tensor_tensor(BH[:, 2 * q:2 * q + 2, :], BH[:, 2 * q:2 * q + 2, :], pair_of(q), ALU.mult))
            settle()
            dve.sem_inc(S("y_normed"), 1)
            for t in range(PAIRS):
                cw, cb = COL["rwkv_ln_w"] + t, COL["rwkv_ln_b"] + t
                ins = V.tensor_scalar(BH[:, t, :], BH[:, t, :], vec[:, cw:cw + 1], vec[:, cb:cb + 1],
                                      ALU.mult, ALU.add)
            step(ins)
            settle()
            step(V.tensor_tensor(BH[:], BH[:], BON[:], ALU.add))
            settle()
            for q in range(4):
                got("heads_summed")
                b2 = BH[:, 2 * q:2 * q + 2, :]
                ins = V.tensor_tensor(b2, b2, ps[q][:, :].rearrange("p (a t) -> p a t", a=2), ALU.mult)
            ins.then_inc(S("ya_full"), 1)

            got("mix_hi")
            V.tensor_tensor(H[:, 1, 0:PAIRS, :], BH[:], H[:, 0, 0:PAIRS, :].bitcast(F32), ALU.subtract)\
                .then_inc(S("mix_made"), 1)
            got("cols_turned")
            V.tensor_copy(COLS[:], ps[4][:, 0:T].rearrange("p (n t) -> p n t", n=NT)).then_inc(S("cols_made"), 1)
            got("cols_exp")
            V.tensor_tensor(beta_exp, g_exp, COLS[:, :, 64:72], ALU.mult).then_inc(S("beta_exp_made"), 1)
            got("g_rows_exp", 4)
            got("gqk_normed")
            step(V.tensor_copy(gdecay, QG[:].rearrange("p h (c j) -> p (h c) j", j=C)[:, :, C - 1]))
            settle()
            step(V.tensor_tensor(QG[:].rearrange("p (a b) t -> p a b t", b=2),
                                 QC.unsqueeze(2).broadcast_to([P, 4, 2, T]),
                                 QG[:].rearrange("p (a b) t -> p a b t", b=2), ALU.mult))
            step(V.memset(gS[0][:], 0.0))
            step(V.memset(VN[:], 0.0))
            settle()
            for n in range(NT):
                for h in range(G_HEADS):
                    ins = V.tensor_scalar(GAM[:, 8 * n + h, :],
                                          ps[h // 2][:, (h % 2) * T + n * P:(h % 2) * T + n * P + P],
                                          COLS[:, n, 32 + h:33 + h], 0.0, ALU.subtract, ALU.min)
                ins.then_inc(S("gam_diff"), 1)
            for b in range(4):
                got("beta_rows")
                V.scalar_tensor_tensor(gPM[:, 4 * b:4 * b + 4, :], bank(4 + b), -1.0, many(upper, 4),
                                       ALU.mult, ALU.mult).then_inc(S("beta_rows_out"), 1)
            got("beta_rows_out", 4)

            def twice(b):
                return ps[b][:, :].rearrange("p (a t) -> p a t", a=4).unsqueeze(2).broadcast_to([P, 4, 2, P])

            def two_by_two(x):
                return x.rearrange("p (a b) t -> p a b t", b=2)
            for n in range(NT):
                n8 = slice(8 * n, 8 * n + 8)
                got("gam_exp")
                step(V.tensor_tensor(GAM[:, n8, :], GAM[:, n8, :], many(upper_eq, 8), ALU.mult))
                settle()
                got("gkk_summed")
                g4 = two_by_two(GAM[:, n8, :])
                step(V.tensor_tensor(two_by_two(gLT[:, n8, :]), g4, twice(4 + 2 * n), ALU.mult))
                V.tensor_tensor(two_by_two(AT[:, n8, :]), g4, twice(5 + 2 * n), ALU.mult).then_inc(S("gkk_out"), 1)
                settle()
                step(V.tensor_tensor(gLT[:, n8, :], gLT[:, n8, :], gPM[:, n8, :], ALU.mult))
                settle()
                step(V.tensor_tensor(gTT[:, n8, :], gLT[:, n8, :], many(off[:, 0, :], 8), ALU.mult))
                settle()
                V.tensor_tensor(gTT[:, n8, :], gTT[:, n8, :], many(ident[:], 8), ALU.add).then_inc(S("gtt_start"), 1)
            got("gtt_start", 2)
            for b in range(4):
                got("gtm_turned")
                V.tensor_copy(gTM[:, 4 * b:4 * b + 4, :], bank((0, 2, 6, 7)[b]))
                inv_off(1, b, lambda b: gLT[:, 4 * b:4 * b + 4, :], gLO)
            inversion(lambda b: gLT[:, 4 * b:4 * b + 4, :], gLO, gTM, gTT)
            for b in range(4):
                got("wt_summed")
                V.tensor_copy(WT[:, 4 * b:4 * b + 4, :], bank(4 + b)).then_inc(S("wt_out"), 1)
            got("u0_out", 4)
            for c in range(NCH):
                n, r = c // 2, slice(C * (c % 2), C * (c % 2) + C)
                for hb in range(2):
                    got("ws_summed")
                    V.tensor_tensor(VN[r, 4 * hb:4 * hb + 4, :], U0[r, 8 * n + 4 * hb:8 * n + 4 * hb + 4, :],
                                    ps[hb][r, :].rearrange("p (h t) -> p h t", h=4), ALU.subtract)\
                        .then_inc(S("vn_made"), 1)
                for hb in range(2):
                    got("gs_summed")
                    for i in range(4):
                        h = 4 * hb + i
                        k = 4 * h + c
                        ins = V.scalar_tensor_tensor(gS[(c + 1) % 2][:, h, :], gS[c % 2][:, h, :], gdecay[:, k:k + 1],
                                                     ps[2 + hb][:, i * P:(i + 1) * P], ALU.mult, ALU.add)
                    ins.then_inc(S("gs_out"), 1)
                got("gs_out", 2)
            head_rsqrt(1.0 / P, 1e-6)
            got("z_act")
            for q in range(4):
                got("hr_bc")
                s2 = slice(2 * q, 2 * q + 2)
                step(V.tensor_tensor(OG[:, s2, :], OG[:, s2, :], pair_of(q), ALU.mult))
            settle()
            c = COL["gdn_norm_w"]
            V.scalar_tensor_tensor(OG[:], OG[:], vec[:, c:c + 1], PR[:, T_Z:T_Z + 8, PAD:TP], ALU.mult, ALU.mult)\
                .then_inc(S("yb_full"), 1)
            lo(U_OUT)
            got("mix_hi")
            V.tensor_tensor(H[:, 1, PAIRS:KT, :], OG[:], H[:, 0, PAIRS:KT, :].bitcast(F32), ALU.subtract)\
                .then_inc(S("mix_made"), 1)

            def residual(m0, u_end, half):
                for f in range(GROUP):
                    summed(m0, f, u_end)
                    x = X[:, half * 8 + f, :]
                    V.tensor_tensor(x, x, ps[f][:, 0:T], ALU.add).then_inc(bank_freed, 1)

            def out_phase(u0, n0, m0, norm_args):
                for g in range(2):
                    u = u0 + g * UG
                    for j in range(2, UG + 1):
                        lo(u + j)
                    residual(m0 + 7 * g, u + UG, g)
                    if g == 0:
                        lo(u + UG + 1)
                dve.wait_ge(bank_freed, n0 + 16 + FREE_BANKS)
                norm(*norm_args, between=lambda: lo(u0 + 2 * UG + 1))

            def down(u0, m0, last=False):
                for half in range(2):
                    b = u0 + half * (FT // 2)
                    done = 2 if half else 6
                    with dve.Fori(0, (22 - done) // 4) as i:
                        for j in range(4):
                            lo(b + done + j, i, 4)
                    if not (last and half):
                        lo(b + 22)
                    residual(m0 + 7 * half, b + 22, half)
                    if not half:
                        lo(b + 23)

            lo(U_OUT + 1)
            out_phase(U_OUT, N_OUT, M_OUT, (1, "ffn_norm_w", 1e-5))
            dve.sem_inc(S("hid_made"), 1)

            def ffn_phase(u0, evac, tail):
                for j in range(2, UG):
                    lo(u0 + j)
                with dve.Fori(0, 10) as g:
                    lo(u0 + UG, g, UG)
                    evac(g)
                    for j in range(1, UG):
                        lo(u0 + UG + j, g, UG)
                        tail(g, j)
                lo(u0 + 11 * UG)
                evac(10)
                for j in range(1, UG):
                    if j < 6:
                        lo(u0 + 11 * UG + j)
                    tail(10, j)

            def evac_ffn1(g):
                for i in range(4):
                    dve.wait_ge(S("gate_act"), g * 4 + (i + 1))
                    if i == 0:
                        dve.wait_ge(S("hid_made"), g + 1)
                    summed(M_FFN1, 2 * i + 1, U_FFN1 + UG, g)
                    V.tensor_tensor(HS[:, i, :], SG[:, i, :], ps[2 * i + 1][:, 0:T], ALU.mult).then_inc(bank_freed, 2)

            def tail_ffn1(g, j):
                if j == 1:
                    dve.wait_ge(S("hid_hi"), g + 1)
                    V.tensor_tensor(HID[:, 1, bass.ds(g * 4, 4), :], HS[:],
                                    HID[:, 0, bass.ds(g * 4, 4), :].bitcast(F32), ALU.subtract)\
                        .then_inc(S("hid_made"), 1)
            ffn_phase(U_FFN1, evac_ffn1, tail_ffn1)
            down(U_DOWN1, M_DOWN1)
            dve.wait_ge(bank_freed, N_MISC2 + FREE_BANKS)
            inverse_root(2, 1e-5)
            c = COL["final_norm_w"]
            for f in range(KT):
                V.scalar_tensor_tensor(X[:, f, :], X[:, f, :], vec[:, c + f:c + f + 1], rstd[:], ALU.mult, ALU.mult)\
                    .then_inc(S("x_scaled"), 1)
            lo(U_MISC2 + 1)
            dve.wait_ge(S("x_scaled"), KT)
            norm(3, "mix_norm_2", 1e-6)
            lo(U_MISC2 + 2)
            lo(U_MISC2 + 3)
            lo(U_FOX)
            dve.wait_ge(unit_used, U_FOX + FREE_UNITS)
            V.tensor_copy(FM[:], ps[0][:, 0:T]).then_inc(bank_freed, 8)
            lo(U_FOX + 1)

            def evac_fox(g):
                for f in range(GROUP):
                    summed(M_FOX, f, U_FOX + UG, g)
                    V.tensor_copy(QKV[:, bass.ds(g * 8 + f, 1), :], ps[f][:, 0:T]).then_inc(bank_freed, 1)
            group_phase(U_FOX, 4, evac_fox)
            for g in (4, 5):
                for j in range(2, UG + 2):
                    lo(U_FOX + g * UG + j)
                    if j == UG:
                        evac_fox(g)
                    if (g, j) == (4, 2):
                        step(V.tensor_scalar(FW[f_in, 0, :], FM[f_in, :], fox_bias, -1.0, ALU.add, ALU.mult))
                        settle()
                        step(V.tensor_scalar(FW[f_in, 1, :], FW[f_in, 0, :], -1.0, None, ALU.mult))
                        settle()
                        V.tensor_tensor(FW[f_in, 1, :], FW[f_in, 1, :], FW[f_in, 0, :], ALU.max)\
                            .then_inc(S("softplus_abs"), 1)
                        step(V.tensor_scalar(FW[f_in, 2, :], FW[f_in, 0, :], 0.0, None, ALU.max))
                    if (g, j) == (4, 4):
                        got("softplus_exp")
                        V.tensor_scalar(FW[f_in, 1, :], FW[f_in, 1, :], 1.0, None, ALU.add)\
                            .then_inc(S("softplus_plus1"), 1)
                    if (g, j) == (4, 6):
                        got("softplus_ln")
                        step(V.tensor_tensor(FW[f_in, 0, :], FW[f_in, 1, :], FW[f_in, 2, :], ALU.add))
                        settle()
                        step(V.memset(FW[f_in, 1, :], 1.0))
                        settle()
                        V.tensor_tensor_scan(FW[f_in, 2, :], FW[f_in, 1, :], FW[f_in, 0, :], 0.0, ALU.mult, ALU.add)\
                            .then_inc(S("forget_summed"), 1)

            got("hr_sum")
            got("forget_summed")
            step(V.tensor_scalar(FW[0:16, 0, :], ps[0][0:16, 0:T], P * 1e-6, None, ALU.add))
            V.tensor_scalar(FW[0:16, 1, :], ps[0][0:16, T:2 * T], 1.0 / P, 1e-6, ALU.mult, ALU.add)\
                .then_inc(S("hr_var"), 1)
            got("forget_cols")
            V.tensor_copy(FQ[:], ps[7][:, 0:64].rearrange("p (n h) -> p n h", n=NT)[:, :, 16:32])\
                .then_inc(S("forget_cols_out"), 1)
            for i in range(8):
                got("forget_rows")
                rows2 = ps[1 + i % 7][:, :].rearrange("p (h n t) -> p h n t", h=2, n=2)
                cb = CB[:, 2 * i:2 * i + 2, :, :]
                V.tensor_tensor(cb[:, :, 0, :], rows2[:, :, 0, :], many(causal[:], 2), ALU.add)
                V.tensor_copy(cb[:, :, 1, :], rows2[:, :, 0, :])
                V.tensor_tensor(cb[:, :, 2, :], rows2[:, :, 1, :], many(causal[:], 2), ALU.add)\
                    .then_inc(S("bias_made"), 1)
                if i == 2:
                    got("hr_root")
                    V.reciprocal(FW[0:16, 0:2, :], FW[0:16, 0:2, :]).then_inc(S("hr_inv"), 1)
            for part, gain in enumerate(("fox_q_gain_2", "fox_k_gain_2")):
                c = COL[gain]
                for q in range(8):
                    got("hr_bc")
                    s2 = QKV[:, 16 * part + 2 * q:16 * part + 2 * q + 2, :]
                    V.scalar_tensor_tensor(s2, s2, vec[:, c:c + 1], pair_of(q), ALU.mult, ALU.mult)\
                        .then_inc(S("qk_normed"), 1)
            got("bias_made", 8)

            def biased(h):
                z = h % 3
                got("scores_made")
                if h > 2:
                    got("pt_turned")
                for n, c0, w, blk in ((0, 0, P, 0), (1, P, T, 1)):
                    src = CB[:, h, blk:blk + w // P, :].rearrange("p b t -> p (b t)")
                    step(V.scalar_tensor_tensor(SC[:, z, c0:c0 + w], src, FQ[:, n, h:h + 1], ps[SCORE_BANKS[z]][:, c0:c0 + w],
                                                ALU.subtract, ALU.add))
                settle()
                for n, c0, w in ((0, 0, P), (1, P, T)):
                    V.tensor_reduce(AST[:, z, n:n + 1], SC[:, z, c0:c0 + w], AX_X, ALU.max, negate=True)\
                        .then_inc(S("score_max"), 1)

            def normalised(h):
                z = h % 3
                got("prob_made", 2)
                step(V.reciprocal(AST[:, z, 4:6], AST[:, z, 2:4]))
                settle()
                for n, c0, w in ((0, 0, P), (1, P, T)):
                    ins = V.tensor_scalar(SC[:, z, c0:c0 + w], SC[:, z, c0:c0 + w], AST[:, z, 4 + n:5 + n], None,
                                          ALU.mult)
                ins.then_inc(S("prob_normed"), 1)

            def out_lo(h):
                got("att_hi")
                V.tensor_tensor(H[:, 1, h, :], ps[4 + h % 2][:, 0:T], H[:, 0, h, :].bitcast(F32), ALU.subtract)\
                    .then_inc(S("att_made"), 1)
            for h in range(A_HEADS + 3):
                if h < A_HEADS:
                    biased(h)
                if 0 < h <= A_HEADS:
                    normalised(h - 1)
                if h > 2:
                    out_lo(h - 3)

            out_phase(U_OUT2, N_OUT2, M_OUT2, (4, "ffn_norm_2", 1e-6))
            step(V.memset(UC[:, :, 0:2], 0.0))
            settle()

            def y(i):
                return (YG, YV)[i % 2][:, i // 2, :]

            def tap(g, k, i):
                c = COL[f"conv{k}"] + (i % 2) * FT + i // 2
                return vec[:, bass.ds(g * 4 + c, 1)]

            def evac_ffn2(g):
                cb = COL["ffn_conv_b_2"]
                for i in range(GROUP):
                    dve.wait_ge(bank_freed, g * 8 + (N_FFN2 + i + 1 + FREE_BANKS))
                    if i == 0:
                        dve.wait_ge(S("hid_made"), g + 12)
                    ins = V.tensor_scalar(y(i), UC[:, i, 0:T], tap(g, 0, i),
                                          vec[:, bass.ds(g * 4 + (cb + (i % 2) * FT + i // 2), 1)], ALU.mult, ALU.add)
                ins.then_inc(S("conv_step"), 1)

            def tail_ffn2(g, j):
                if j in (1, 2):
                    dve.wait_ge(S("conv_step"), g * 3 + j)
                    for i in range(GROUP):
                        ins = V.scalar_tensor_tensor(y(i), UC[:, i, j:j + T], tap(g, j, i), y(i), ALU.mult, ALU.add)
                    ins.then_inc(S("conv_step"), 1)
                elif j == 4:
                    dve.wait_ge(S("conv_gate"), g + 1)
                    V.tensor_tensor(YV[:], YG[:], YV[:], ALU.mult).then_inc(S("hid_full"), 1)
                elif j == 6:
                    dve.wait_ge(S("hid_hi"), g + 12)
                    V.tensor_tensor(HID[:, 1, bass.ds(g * 4, 4), :], YV[:],
                                    HID[:, 0, bass.ds(g * 4, 4), :].bitcast(F32), ALU.subtract)\
                        .then_inc(S("hid_made"), 1)
            ffn_phase(U_FFN2, evac_ffn2, tail_ffn2)
            down(U_DOWN2, M_DOWN2, last=True)
            for q in range(4):
                got("turned_v")
                V.tensor_copy(OUTT[:, 1, q * 512:(q + 1) * 512], ps[4 + q][:, :]).then_inc(S("y_tokens_1"), 1)

        @block.tensor
        def _(pe):
            mm = nc.tensor.matmul

            def h_in(part, k):
                return H[:, part, k, :]

            def unit(u, tiles, nf, wcol, first=False, last=False, g=None, step=0, n0=None, hcol=h_in, h_wait=None):
                v = u + 1
                pe.wait_ge(lo_made, v if g is None else g * step + v)
                for kk, k in enumerate(tiles):
                    if h_wait is not None and kk == 0:
                        pe.wait_ge(*h_wait)
                    for f in range(nf):
                        if first and kk == 0:
                            bv = n0 + f + 1 - 8 + FREE_BANKS
                            pe.wait_ge(bank_freed, bv if g is None else g * 8 + bv)
                        c = wcol(kk, f)
                        hi_w, lo_w = HIW[:, u % 2, c:c + P], LOW[:, u % 4, c:c + P]
                        h_hi, h_lo = hcol(0, k), hcol(1, k)
                        start, stop = first and kk == 0, last and kk == len(tiles) - 1
                        o_ = ps[f][:, 0:T]
                        mm(o_, hi_w, h_hi, start=start, stop=False)
                        mm(o_, hi_w, h_lo, start=False, stop=False)
                        i = mm(o_, lo_w, h_hi, start=False, stop=stop)
                        if kk == len(tiles) - 1 and f == nf - 1:
                            i.then_inc(unit_used, 1)
                        elif stop:
                            i.then_inc(tile_summed, 1)

            def plain(kk, f):
                return kk * 1024 + f * P

            def gate_up_col(kk, i):
                return kk * 1024 + (i % 2) * 512 + (i // 2) * P

            def group_phase(u0, n0, groups, wcol=plain, k_norm=None, h_wait={}):
                with pe.Fori(0, groups) as g:
                    for j in range(UG):
                        hw = h_wait.get(j) if k_norm is None else (S("h_made"), 8 * HN[k_norm] + j + 1)
                        unit(u0 + j, [2 * j, 2 * j + 1], GROUP, wcol, j == 0, j == UG - 1, g, UG, n0, h_wait=hw)

            def down(u0, n0, made0):
                for half in range(2):
                    b = u0 + half * (FT // 2)
                    for j in range(2):
                        unit(b + j, [2 * j, 2 * j + 1], GROUP, plain, j == 0, n0=n0 + 8 * half,
                             hcol=lambda part, k: HID[:, part, k, :], h_wait=(S("hid_made"), made0 + 10))
                    with pe.Fori(0, 4) as i:
                        for j in range(4):
                            unit(b + 2 + j, [4 + 2 * j, 5 + 2 * j], GROUP, plain, g=i, step=4,
                                 hcol=lambda part, k: HID[:, part, bass.ds(i * 8 + k, 1), :])
                    for j in range(18, 22):
                        unit(b + j, [2 * j, 2 * j + 1], GROUP, plain, last=j == 21,
                             hcol=lambda part, k: HID[:, part, k, :], h_wait=(S("hid_made"), made0 + 11))

            def norm(k, presummed=True):
                sq = NSQ_H if k == 2 else NSQ
                for f in range(8 if presummed else 0, KT):
                    pe.wait_ge(S("squared"), KT * k + f + 1)
                    i = mm(ps[0][:, 0:T], ones[:], sq[:, f, :], start=f == (8 if presummed else 0),
                           stop=f == KT - 1 and not presummed)
                if presummed:
                    pe.wait_ge(S("squares_presummed"), {1: 1, 2: 2, 4: 3}[k])
                    i = mm(ps[0][:, 0:T], ones[:], sq[:, 0, :], start=False, stop=True)
                i.then_inc(S("squares_summed"), 1)

            pe.sem_inc(unit_used, FREE_UNITS)
            pe.wait_ge(S("ident_made"), 1)
            for n in range(NT):
                pe.wait_ge(S(f"x_landed_{n}"), 16)
                for q in range(4):
                    for i in range(4):
                        f = 4 * q + i
                        ins = nc.tensor.transpose(ps[4 * n + q][:, i * P:(i + 1) * P], XIN[:, n, f * P:(f + 1) * P],
                                                  ident[:])
                    ins.then_inc(S("x_turned"), 1)
            pe.wait_ge(S("vecs_landed"), counts["vecs_landed"])
            pe.wait_ge(S("x_tiles"), 8)
            for i, pack in enumerate(PACKS):
                r = sum(n for _, n in pack)
                if i >= 4:
                    pe.wait_ge(S("vecs_made"), i - 3)
                nc.tensor.transpose(ps[i % 4][:, (i // 4) * P:(i // 4) * P + r], VPACK[0:r, i, :],
                                    ident[0:r, 0:r]).then_inc(S("vecs_turned"), 1)
            pe.wait_ge(S("vecs_made"), len(PACKS))
            norm(0, presummed=False)
            for j in range(4):
                unit(j, [4 * j + i for i in range(4)], 3, lambda kk, f: kk * 384 + f * P, j == 0, j == 3,
                     n0=N_MISC1, h_wait=(S("h_made"), 2 * j + 2))
            group_phase(U_IN, N_IN, 6)

            got = waiter(pe)
            got("loras_landed", 64)
            got("lowrank_ready")
            for name, r, b0 in (("w_lora", slice(0, 64), 0), ("a_lora", slice(64, 128), 4)):
                for t in range(PAIRS):
                    pe.wait_ge(bank_freed, N_OUT - 8 + b0 + t // 2 + 1 + FREE_BANKS)
                    ins = mm(ps[b0 + t // 2][:, (t % 2) * T:(t % 2 + 1) * T], WA_UP[r, t * P:(t + 1) * P],
                             PR[r, T_WA, PAD:TP], start=True, stop=True)
                    if t % 2:
                        ins.then_inc(S(name), 1)

            def head_rsqrt(src, tiles, sel, width, buf=None, b0=0):
                got("hr_sq")
                for f in range(tiles):
                    c = 15 - f * width - (width - 1)
                    ins = mm(ps[b0][0:16, 0:T], sel[:, c:c + 16], src[:, f, :], start=f == 0, stop=f == tiles - 1)
                ins.then_inc(S("hr_sum"), 1)
                got("hr_inv")
                for f in range(tiles):
                    n = P // width
                    for e in range(width):
                        h = f * width + e
                        ins = mm(ps[b0 + f // 2][e * n:(e + 1) * n, (f % 2) * T:(f % 2 + 1) * T],
                                 ident[0:16, h:h + 1].broadcast_to([16, n]), rstd[0:16] if buf is None else buf,
                                 start=True, stop=True)
                    if f % 2:
                        ins.then_inc(S("hr_bc"), 1)

            def head_sums(src, b0, name):
                for q in range(4):
                    mm(ps[b0 + q][:, :], headones[:], src[:, 2 * q:2 * q + 2, :], start=True, stop=True)\
                        .then_inc(S(name), 1)
            got("w_lora_sigmoid")
            head_rsqrt(KSQ, PAIRS, sel2, 2)
            got("bonus_terms")
            got("a_lora_sigmoid")
            head_sums(TMP, 4, "heads_summed")
            got("hats_made")
            got("r_hat_made")
            got("bonus_out", 4)

            def inversion(LO, TM, TT, PM):
                for lev in range(1, 6):
                    for b in range(4):
                        got("inv_off" if lev > 1 or LO is gLO else "tt_started")
                        if lev > 1:
                            got("inv_added")
                        for h in range(4 * b, 4 * b + 4):
                            ins = mm(ps[2 * b][:, (h % 4) * P:(h % 4 + 1) * P], LO[:, h, :], TM[:, h, :],
                                     start=True, stop=True)
                        ins.then_inc(S("inv_p"), 1)
                    for b in range(4):
                        got("inv_pm")
                        if lev < 5:
                            for h in range(4 * b, 4 * b + 4):
                                mm(ps[2 * b][:, (h % 4) * P:(h % 4 + 1) * P], TT[:, h, :], PM[:, h, :],
                                   start=True, stop=True)
                        for h in range(4 * b, 4 * b + 4):
                            ins = mm(ps[2 * b + 1][:, (h % 4) * P:(h % 4 + 1) * P], PM[:, h, :], TT[:, h, :],
                                     start=True, stop=True)
                        ins.then_inc(S("inv_t"), 1)
                got("inv_added", 4)

            for n in range(NT):
                tn = slice(n * P, n * P + P)
                pn = slice(PAD + n * P, PAD + n * P + P)
                for i, src in enumerate((lambda t: PR[:, T_V + t, pn], lambda t: BH[:, t, tn],
                                         lambda t: PR[:, T_K + t, pn])):
                    for t in range(PAIRS):
                        ins = nc.tensor.transpose(ps[2 * i + t // 4][:, (t % 4) * P:(t % 4 + 1) * P], src(t), ident[:])
                        if t % 4 == 3:
                            ins.then_inc(S("tok_turned"), 1)
                def l_fills(which, fill, free):
                    for hp in range(2):
                        rr = slice(64 * hp, 64 * hp + 64)
                        for t in range(PAIRS):
                            if t % 2 == 0 and free(fill):
                                got(free(fill))
                            w = BH[rr, t, tn] if which == 0 else PR[rr, T_K + t, pn]
                            ins = mm(ps[fill % 8][:, (t % 2) * T:(t % 2 + 1) * T], w,
                                     AR[rr, t, :, tn], start=True, stop=True)
                            if t % 2:
                                ins.then_inc(S("l_summed"), 1)
                                fill += 1
                l_fills(0, 6, lambda fill: "tok_made" if fill >= 8 else None)
                for b in range(4):
                    got("lbr_out")
                    rr = slice(64 * (b // 2), 64 * (b // 2) + 64)
                    for i in range(4):
                        t = 4 * (b % 2) + i
                        ins = mm(ps[(14 + b) % 8][:, i * P:(i + 1) * P], AR[rr, t, 0, tn], BH[rr, t, tn],
                                 start=True, stop=True)
                    ins.then_inc(S("l_plain"), 1)
                l_fills(1, 18, lambda fill: "lbr_out" if fill < 22 else "l_out")
                got("lkr_out", 8)
                inversion(LO, TM, TT, PM)
                for c in (2 * n, 2 * n + 1):
                    r = slice(C * (c % 2), C * (c % 2) + C)
                    cc = slice(c * C, c * C + C)
                    s0 = ST[:, c % 2]
                    for hb in range(2):
                        if c % 2:
                            got("s_out")
                        for i in range(4):
                            t = 4 * hb + i
                            mm(ps[4 * hb][r, i * P:(i + 1) * P], AR[:, t, 0, cc], s0[:, t, :], start=True, stop=False)
                            for hp in range(2):
                                v = slice(64 * hp, 64 * hp + 64)
                                ins = mm(ps[4 * hb][r, i * P + 64 * hp:i * P + 64 * hp + 64],
                                         LKR[:, 8 * hp + t, 0, r], VTOK[:, t, v], start=False, stop=hp == 1)
                        ins.then_inc(S("r1_summed"), 1)
                    for hb in range(2):
                        got("r1_out")
                        for i in range(4):
                            t = 4 * hb + i
                            for hp in range(2):
                                v = slice(64 * hp, 64 * hp + 64)
                                ins = mm(ps[1 + 4 * hb][r, i * P + 64 * hp:i * P + 64 * hp + 64],
                                         TT[:, 8 * hp + t, r], R1[:, t, v], start=True, stop=True)
                        ins.then_inc(S("u_summed"), 1)
                    for hb in range(2):
                        got("u_out")
                        for i in range(4):
                            t = 4 * hb + i
                            o_ = ps[3 + 4 * hb][:, i * P:(i + 1) * P]
                            mm(o_, BTOK[r, t, :], UU[r, t, :], start=True, stop=False)
                            ins = mm(o_, KTOK[r, t, :], VTOK[r, t, :], start=False, stop=True)
                        ins.then_inc(S("s_summed"), 1)
                    for hb in range(2):
                        if c % 2:
                            got("y_out")
                        for i in range(4):
                            t = 4 * hb + i
                            o_ = ps[2 + 4 * hb]
                            mm(o_[:, i * C:(i + 1) * C], s0[:, t, :], AR[:, t, 1, cc], start=True, stop=False)
                            for hp in range(2):
                                v = slice(64 * hp, 64 * hp + 64)
                                mm(o_[v, i * C:(i + 1) * C], UU[:, t, v], LBR[:, 8 * hp + t, 1, r],
                                   start=False, stop=False)
                                ins = mm(o_[v, i * C:(i + 1) * C], VTOK[:, t, v], LKR[:, 8 * hp + t, 1, r],
                                         start=False, stop=True)
                        ins.then_inc(S("y_summed"), 1)
                got("y_out", 2)
                got("s_out", 2)
            head_sums(BH, 0, "heads_summed")
            head_rsqrt(QKSQ, 8, sel1, 1, RWK[0:16, 0, :], 4)
            head_rsqrt(RN, PAIRS, sel2, 2)
            got("y_normed")
            for t in range(PAIRS):
                o_ = ps[t // 2][:, (t % 2) * T:(t % 2 + 1) * T]
                mm(o_, G_UP[:, 0, t * P:(t + 1) * P], PR[:, T_G0, PAD:TP], start=True, stop=False)
                ins = mm(o_, G_UP[0:32, 1, t * P:(t + 1) * P], PR[0:32, T_G1, PAD:TP], start=False, stop=True)
                if t % 2:
                    ins.then_inc(S("heads_summed"), 1)

            got("gqk_normed")
            got("rows_made")
            got("beta_made")
            for n in range(NT):
                ins = nc.tensor.transpose(ps[4][:, n * P:(n + 1) * P], ROWS[:, n * P:(n + 1) * P], ident[:])
            ins.then_inc(S("cols_turned"), 1)
            got("ya_full")

            def g_rows(name):
                for h in range(G_HEADS):
                    ins = mm(ps[h // 2][:, (h % 2) * T:(h % 2 + 1) * T],
                             ident[32:40, 32 + h:33 + h].broadcast_to([8, P]), ROWS[32:40, :], start=True, stop=True)
                    if h % 2:
                        ins.then_inc(S(name), 1)
            g_rows("g_rows")
            got("cols_made")
            for n in range(NT):
                for h in range(G_HEADS):
                    ins = mm(ps[4 + 2 * n + h // 4][:, (h % 4) * P:(h % 4 + 1) * P],
                             ident[64:72, 64 + h:65 + h].broadcast_to([8, P]), ROWS[64:72, n * P:(n + 1) * P],
                             start=True, stop=True)
                    if h % 4 == 3:
                        ins.then_inc(S("beta_rows"), 1)
            got("g_rows_exp", 4)
            got("gam_diff", 2)

            def key_tokens(n):
                for i in range(G_QK):
                    ins = nc.tensor.transpose(ps[n][:, i * P:(i + 1) * P], KC[:, i, n * P:(n + 1) * P], ident[:])
                ins.then_inc(S("tok_turned"), 1)

            def value_tokens(n):
                for h in range(G_HEADS):
                    ins = nc.tensor.transpose(ps[2 + 2 * n + h // 4][:, (h % 4) * P:(h % 4 + 1) * P],
                                              VC[:, h, n * P:(n + 1) * P], ident[:])
                ins.then_inc(S("tok_turned"), 1)
            key_tokens(0)
            value_tokens(0)
            key_tokens(1)
            for n in range(NT):
                tn = slice(n * P, n * P + P)
                got("beta_rows_out", 2)
                for i in range(G_QK):
                    mm(ps[4 + 2 * n][:, i * P:(i + 1) * P], KC[:, i, tn], KC[:, i, tn], start=True, stop=True)
                for i in range(G_QK):
                    ins = mm(ps[5 + 2 * n][:, i * P:(i + 1) * P], KC[:, i, tn], QC[:, i, tn], start=True, stop=True)
                ins.then_inc(S("gkk_summed"), 1)
            got("gkk_out")
            value_tokens(1)
            for b in range(4):
                if b % 2 == 0:
                    got("gtok_made")
                    got("gtt_start")
                for i in range(4):
                    ins = nc.tensor.transpose(ps[(0, 2, 6, 7)[b]][:, i * P:(i + 1) * P], gTT[:, 4 * b + i, :], ident[:])
                ins.then_inc(S("gtm_turned"), 1)
            inversion(gLO, gTM, gTT, gPM)
            for b in range(4):
                for i in range(4):
                    ins = mm(ps[b][:, i * P:(i + 1) * P], gTT[:, 4 * b + i, :], VB[:, 4 * b + i, :],
                             start=True, stop=True)
                ins.then_inc(S("u0_summed"), 1)
            for b in range(4):
                for i in range(4):
                    ins = mm(ps[4 + b][:, i * P:(i + 1) * P], KBE[:, 4 * b + i, :], gTT[:, 4 * b + i, :],
                             start=True, stop=True)
                ins.then_inc(S("wt_summed"), 1)
            got("u0_out", 4)
            got("wt_out", 4)
            for c in range(NCH):
                n, r = c // 2, slice(C * (c % 2), C * (c % 2) + C)
                cc = slice(c * C, c * C + C)
                s0 = gS[c % 2]
                for hb in range(2):
                    if c:
                        got("gs_out")
                    for h in range(4 * hb, 4 * hb + 4):
                        ins = mm(ps[hb][r, (h % 4) * P:(h % 4 + 1) * P], WT[:, 8 * n + h, r], s0[:, h, :],
                                 start=True, stop=True)
                    ins.then_inc(S("ws_summed"), 1)
                for hb in range(2):
                    got("vn_made")
                    for h in range(4 * hb, 4 * hb + 4):
                        ins = mm(ps[2 + hb][:, (h % 4) * P:(h % 4 + 1) * P], KG[r, 8 * n + h, :], VN[r, h, :],
                                 start=True, stop=True)
                    ins.then_inc(S("gs_summed"), 1)
                for hb in range(2):
                    if c:
                        got("o_out")
                    for h in range(4 * hb, 4 * hb + 4):
                        o_ = ps[4 + hb][:, (h % 4) * C:(h % 4 + 1) * C]
                        mm(o_, s0[:, h, :], QG[:, h, cc], start=True, stop=False)
                        ins = mm(o_, VN[:, h, :], AT[:, 8 * n + h, r], start=False, stop=True)
                    ins.then_inc(S("o_summed"), 1)
            got("o_out", 2)
            got("gs_out", 2)
            pe.sem_inc(S("weights_place_free"), 1)
            head_rsqrt(GSQ, 8, sel1, 1)

            got("yb_full")
            group_phase(U_OUT, N_OUT, 2, h_wait={0: (S("mix_made"), 1), 4: (S("mix_made"), 2)})
            norm(1)
            group_phase(U_FFN1, N_FFN1, 11, gate_up_col, 1)
            down(U_DOWN1, N_DOWN1, 1)
            norm(2)
            norm(3, presummed=False)
            for j in range(4):
                unit(U_MISC2 + j, [4 * j + i for i in range(4)], 1, lambda kk, f: kk * P, j == 0, j == 3,
                     n0=N_MISC2, h_wait=(S("h_made"), 8 * HN[3] + 2 * j + 2))
            group_phase(U_FOX, N_FOX, 6)

            got("hr_sq")
            pe.wait_ge(bank_freed, N_OUT2 + FREE_BANKS)
            for part in range(2):
                for h in range(A_HEADS):
                    ins = mm(ps[0][0:16, part * T:(part + 1) * T], sel1[:, 15 - h:31 - h], ASQ[:, 16 * part + h, :],
                             start=h == 0, stop=h == A_HEADS - 1)
            ins.then_inc(S("hr_sum"), 1)
            got("forget_summed")
            for n in range(NT):
                ins = nc.tensor.transpose(ps[7][:, n * 32:(n + 1) * 32], FW[f_in, 2, n * P:(n + 1) * P],
                                          ident[f_in, f_in])
            ins.then_inc(S("forget_cols"), 1)
            for i in range(8):
                if i == 6:
                    got("forget_cols_out")
                if i == 7:
                    got("bias_made")
                for e in range(2):
                    r = 112 + 2 * i + e
                    ins = mm(ps[1 + i % 7][:, e * T:(e + 1) * T], ident[f_in, r:r + 1].broadcast_to([32, P]),
                             FW[f_in, 2, :], start=True, stop=True)
                ins.then_inc(S("forget_rows"), 1)
            for i in range(8):
                got("bias_made" if i < 7 else "vt_made")
                for e in range(4):
                    ins = nc.tensor.transpose(ps[1 + (8 + i) % 7][:, e * P:(e + 1) * P],
                                              QKV[:, 32 + (i % 4) * 4 + e, (i // 4) * P:(i // 4 + 1) * P], ident[:])
                ins.then_inc(S("turned_a"), 1)
            got("hr_inv")
            got("vt_made", 7)
            for part in range(2):
                for h in range(A_HEADS):
                    if part and h % 2 == 0:
                        got("qk_normed")
                    ins = mm(ps[h // 2][:, (h % 2) * T:(h % 2 + 1) * T], ident[0:16, h:h + 1].broadcast_to([16, P]),
                             FW[0:16, part, :], start=True, stop=True)
                    if h % 2:
                        ins.then_inc(S("hr_bc"), 1)
            got("qk_normed", 8)

            def scores(h):
                o_ = ps[SCORE_BANKS[h % 3]]
                mm(o_[:, 0:P], QKV[:, h, 0:P], QKV[:, 16 + h, 0:P], start=True, stop=True)
                mm(o_[:, P:3 * P], QKV[:, h, P:T], QKV[:, 16 + h, :], start=True, stop=True)\
                    .then_inc(S("scores_made"), 1)

            def turn(h):
                z = h % 2
                got("prob_normed")
                for i in range(3):
                    ins = nc.tensor.transpose(ps[2 + z][:, i * P:(i + 1) * P], SC[:, h % 3, i * P:(i + 1) * P], ident[:])
                ins.then_inc(S("pt_turned"), 1)

            def mix(h):
                z = h % 2
                got("pt_made")
                if h >= 2:
                    got("att_made")
                v0, v1 = (VT[:, n, h * P:(h + 1) * P] for n in range(NT))
                mm(ps[4 + z][:, 0:P], v0, PT[:, z, 0:P], start=True, stop=True)
                mm(ps[4 + z][:, P:T], v0, PT[:, z, P:2 * P], start=True, stop=False)
                mm(ps[4 + z][:, P:T], v1, PT[:, z, 2 * P:3 * P], start=False, stop=True)\
                    .then_inc(S("att_summed"), 1)
            scores(0)
            for h in range(A_HEADS + 2):
                if h < A_HEADS - 1:
                    scores(h + 1)
                if 0 < h <= A_HEADS:
                    turn(h - 1)
                if h > 1:
                    mix(h - 2)

            got("att_made", 2)
            group_phase(U_OUT2, N_OUT2, 2)
            norm(4)
            group_phase(U_FFN2, N_FFN2, 11, gate_up_col, 4)
            down(U_DOWN2, N_DOWN2, 12)
            pe.wait_ge(bank_freed, N_END + FREE_BANKS)
            for n in range(NT):
                for q in range(4):
                    for i in range(4):
                        ins = nc.tensor.transpose(ps[4 * n + q][:, i * P:(i + 1) * P],
                                                  X[:, 4 * q + i, n * P:(n + 1) * P], ident[:])
                    ins.then_inc(S("turned_v" if n else "turned_a"), 1)


def kernel(**inputs):
    import numpy as np
    import concourse.bacc as bacc
    from concourse.bass_utils import run_bass_kernel_spmd

    nc = bacc.Bacc("TRN2", target_bir_lowering=False, num_devices=1)
    arrays, io = {}, {}
    for name in NAMES:
        a = np.ascontiguousarray(inputs[name])
        arrays[f"in_{name}"] = a
        io[name] = nc.dram_tensor(f"in_{name}", a.shape, mybir.dt.from_np(a.dtype), kind="ExternalInput").ap()
    out = nc.dram_tensor("out_y", (1, T, D), F32, kind="ExternalOutput").ap()
    build(nc, io, out)
    return run_bass_kernel_spmd(nc, [arrays], core_ids=[0]).results[0]["out_y"]
```
